# Optimizing a Trainium2 kernel written in Bass

```python
import jax, jax.numpy as jnp
from jax import lax
import numpy as np
import math

D_MODEL = 1024
BATCH = 1
SEQ = 512
DEPTH = 2

N_MIXERS = 3
BLOCK = 128
ROPE_THETA = 500000.0
ROPE_FRAC = 4
EPS = 1e-6
NEG_INF = -1e30

A_HEADS = 8
A_QK_DIM = 128
A_ROPE_DIM = A_QK_DIM // ROPE_FRAC
A_NOPE_DIM = A_QK_DIM - A_ROPE_DIM
A_V_DIM = 128
A_KV_RANK = 256
IDX_HEADS = 16
IDX_DIM = 64
TOPK_MAX = 256

B_HEADS = 16
B_KV_HEADS = 4
B_HEAD_DIM = 64
B_WINDOW = 128

C_HEADS = 8
C_HEAD_DIM = 128
C_BRANCHES = ((128, 1), (512, 4), (2048, 16))

MEM_LEN = 256
MEM_HEADS = 4
MEM_HEAD_DIM = 64
MEM_WIDTH = MEM_HEADS * MEM_HEAD_DIM

D_FF = 2816
CONV_WIDTH = 3

MIX_WIDTH = 1024
OUT_IN = MIX_WIDTH + MEM_WIDTH
A_SPLITS = (A_HEADS * A_QK_DIM, A_KV_RANK, A_ROPE_DIM, IDX_HEADS * IDX_DIM, IDX_DIM, IDX_HEADS, MEM_WIDTH)
B_SPLITS = (B_HEADS * B_HEAD_DIM, B_KV_HEADS * B_HEAD_DIM, B_KV_HEADS * B_HEAD_DIM, MEM_WIDTH)
C_SPLITS = (C_HEADS * C_HEAD_DIM, C_HEADS * C_HEAD_DIM, C_HEADS * C_HEAD_DIM, MEM_WIDTH)
N_A = len(range(0, DEPTH, N_MIXERS))
N_B = len(range(1, DEPTH, N_MIXERS))
N_C = len(range(2, DEPTH, N_MIXERS))


def rmsnorm(x, g):
    xf = x.astype(jnp.float32)
    y = xf * lax.rsqrt(jnp.mean(xf * xf, axis=-1, keepdims=True) + EPS)
    return (y * g.astype(jnp.float32)).astype(x.dtype)

def split_cols(t, sizes):
    return jnp.split(t, np.cumsum(sizes)[:-1].tolist(), axis=-1)

def rope_tables(positions, rot_dim):
    inv = ROPE_THETA ** (-jnp.arange(0, rot_dim, 2, dtype=jnp.float32) / rot_dim)
    ang = positions.astype(jnp.float32)[..., None] * inv
    return jnp.cos(ang), jnp.sin(ang)

def apply_partial_rope(x, cos, sin):
    half = cos.shape[-1]
    rot = 2 * half
    xf = x[..., :rot].astype(jnp.float32)
    x1, x2 = xf[..., :half], xf[..., half:]
    c, s = cos[:, :, None, :], sin[:, :, None, :]
    xr = jnp.concatenate([x1 * c - x2 * s, x2 * c + x1 * s], axis=-1).astype(x.dtype)
    return jnp.concatenate([xr, x[..., rot:]], axis=-1)

def banded_window_attention(q, k, v, max_dist, scale, sink=None):
    B, n = q.shape[0], q.shape[1]
    nb = -(-n // BLOCK)
    pad = nb * BLOCK - n
    if pad:
        q = jnp.pad(q, ((0, 0), (0, pad), (0, 0), (0, 0), (0, 0)))
        k = jnp.pad(k, ((0, 0), (0, pad), (0, 0), (0, 0)))
        v = jnp.pad(v, ((0, 0), (0, pad), (0, 0), (0, 0)))
    qb = q.reshape(B, nb, BLOCK, *q.shape[2:])
    kb = k.reshape(B, nb, BLOCK, *k.shape[2:])
    vb = v.reshape(B, nb, BLOCK, *v.shape[2:])
    prev = ((0, 0), (1, 0), (0, 0), (0, 0), (0, 0))
    kk = jnp.concatenate([jnp.pad(kb[:, :-1], prev), kb], axis=2)
    vv = jnp.concatenate([jnp.pad(vb[:, :-1], prev), vb], axis=2)
    s = jnp.einsum('bnqhgd,bnkhd->bnhgqk', qb, kk).astype(jnp.float32) * scale
    qi = jnp.arange(BLOCK)[:, None]
    kj = jnp.arange(2 * BLOCK)[None, :]
    dist = BLOCK + qi - kj
    band = (dist >= 0) & (dist <= max_dist)
    blk = jnp.arange(nb)[:, None, None]
    mask = band[None] & ((blk > 0) | (kj >= BLOCK)[None])
    s = jnp.where(mask[None, :, None, None], s, NEG_INF)
    m = jnp.max(s, axis=-1)
    if sink is not None:
        sk = sink.astype(jnp.float32)[None, None, :, :, None]
        m = jnp.maximum(m, sk)
    p = jnp.exp(s - m[..., None])
    l = jnp.sum(p, axis=-1)
    if sink is not None:
        l = l + jnp.exp(sk - m)
    p = p / l[..., None]
    o = jnp.einsum('bnhgqk,bnkhd->bnqhgd', p, vv.astype(jnp.float32))
    o = o.reshape(B, nb * BLOCK, *o.shape[3:])[:, :n].astype(q.dtype)
    lse = (m + jnp.log(l)).transpose(0, 1, 4, 2, 3)
    lse = lse.reshape(B, nb * BLOCK, *lse.shape[3:])[:, :n]
    return o, lse

def dsa_attention(q_nope, q_rope, c_kv, k_rope, q_idx, k_idx, w_idx, w_uk, w_uv):
    B, S = q_nope.shape[0], q_nope.shape[1]
    topk = min(TOPK_MAX, S // 4)
    nb = S // BLOCK
    scale = A_QK_DIM ** -0.5
    q_lat = jnp.einsum('bshn,rhn->bshr', q_nope, w_uk)
    key_pos = jnp.arange(S)

    def to_blocks(t):
        return t.reshape(B, nb, BLOCK, *t.shape[2:]).swapaxes(0, 1)

    def one_block(args):
        ql, qr, qi, wi, t = args
        dots = jnp.einsum('bqhd,bsd->bqhs', qi, k_idx).astype(jnp.float32)
        score = jnp.einsum('bqhs,bqh->bqs', jax.nn.relu(dots), wi.astype(jnp.float32))
        causal = key_pos[None, :] <= t[:, None]
        score = jnp.where(causal[None], score, -jnp.inf)
        _, idx = lax.top_k(score, topk)
        c_sel = jax.vmap(lambda c, i: c[i])(c_kv, idx)
        kr_sel = jax.vmap(lambda c, i: c[i])(k_rope, idx)
        s = (jnp.einsum('bqhr,bqkr->bqhk', ql, c_sel)
             + jnp.einsum('bqhe,bqke->bqhk', qr, kr_sel)).astype(jnp.float32) * scale
        valid = idx <= t[None, :, None]
        s = jnp.where(valid[:, :, None, :], s, NEG_INF)
        p = jax.nn.softmax(s, axis=-1)
        return jnp.einsum('bqhk,bqkr->bqhr', p, c_sel.astype(jnp.float32)).astype(ql.dtype)

    t_ids = jnp.arange(S).reshape(nb, BLOCK)
    o_lat = lax.map(one_block, (to_blocks(q_lat), to_blocks(q_rope), to_blocks(q_idx), to_blocks(w_idx), t_ids))
    o_lat = o_lat.swapaxes(0, 1).reshape(B, S, A_HEADS, A_KV_RANK)
    return jnp.einsum('bshr,rhv->bshv', o_lat, w_uv)

def mixer_a(h, cos32, sin32, cos16, sin16, w_in, kv_norm, w_uk, w_uv):
    B, S, _ = h.shape
    q, c_kv, k_rope, q_idx, k_idx, w_idx, q_mem = split_cols(h @ w_in, A_SPLITS)
    q = apply_partial_rope(q.reshape(B, S, A_HEADS, A_QK_DIM), cos32, sin32)
    q_rope, q_nope = q[..., :A_ROPE_DIM], q[..., A_ROPE_DIM:]
    k_rope = apply_partial_rope(k_rope[:, :, None, :], cos32, sin32)[:, :, 0]
    c_kv = rmsnorm(c_kv, kv_norm)
    q_idx = apply_partial_rope(q_idx.reshape(B, S, IDX_HEADS, IDX_DIM), cos16, sin16)
    k_idx = apply_partial_rope(k_idx[:, :, None, :], cos16, sin16)[:, :, 0]
    w_idx = w_idx * (IDX_HEADS * IDX_DIM) ** -0.5
    o = dsa_attention(q_nope, q_rope, c_kv, k_rope, q_idx, k_idx, w_idx, w_uk, w_uv)
    return o.reshape(B, S, A_HEADS * A_V_DIM), q_mem

def mixer_b(h, cos16, sin16, w_in, sinks):
    B, S, _ = h.shape
    q, k, v, q_mem = split_cols(h @ w_in, B_SPLITS)
    group = B_HEADS // B_KV_HEADS
    q = apply_partial_rope(q.reshape(B, S, B_HEADS, B_HEAD_DIM), cos16, sin16)
    k = apply_partial_rope(k.reshape(B, S, B_KV_HEADS, B_HEAD_DIM), cos16, sin16)
    v = v.reshape(B, S, B_KV_HEADS, B_HEAD_DIM)
    q = q.reshape(B, S, B_KV_HEADS, group, B_HEAD_DIM)
    o, _ = banded_window_attention(q, k, v, B_WINDOW - 1, B_HEAD_DIM ** -0.5,
                                   sink=sinks.reshape(B_KV_HEADS, group))
    return o.reshape(B, S, B_HEADS * B_HEAD_DIM), q_mem

def dilate(t, d):
    B, S = t.shape[0], t.shape[1]
    return t.reshape(B, S // d, d, *t.shape[2:]).swapaxes(1, 2).reshape(B * d, S // d, *t.shape[2:])

def undilate(t, d, B):
    n = t.shape[1]
    return t.reshape(B, d, n, *t.shape[2:]).swapaxes(1, 2).reshape(B, n * d, *t.shape[2:])

def mixer_c(h, cos32, sin32, w_in):
    B, S, _ = h.shape
    q, k, v, q_mem = split_cols(h @ w_in, C_SPLITS)
    q = apply_partial_rope(q.reshape(B, S, C_HEADS, C_HEAD_DIM), cos32, sin32)
    k = apply_partial_rope(k.reshape(B, S, C_HEADS, C_HEAD_DIM), cos32, sin32)
    v = v.reshape(B, S, C_HEADS, C_HEAD_DIM)
    outs, lses = [], []
    for window, d in C_BRANCHES:
        o_g, lse_g = banded_window_attention(dilate(q, d)[:, :, :, None], dilate(k, d), dilate(v, d),
                                             window // d, C_HEAD_DIM ** -0.5)
        outs.append(undilate(o_g[:, :, :, 0], d, B))
        lses.append(undilate(lse_g[..., 0], d, B))
    alpha = jax.nn.softmax(jnp.stack(lses), axis=0)
    o = jnp.sum(alpha[..., None] * jnp.stack(outs).astype(jnp.float32), axis=0).astype(h.dtype)
    return o.reshape(B, S, C_HEADS * C_HEAD_DIM), q_mem

def memory_cross_attention(q_mem, mem_n, w_mem_kv):
    B, S, _ = q_mem.shape
    k, v = jnp.split(mem_n @ w_mem_kv, 2, axis=-1)
    k = k.reshape(B, -1, MEM_HEADS, MEM_HEAD_DIM)
    v = v.reshape(B, -1, MEM_HEADS, MEM_HEAD_DIM)
    q = q_mem.reshape(B, S, MEM_HEADS, MEM_HEAD_DIM)
    s = jnp.einsum('bshd,bmhd->bhsm', q, k).astype(jnp.float32) * MEM_HEAD_DIM ** -0.5
    p = jax.nn.softmax(s, axis=-1)
    o = jnp.einsum('bhsm,bmhd->bshd', p, v.astype(jnp.float32)).astype(q_mem.dtype)
    return o.reshape(B, S, MEM_WIDTH)

def conv_glu_ffn(h, w_up, conv_w, conv_b, w_down):
    S = h.shape[1]
    a, b = jnp.split(h @ w_up, 2, axis=-1)
    a_pad = jnp.pad(a, ((0, 0), (CONV_WIDTH - 1, 0), (0, 0)))
    a = sum(conv_w[j] * a_pad[:, j:j + S] for j in range(CONV_WIDTH)) + conv_b
    return (jax.nn.silu(a) * b) @ w_down

def first_inputs(seed: int = 0) -> dict:
    key = jax.random.key(seed)
    ks = iter(jax.random.split(key, 40))

    def w(shape, fan_in):
        return jax.random.normal(next(ks), shape, jnp.float32) * fan_in ** -0.5

    def gain(shape):
        return 1.0 + 0.02 * jax.random.normal(next(ks), shape, jnp.float32)

    x = jax.random.normal(next(ks), (BATCH, SEQ, D_MODEL), jnp.float32)
    mem = jax.random.normal(next(ks), (BATCH, MEM_LEN, D_MODEL), jnp.float32)
    offset = jax.random.randint(next(ks), (BATCH, 1), 0, 4096, dtype=jnp.int32)
    positions = offset + jnp.arange(SEQ, dtype=jnp.int32)[None, :]
    return {
        'x': x, 'mem': mem, 'positions': positions,
        'g_mix': gain((DEPTH, D_MODEL)), 'g_ffn': gain((DEPTH, D_MODEL)),
        'g_mem': gain((D_MODEL,)), 'g_final': gain((D_MODEL,)),
        'w_mem_kv': w((DEPTH, D_MODEL, 2 * MEM_WIDTH), D_MODEL),
        'a_w_in': w((N_A, D_MODEL, sum(A_SPLITS)), D_MODEL),
        'a_kv_norm': gain((N_A, A_KV_RANK)),
        'a_w_uk': w((N_A, A_KV_RANK, A_HEADS, A_NOPE_DIM), A_KV_RANK),
        'a_w_uv': w((N_A, A_KV_RANK, A_HEADS, A_V_DIM), A_KV_RANK),
        'a_w_out': w((N_A, OUT_IN, D_MODEL), OUT_IN),
        'b_w_in': w((N_B, D_MODEL, sum(B_SPLITS)), D_MODEL),
        'b_sinks': 0.5 * jax.random.normal(next(ks), (N_B, B_HEADS), jnp.float32),
        'b_w_out': w((N_B, OUT_IN, D_MODEL), OUT_IN),
        'c_w_in': w((N_C, D_MODEL, sum(C_SPLITS)), D_MODEL),
        'c_w_out': w((N_C, OUT_IN, D_MODEL), OUT_IN),
        'f_w_up': w((DEPTH, D_MODEL, 2 * D_FF), D_MODEL),
        'f_conv_w': w((DEPTH, CONV_WIDTH, D_FF), CONV_WIDTH),
        'f_conv_b': 0.02 * jax.random.normal(next(ks), (DEPTH, D_FF), jnp.float32),
        'f_w_down': w((DEPTH, D_FF, D_MODEL), D_FF),
    }

def first_block(x, mem, positions, g_mix, g_ffn, g_mem, g_final, w_mem_kv,
              a_w_in, a_kv_norm, a_w_uk, a_w_uv, a_w_out,
              b_w_in, b_sinks, b_w_out, c_w_in, c_w_out,
              f_w_up, f_conv_w, f_conv_b, f_w_down):
    cos32, sin32 = rope_tables(positions, A_QK_DIM // ROPE_FRAC)
    cos16, sin16 = rope_tables(positions, B_HEAD_DIM // ROPE_FRAC)
    mem_n = rmsnorm(mem, g_mem)
    for i in range(DEPTH):
        kind, j = i % N_MIXERS, i // N_MIXERS
        h = rmsnorm(x, g_mix[i])
        if kind == 0:
            mix, q_mem = mixer_a(h, cos32, sin32, cos16, sin16, a_w_in[j], a_kv_norm[j], a_w_uk[j], a_w_uv[j])
            w_out = a_w_out[j]
        elif kind == 1:
            mix, q_mem = mixer_b(h, cos16, sin16, b_w_in[j], b_sinks[j])
            w_out = b_w_out[j]
        else:
            mix, q_mem = mixer_c(h, cos32, sin32, c_w_in[j])
            w_out = c_w_out[j]
        mem_o = memory_cross_attention(q_mem, mem_n, w_mem_kv[i])
        x = x + jnp.concatenate([mix, mem_o], axis=-1) @ w_out
        x = x + conv_glu_ffn(rmsnorm(x, g_ffn[i]), f_w_up[i], f_conv_w[i], f_conv_b[i], f_w_down[i])
    return rmsnorm(x, g_final)


DEPTH_2 = 1

GRID_W = 64
CTX_LEN = 256
HEAD_DIM = 64
N_Q_HEADS = 8
N_KV_HEADS = 2
GROUP = N_Q_HEADS // N_KV_HEADS
WINDOW = 128
ROPE_THETA_2 = 10000.0
N_FOURIER_GROUPS = 4
FOURIER_GROUP_CH = 128
FOURIER_W = N_FOURIER_GROUPS * FOURIER_GROUP_CH
Q_W = N_Q_HEADS * HEAD_DIM
KV_W = N_KV_HEADS * HEAD_DIM
IN_W = Q_W + 2 * KV_W + FOURIER_W + 2 * D_MODEL
NEG = -1e30


def rmsnorm_2(x, g):
    xf = x.astype(jnp.float32)
    xf = xf * lax.rsqrt(jnp.mean(xf * xf, axis=-1, keepdims=True) + EPS)
    return xf.astype(x.dtype) * g

def modulate(h, shift, scale):
    return h * (1 + scale) + shift

def adaln(cvec, w_mod, b_mod):
    return jnp.split(jax.nn.silu(cvec) @ w_mod + b_mod, 6, axis=-1)

def axial_rope_tables(rows, dtype):
    row = jnp.repeat(jnp.arange(rows), GRID_W).astype(jnp.float32)
    col = jnp.tile(jnp.arange(GRID_W), rows).astype(jnp.float32)
    half = HEAD_DIM // 2
    inv_freq = ROPE_THETA_2 ** (-jnp.arange(0, half, 2, dtype=jnp.float32) / half)
    ang_r = (row[:, None] * inv_freq)[:, None, :]
    ang_c = (col[:, None] * inv_freq)[:, None, :]
    return tuple(t.astype(dtype) for t in (jnp.cos(ang_r), jnp.sin(ang_r), jnp.cos(ang_c), jnp.sin(ang_c)))

def rotate(x, cos, sin):
    x1, x2 = jnp.split(x, 2, axis=-1)
    return jnp.concatenate([x1 * cos - x2 * sin, x2 * cos + x1 * sin], axis=-1)

def apply_axial_rope(x, tabs):
    cos_r, sin_r, cos_c, sin_c = tabs
    xr, xc = jnp.split(x, 2, axis=-1)
    return jnp.concatenate([rotate(xr, cos_r, sin_r), rotate(xc, cos_c, sin_c)], axis=-1)

def split_proj(p):
    o1 = Q_W
    o2 = o1 + KV_W
    o3 = o2 + KV_W
    o4 = o3 + FOURIER_W
    o5 = o4 + D_MODEL
    return p[..., :o1], p[..., o1:o2], p[..., o2:o3], p[..., o3:o4], p[..., o4:o5], p[..., o5:]

def banded_window_attention_2(q, k, v, k_ctx, v_ctx, sink):
    B, S = q.shape[:2]
    L = k_ctx.shape[1]
    nb = S // BLOCK
    scale = HEAD_DIM ** -0.5
    qb = q.reshape(B, nb, BLOCK, N_KV_HEADS, GROUP, HEAD_DIM)

    def band(t):
        tp = jnp.pad(t, ((0, 0), (BLOCK, BLOCK), (0, 0), (0, 0)))
        tp = tp.reshape(B, nb + 2, BLOCK, N_KV_HEADS, HEAD_DIM)
        return jnp.concatenate([tp[:, :-2], tp[:, 1:-1], tp[:, 2:]], axis=2)

    kw, vw = band(k), band(v)
    s_loc = jnp.einsum('bnqhgd,bnkhd->bnhgqk', qb, kw).astype(jnp.float32) * scale
    s_ctx = jnp.einsum('bnqhgd,blhd->bnhgql', qb, k_ctx).astype(jnp.float32) * scale
    qi = jnp.arange(BLOCK)[:, None]
    kj = jnp.arange(3 * BLOCK)[None, :]
    rel = kj - BLOCK - qi
    kpos = jnp.arange(nb)[:, None, None] * BLOCK + kj[None] - BLOCK
    valid = (jnp.abs(rel) <= WINDOW)[None] & (kpos >= 0) & (kpos < S)
    s_loc = jnp.where(valid[None, :, None, None], s_loc, NEG)
    sink_l = jnp.broadcast_to(sink.astype(jnp.float32).reshape(1, 1, N_KV_HEADS, GROUP, 1, 1),
                              s_loc.shape[:-1] + (1,))
    p = jax.nn.softmax(jnp.concatenate([s_loc, s_ctx, sink_l], axis=-1), axis=-1)
    p_loc = p[..., :3 * BLOCK].astype(v.dtype)
    p_ctx = p[..., 3 * BLOCK:3 * BLOCK + L].astype(v.dtype)
    o = (jnp.einsum('bnhgqk,bnkhd->bnqhgd', p_loc, vw)
         + jnp.einsum('bnhgql,blhd->bnqhgd', p_ctx, v_ctx))
    return o.reshape(B, S, Q_W)

def context_attention(q, k, v, sink):
    B, L = q.shape[:2]
    scale = HEAD_DIM ** -0.5
    qg = q.reshape(B, L, N_KV_HEADS, GROUP, HEAD_DIM)
    s = jnp.einsum('blhgd,bmhd->bhglm', qg, k).astype(jnp.float32) * scale
    sink_l = jnp.broadcast_to(sink.astype(jnp.float32).reshape(1, N_KV_HEADS, GROUP, 1, 1),
                              s.shape[:-1] + (1,))
    p = jax.nn.softmax(jnp.concatenate([s, sink_l], axis=-1), axis=-1)[..., :L].astype(v.dtype)
    o = jnp.einsum('bhglm,bmhd->blhgd', p, v)
    return o.reshape(B, L, Q_W)

def fourier_mix(f):
    B, S = f.shape[:2]
    fg = f.reshape(B, S, N_FOURIER_GROUPS, FOURIER_GROUP_CH).astype(jnp.float32)
    out = jnp.fft.fft2(fg, axes=(1, 3), norm='ortho').real
    return out.reshape(B, S, FOURIER_W).astype(f.dtype)

def merge_branches(attn_o, four_o, g_a, g_f, w_pa, w_pf, w_out):
    m = jax.nn.sigmoid(g_a) * (attn_o @ w_pa) + jax.nn.sigmoid(g_f) * (four_o @ w_pf)
    return m @ w_out

def conv_ffn(h, w_up, conv_w, conv_b, w_down):
    u, gate = jnp.split(h @ w_up, 2, axis=-1)
    up = jnp.pad(u, ((0, 0), (1, 1), (0, 0)))
    u = up[:, :-2] * conv_w[0] + up[:, 1:-1] * conv_w[1] + up[:, 2:] * conv_w[2] + conv_b
    return (jax.nn.silu(u) * gate) @ w_down

def second_inputs(seed: int = 0) -> dict:
    key = jax.random.key(seed)
    ks = jax.random.split(key, 19)
    f32 = jnp.float32
    D = D_MODEL

    def nrm(k, shape, s):
        return jax.random.normal(k, shape, f32) * s

    return {
        'x': nrm(ks[0], (BATCH, SEQ, D), 1.0),
        'c': nrm(ks[1], (BATCH, D), 1.0),
        'ctx': nrm(ks[2], (BATCH, CTX_LEN, D), 1.0),
        'c_ctx': nrm(ks[3], (D,), 1.0),
        'w_mod': nrm(ks[4], (DEPTH_2, D, 6 * D), 0.5 * D ** -0.5),
        'b_mod': nrm(ks[5], (DEPTH_2, 6 * D), 0.01),
        'g_pre1': 1.0 + nrm(ks[6], (DEPTH_2, D), 0.05),
        'g_post1': 1.0 + nrm(ks[7], (DEPTH_2, D), 0.05),
        'g_pre2': 1.0 + nrm(ks[8], (DEPTH_2, D), 0.05),
        'g_post2': 1.0 + nrm(ks[9], (DEPTH_2, D), 0.05),
        'w_in': nrm(ks[10], (DEPTH_2, D, IN_W), D ** -0.5),
        'sink': nrm(ks[11], (DEPTH_2, N_Q_HEADS), 0.5),
        'w_pa': nrm(ks[12], (DEPTH_2, Q_W, D), Q_W ** -0.5),
        'w_pf': nrm(ks[13], (DEPTH_2, FOURIER_W, D), FOURIER_W ** -0.5),
        'w_out': nrm(ks[14], (DEPTH_2, D, D), D ** -0.5),
        'w_up': nrm(ks[15], (DEPTH_2, D, 2 * D_FF), D ** -0.5),
        'conv_w': nrm(ks[16], (DEPTH_2, CONV_WIDTH, D_FF), CONV_WIDTH ** -0.5),
        'conv_b': nrm(ks[17], (DEPTH_2, D_FF), 0.01),
        'w_down': nrm(ks[18], (DEPTH_2, D_FF, D), D_FF ** -0.5),
    }

def second_block(x, c, ctx, c_ctx, w_mod, b_mod, g_pre1, g_post1, g_pre2, g_post2,
              w_in, sink, w_pa, w_pf, w_out, w_up, conv_w, conv_b, w_down):
    B, S, _ = x.shape
    L = ctx.shape[1]
    ROWS = S // GRID_W
    tabs = axial_rope_tables(ROWS, x.dtype)
    for l in range(DEPTH_2):
        last = l == DEPTH_2 - 1
        sh1, sc1, gt1, sh2, sc2, gt2 = [m[:, None] for m in adaln(c, w_mod[l], b_mod[l])]
        csh1, csc1, cgt1, csh2, csc2, cgt2 = adaln(c_ctx, w_mod[l], b_mod[l])

        h = modulate(rmsnorm_2(x, g_pre1[l]), sh1, sc1)
        hc = modulate(rmsnorm_2(ctx, g_pre1[l]), csh1, csc1)
        q, k, v, f, g_a, g_f = split_proj(h @ w_in[l])
        q = apply_axial_rope(q.reshape(B, S, N_Q_HEADS, HEAD_DIM), tabs)
        k = apply_axial_rope(k.reshape(B, S, N_KV_HEADS, HEAD_DIM), tabs)
        v = v.reshape(B, S, N_KV_HEADS, HEAD_DIM)
        if last:
            pc = hc @ w_in[l, :, :Q_W + 2 * KV_W]
        else:
            pc = hc @ w_in[l]
        kc = pc[..., Q_W:Q_W + KV_W].reshape(B, L, N_KV_HEADS, HEAD_DIM)
        vc = pc[..., Q_W + KV_W:Q_W + 2 * KV_W].reshape(B, L, N_KV_HEADS, HEAD_DIM)

        attn = banded_window_attention_2(q, k, v, kc, vc, sink[l])
        y = merge_branches(attn, fourier_mix(f), g_a, g_f, w_pa[l], w_pf[l], w_out[l])
        x = x + gt1 * rmsnorm_2(y, g_post1[l])

        if not last:
            qc, _, _, fc, g_ac, g_fc = split_proj(pc)
            attn_c = context_attention(qc.reshape(B, L, N_Q_HEADS, HEAD_DIM), kc, vc, sink[l])
            yc = merge_branches(attn_c, fourier_mix(fc), g_ac, g_fc, w_pa[l], w_pf[l], w_out[l])
            ctx = ctx + cgt1 * rmsnorm_2(yc, g_post1[l])

        h2 = modulate(rmsnorm_2(x, g_pre2[l]), sh2, sc2)
        x = x + gt2 * rmsnorm_2(conv_ffn(h2, w_up[l], conv_w[l], conv_b[l], w_down[l]), g_post2[l])

        if not last:
            hc2 = modulate(rmsnorm_2(ctx, g_pre2[l]), csh2, csc2)
            ctx = ctx + cgt2 * rmsnorm_2(conv_ffn(hc2, w_up[l], conv_w[l], conv_b[l], w_down[l]), g_post2[l])
    return x


def setup_inputs(seed=0):
    out = dict(first_inputs(seed))
    for name, value in second_inputs(seed + 1).items():
        if name != "x":
            out[name + "_2"] = value
    return out


def reference(
    x, mem, positions, g_mix, g_ffn, g_mem, g_final, w_mem_kv, a_w_in, a_kv_norm, a_w_uk,
    a_w_uv, a_w_out, b_w_in, b_sinks, b_w_out, c_w_in, c_w_out, f_w_up, f_conv_w, f_conv_b,
    f_w_down, c_2, ctx_2, c_ctx_2, w_mod_2, b_mod_2, g_pre1_2, g_post1_2, g_pre2_2, g_post2_2,
    w_in_2, sink_2, w_pa_2, w_pf_2, w_out_2, w_up_2, conv_w_2, conv_b_2, w_down_2,
):
    x = first_block(
        x, mem, positions, g_mix, g_ffn, g_mem, g_final, w_mem_kv, a_w_in, a_kv_norm, a_w_uk,
        a_w_uv, a_w_out, b_w_in, b_sinks, b_w_out, c_w_in, c_w_out, f_w_up, f_conv_w, f_conv_b,
        f_w_down,
    )
    return second_block(
        x, c_2, ctx_2, c_ctx_2, w_mod_2, b_mod_2, g_pre1_2, g_post1_2, g_pre2_2, g_post2_2,
        w_in_2, sink_2, w_pa_2, w_pf_2, w_out_2, w_up_2, conv_w_2, conv_b_2, w_down_2,
    )


_drawn_inputs = setup_inputs


def setup_inputs(seed=0):
    import zlib

    import numpy as np

    out = dict(_drawn_inputs(seed))
    spreads = {}
    factors = {'g_mem': 8.0,
     'a_kv_norm': 8.0,
     'b_sinks': 22.042,
     'f_conv_b': 3.744,
     'b_mod_2': 3.682,
     'g_pre1_2': 3.705,
     'g_post1_2': 4.058,
     'g_pre2_2': 2.72,
     'g_post2_2': 4.01,
     'sink_2': 8.0,
     'conv_b_2': 25.784,
     'g_ffn': 3.285}
    for name, (base, spread) in spreads.items():
        noise = np.random.default_rng([zlib.crc32(name.encode()), seed]).standard_normal(out[name].shape)
        drawn = base * np.exp(spread * noise) if base else spread * noise
        out[name] = __import__('jax').numpy.asarray(drawn.astype(out[name].dtype))
    for name, factor in factors.items():
        out[name] = (out[name] * factor).astype(out[name].dtype)
    return out
```

```python
import math
from contextlib import ExitStack

import numpy as np

import concourse.bass as bass
from concourse import mybir

F32 = mybir.dt.float32
F32R = mybir.dt.float32r
I32 = mybir.dt.int32
ALU = mybir.AluOpType
ACT = mybir.ActivationFunctionType
AX = mybir.AxisListType

P = 128
S = 512
ROWT = S // P
D = 1024
DC = D // P
MEM = 256
FF = 2816
FC = FF // P
HALF = FC // 2
KB = 1024
EPS = 1e-6
NEG = -1e30
PICKED = -3e38
TOPK = 128
A_HEADS = 8
IDX_HEADS = 16
KV_RANK = 256

PARAMS = [("g_mix", 16), ("g_ffn", 16), ("g_mem", 8), ("g_final", 8), ("g_pre1", 8), ("g_post1", 8),
          ("g_pre2", 8), ("g_post2", 8), ("kv_norm", 2), ("conv0", 4 * FC), ("conv1", 4 * FC),
          ("conv2", 4 * FC), ("b_mod", 48), ("cvec", 16), ("sink_b", 16), ("sink_c", 8)]
PCOL, _n = {}, 0
for _name, _w in PARAMS:
    PCOL[_name] = _n
    _n += _w
NPARAM = _n

CONSTS = [("ge", P), ("z0", P), ("le", P), ("z1", P), ("z2", P), ("z3", P), ("ge2", P), ("gt", P), ("le2", P),
          ("ident", P), ("dft_c", 2 * P), ("inv32", 1), ("inv16", 1), ("sgn32", 1), ("sgn16", 1), ("eps", 1)]
CCOL, _n = {}, 0
for _name, _w in CONSTS:
    CCOL[_name] = _n
    _n += _w
NCONST = _n


def constants():
    q, k = np.arange(P)[:, None], np.arange(P)[None, :]
    c = np.zeros((P, NCONST), np.float32)

    def put(name, a):
        c[:, CCOL[name]:CCOL[name] + a.shape[1]] = a

    ge, le, gt = (np.where(ok, 0.0, NEG).astype(np.float32) for ok in (k >= q, k <= q, k > q))
    for name, a in (("ge", ge), ("ge2", ge), ("le", le), ("le2", le), ("gt", gt)):
        put(name, a)
    put("ident", np.eye(P, dtype=np.float32))
    ang = 2 * np.pi * ((q * k) % P) / P
    put("dft_c", np.concatenate([np.cos(ang), np.sin(ang)], 1).astype(np.float32))
    p = np.arange(P)
    for name, head, rot in (("32", 128, 32), ("16", 64, 16)):
        d, half = p % head, rot // 2
        inv = np.float32(500000.0) ** (-(2.0 * (d % half)).astype(np.float32) / np.float32(rot))
        put("inv" + name, np.where(d < rot, inv, 0.0).astype(np.float32)[:, None])
        put("sgn" + name, np.where(d < half, -1.0, 1.0).astype(np.float32)[:, None])
    put("eps", np.full((P, 1), EPS, np.float32))
    s = np.arange(S)
    d = p % 64
    inv = np.float32(10000.0) ** (-(2.0 * (d % 16)).astype(np.float32) / np.float32(32))
    at = np.where((d < 32)[:, None], (s // 64)[None, :], (s % 64)[None, :]).astype(np.float32)
    ang = at * inv[:, None]
    sgn = np.where(d % 32 < 16, -1.0, 1.0)[:, None]
    axial = np.stack([np.cos(ang), np.sin(ang) * sgn], 1).astype(np.float32)
    i = np.arange(S)
    ang = 2 * np.pi * ((i[:, None] * i[None, :]) % S) / S
    rows = np.concatenate([np.cos(ang), -np.sin(ang)], 1) / math.sqrt(S * P)
    rows = rows.astype(np.float32).reshape(ROWT, P, 2 * S).transpose(1, 0, 2)
    return c, axial, np.ascontiguousarray(rows)


STREAM = [("memkv", 4, 2048, [2, 2, 2, 2]),
          ("a_in", 11, 2048, [2, 3, 2, 2, 2, 2, 2, 2, 2, 2, 2]),
          ("mod", 24, 2048, 1), ("uk", 1, 2048, 8), ("uv", 1, 2048, 8),
          ("a_out", 8, 1280, 1),
          ("up00", HALF, 2048, 2), ("dn00", 8, HALF * P, 1), ("up01", HALF, 2048, 2), ("dn01", 8, HALF * P, 1),
          ("b_in", 7, 2048, [2, 2, 2, 2, 2, 4, 2]), ("b_out", 8, 1280, 1),
          ("up10", HALF, 2048, 2), ("dn10", 8, HALF * P, 1), ("up11", HALF, 2048, 2), ("dn11", 8, HALF * P, 1),
          ("ctx", 1, 2048, 3),
          ("c_in", 13, 2048, [2, 2, 5] + [2] * 10),
          ("merge", 4, 2048, 4), ("c_out", 4, 2048, 2),
          ("up20", HALF, 2048, 2), ("dn20", 8, HALF * P, 1), ("up21", HALF, 2048, 2), ("dn21", 8, HALF * P, 1)]


def units(w, width):
    k, n = w.shape
    return w.reshape(k // P, P, n // width, width).transpose(2, 1, 0, 3).reshape(n // width, P, -1)


def lay_out(x):
    w = {}
    kv = x["w_mem_kv"]
    w["memkv"] = np.concatenate([units(kv[0], 256), units(kv[1], 256)])
    a = x["a_w_in"][0]
    q, ckv, kr, qi, ki, wi, qm = np.split(a, np.cumsum([1024, 256, 32, 1024, 64, 16]).tolist(), axis=1)
    misc = np.concatenate([kr, wi, np.zeros((D, 80), np.float32), ki, ki], 1)
    w["a_in"] = units(np.concatenate([ckv, misc, qi, q, qm], 1), 256)
    w["mod"] = units(x["w_mod_2"][0], 256)
    uk = x["a_w_uk"][0]
    w["uk"] = units(np.concatenate([np.zeros((KV_RANK, 8, 32), np.float32), uk], 2).reshape(KV_RANK, 1024), 1024)
    w["uv"] = units(x["a_w_uv"][0].reshape(KV_RANK, 1024), 1024)
    w["a_out"] = units(x["a_w_out"][0], P)
    pair8 = [h for c in range(4) for h in (c, c + 4)]
    pair16 = pair8 + [h + 8 for h in pair8]
    b = x["b_w_in"][0]
    bq = b[:, :1024].reshape(D, 16, 64)[:, pair16].reshape(D, 1024)
    w["b_in"] = units(np.concatenate([bq, b[:, 1024:]], 1), 256)
    bo = x["b_w_out"][0]
    w["b_out"] = units(np.concatenate([bo[:1024].reshape(16, 64, D)[pair16].reshape(1024, D), bo[1024:]]), P)
    ups = [x["f_w_up"][0], x["f_w_up"][1], x["w_up_2"][0]]
    downs = [x["f_w_down"][0], x["f_w_down"][1], x["w_down_2"][0]]
    for l in range(3):
        up = ups[l].reshape(DC, P, 2, FC, P).transpose(3, 1, 0, 2, 4).reshape(FC, P, 2048)
        down = downs[l].reshape(2, HALF, P, DC, P).transpose(0, 3, 2, 1, 4).reshape(2, DC, P, HALF * P)
        for h in range(2):
            w[f"up{l}{h}"] = up[h * HALF:(h + 1) * HALF]
            w[f"dn{l}{h}"] = down[h]
    c = x["w_in_2"][0]
    w["ctx"] = units(c[:, 512:768], 256)
    cq = c[:, :512].reshape(D, 8, 64)[:, pair8].reshape(D, 512)
    w["c_in"] = units(np.concatenate([cq, c[:, 512:]], 1), 256)
    pa = x["w_pa_2"][0].reshape(8, 64, D)[pair8].reshape(512, D)
    w["merge"] = np.concatenate([units(pa, 256), units(x["w_pf_2"][0], 256)], 2)
    w["c_out"] = units(x["w_out_2"][0], 256)
    w["up"] = None
    del w["up"]

    def cols(v):
        return v.reshape(-1, P).T

    def conv(cw, cb):
        return np.stack([cols(cw[0]), cols(cw[1]), cols(cw[2]), cols(cb)], 2).reshape(P, 4 * FC)

    sink_b = np.broadcast_to(x["b_sinks"][0][pair16], (P, 16))
    sink_c = np.broadcast_to(x["sink_2"][0][pair8], (P, 8))
    cvec = np.stack([cols(x["c_2"]), cols(x["c_ctx_2"])], 2).reshape(P, 16)
    params = np.concatenate([
        cols(x["g_mix"]), cols(x["g_ffn"]), cols(x["g_mem"]), cols(x["g_final"]), cols(x["g_pre1_2"]),
        cols(x["g_post1_2"]), cols(x["g_pre2_2"]), cols(x["g_post2_2"]), cols(x["a_kv_norm"]),
        conv(x["f_conv_w"][0], x["f_conv_b"][0]), conv(x["f_conv_w"][1], x["f_conv_b"][1]),
        conv(x["conv_w_2"][0], x["conv_b_2"][0]), cols(x["b_mod_2"]), cvec, sink_b, sink_c], 1)

    def turned(t):
        n = t.shape[1]
        return t[0].reshape(n, DC, P).transpose(2, 1, 0)

    return w, params, turned(x["x"]), turned(x["mem"]), turned(x["ctx_2"])


class Phase:

    def __init__(self, name, n, size, tiles, land, split):
        self.name, self.n, self.size, self.tiles = name, n, size, tiles
        self.land = land
        self.split = split
        self.done = None
        self.free = None

    def before(self, u):
        return sum(self.tiles[:u]) if isinstance(self.tiles, list) else u * self.tiles

    @property
    def total(self):
        return self.before(self.n)


class Chain:

    def __init__(self, eng, sem):
        self.eng, self.sem, self.n, self.off = eng, sem, 0, 0

    def step(self, ins):
        ins.then_inc(self.sem, 1)
        self.n += 1
        self.eng.wait_ge(self.sem, self.off + self.n)


def each_unit(eng, n, body, chain=None):
    if n < 8:
        for u in range(n):
            body(u // 2, u % 2)
        return
    at = chain.n if chain else 0
    body(0, 0)
    body(0, 1)
    per = chain.n - at if chain else 0
    last = (n - 1) // 2
    with eng.Fori(1, last) as i:
        if chain:
            chain.off = i * per - per
        body(i, 0)
        body(i, 1)
    if chain:
        chain.off = 0
        chain.n = at + per * last
    for u in range(2 * last, n):
        body(u // 2, u % 2)


def program(nc, wdram, params_d, const_d, axial_d, rows_d, x_d, mem_d, ctx_d, pos_d, out_d):
    ctx = ExitStack()
    with ctx:
        def sem(name):
            return ctx.enter_context(nc.semaphore(name))

        base = (nc.sbuf_base + 63) // 64 * 64

        def at(name, kb, shape, dt=F32):
            return nc.alloc_sbuf_tensor_at(name, [P] + shape, dt, offset=base + int(kb * KB))

        XT = at("xT", 0, [DC, S])
        HH, HL = at("h_hi", 16, [10, S], F32R), at("h_lo", 36, [10, S], F32R)
        RAW = [at(f"raw{i}", 56 + 8 * i, [2048]) for i in range(2)]
        HI = [at(f"w_hi{i}", 72 + 8 * i, [2048], F32R) for i in range(2)]
        LO = [at(f"w_lo{i}", 88 + 8 * i, [2048], F32R) for i in range(2)]
        R = 104
        MEMT = at("memT", R, [DC, MEM])
        AQ = at("a_q", R, [8, S])
        AQI, AK = at("a_q_idx", R + 16, [8, S]), at("a_k", R + 16, [8, S])
        CKV, KIDX, KROPE = at("c_kv", R + 32, [2, S]), at("k_idx", R + 36, [S]), at("k_rope", R + 38, [S])
        AV = at("a_v", R + 32, [ROWT, 1024])
        PICK = at("picked", R + 48, [3, S])
        CH, CL = at("c_hi", R + 56, [2, S], F32R), at("c_lo", R + 60, [2, S], F32R)
        WIDX = at("w_idx", R + 54, [ROWT, IDX_HEADS])
        QM = at("q_mem", R + 184 - 104 + 10, [2, S])
        GH, GL = at("g_hi", R, [HALF, S], F32R), at("g_lo", R + 22, [HALF, S], F32R)
        BQ, BK, BV = at("b_q", R, [8, S]), at("b_k", R + 16, [2, S]), at("b_v", R + 20, [ROWT, 256])
        CTXT = at("ctxT", R + 48, [DC, MEM])
        GA, GF = at("gate_a", R, [8, S]), at("gate_f", R + 16, [8, S])
        CQ, CK, CV = at("c_q", R + 32, [4, S]), at("c_k", R + 40, [S]), at("c_v", R + 42, [ROWT, P])
        FT = at("f_t", R + 44, [4, S])
        F1 = [at(f"f_rows{i}", R + 52 + 4 * i, [ROWT, 256]) for i in range(2)]
        MH, ML = at("m_hi", R + 32, [8, S], F32R), at("m_lo", R + 48, [8, S], F32R)
        Y = at("y", R, [DC, S])
        Y2 = at("y2", R + 44, [DC, S])
        C32, S32, C16, S16 = (at(n, R + 64 + 2 * i, [S]) for i, n in enumerate(("cos32", "sin32", "cos16", "sin16")))
        MK = [at(f"mem_k{l}", R + 72 + 4 * l, [2, MEM]) for l in range(2)]
        MV = [at(f"mem_v{l}", R + 74 + 4 * l, [2, 256]) for l in range(2)]
        DFT = at("dft_rows", R + 64, [ROWT, 1024])
        T = at("work", R + 80, [7, S])
        TW = at("work_flat", R + 80, [7 * S])
        small = [R + 94.0]

        def after(name, shape):
            t = at(name, small[0], shape)
            small[0] += -(-4 * math.prod(shape) // 32) * 32 / KB
            return t

        CST, PRM, ONES = after("const", [NCONST]), after("params", [NPARAM]), after("ones", [P])
        MODV, DER, SV = after("mod", [48, 2]), after("derived", [5, 8]), after("silu_c", [16])
        ST, M8 = after("stats", [2, 12]), after("top8", [8])
        CKX, CVX = at("ctx_k", 32, [MEM]), at("ctx_v", 33, [2, P])
        assert base + small[0] * KB <= nc.sbuf_usable_end
        AXC, AXS = C16, S16
        POS = at("positions", 184 + 8, [S], I32)

        ps = ctx.enter_context(nc.psum_tensor("psum", [P, 8 * S], F32))

        def bank(b, a=0, z=S):
            return ps[:, b * S + a:b * S + z]

        def par(name, k, n=1):
            return PRM[:, PCOL[name] + k:PCOL[name] + k + n]

        def cst(name, n=1, off=0):
            return CST[:, CCOL[name] + off:CCOL[name] + off + n]

        PH, land, split = {}, 0, 0
        for name, n, size, tiles in STREAM:
            ph = PH[name] = Phase(name, n, size, tiles, land, split)
            ph.done, ph.free = sem(f"{name}_done"), sem(f"{name}_read")
            land += n
            if name != "mod":
                split += n
        order = [PH[s[0]] for s in STREAM]
        split_order = [p for p in order if p.name != "mod"]

        raw_landed = [sem("raw_landed0"), sem("raw_landed1")]
        hi_ready, lo_ready = sem("w_hi_ready"), sem("w_lo_ready")

        NORMS = {}
        nb = sc = 0
        for i, (name, nch, rows, splits) in enumerate([
                ("mem", 8, MEM, True), ("mix0", 8, S, True), ("ckv", 2, S, True), ("ffn0", 8, S, True),
                ("mix1", 8, S, True), ("ffn1", 8, S, True), ("final", 8, S, False), ("ctx", 8, MEM, True),
                ("pre1", 8, S, True), ("post1", 8, S, False), ("pre2", 8, S, True), ("post2", 8, S, False)]):
            NORMS[name] = (i, nch, rows, nb, sc)
            nb += nch
            sc += nch if splits else 0
        square_ready, square_used, root_ready = sem("square_ready"), sem("square_used"), sem("root_ready")
        scaled_ready, h_hi_ready, h_ready = sem("scaled_ready"), sem("h_hi_ready"), sem("h_ready")
        x_ready = sem("x_ready")
        XR = {"final": 0, "post1": 8, "post2": 16}

        steps, flushes = [], []

        def add_steps(group, last_of, chunk):
            for n, s in enumerate(group):
                s["flush"] = len(flushes) + n // last_of
                s["first"] = n % last_of == 0
                s["last"] = n % last_of == last_of - 1
            for n in range(len(group) // last_of):
                flushes.append(chunk + n)
            lo = len(steps)
            steps.extend(group)
            return lo, len(steps)

        def q_tile(buf, c, j, t):
            return buf[64 * j:64 * j + 64, c, t * P:(t + 1) * P]

        def mem_steps(l):
            return [dict(nh=2, nk=256, mask=None, scale=0.125, sink=None,
                         qk=[(j * S, q_tile(QM, c, j, t), MK[l][64 * j:64 * j + 64, c, :]) for j in range(2)],
                         pv=[[(MV[l][:, kb_, (2 * c + j) * 64:(2 * c + j + 1) * 64]) for kb_ in range(2)] for j in range(2)],
                         out=[(64 * j, 64, t) for j in range(2)])
                    for c in range(2) for t in range(ROWT)]

        a_range = add_steps(
            [dict(nh=1, nk=(t + 1) * P, mask=cst("le", P) if t == 0 else PICK[:, t - 1, 0:(t + 1) * P],
                  scale=128 ** -0.5, sink=None,
                  qk=[(0, AQ[:, h, t * P:(t + 1) * P], AK[:, h, 0:(t + 1) * P])],
                  pv=[[AV[:, kb_, h * P:(h + 1) * P] for kb_ in range(t + 1)]], out=[(0, P, t)])
             for h in range(8) for t in range(ROWT)], ROWT, 0)
        am_range = add_steps(mem_steps(0), ROWT, 8)
        b_range = add_steps(
            [dict(nh=2, nk=min(t + 1, 2) * P, mask=cst("le", P) if t == 0 else cst("gt", 2 * P), scale=0.125,
                  sink=par("sink_b", 2 * c, 2),
                  qk=[(j * S, q_tile(BQ, c, j, t),
                       BK[64 * j:64 * j + 64, c // 4, max(t - 1, 0) * P:(t + 1) * P]) for j in range(2)],
                  pv=[[BV[:, kb_, (2 * (c // 4) + j) * 64:(2 * (c // 4) + j + 1) * 64]
                       for kb_ in range(max(t - 1, 0), t + 1)] for j in range(2)],
                  out=[(64 * j, 64, t) for j in range(2)])
             for c in range(8) for t in range(ROWT)], ROWT, 0)
        bm_range = add_steps(mem_steps(1), ROWT, 8)

        def c_step(c, j, t):
            rows = slice(64 * j, 64 * j + 64)
            q = q_tile(CQ, c, j, t)
            k = [CK[rows, b * P:(b + 1) * P] for b in range(ROWT)]
            v = [CV[:, b, 64 * j:64 * j + 64] for b in range(ROWT)]
            kx = [CKX[rows, b * P:(b + 1) * P] for b in range(2)]
            vx = [CVX[:, b, 64 * j:64 * j + 64] for b in range(2)]
            if t == 0:
                mask, ks, vs = "z0", [k[0], k[1], *kx], [v[0], v[1], *vx]
            elif t == ROWT - 1:
                mask, ks, vs = "z1", [k[t], *kx, k[t - 1]], [v[t], *vx, v[t - 1]]
            else:
                mask, ks, vs = "ge", [*k[t - 1:t + 2], *kx], [*v[t - 1:t + 2], *vx]
            n = len(ks)
            return dict(nh=1, nk=n * P, mask=cst(mask, n * P), scale=0.125, sink=par("sink_c", 2 * c + j, 1),
                        qk=[(b * P, q, ks[b]) for b in range(n)], pv=[vs], out=[(64 * j, 64, t)])

        c_range = add_steps([c_step(c, j, t) for c in range(4) for j in range(2) for t in range(ROWT)], 2 * ROWT, 0)
        scores_done, max_ready, exp_done, p_ready = sem("scores_done"), sem("max_ready"), sem("exp_done"), sem("p_ready")
        turned_done, turned_ready, pv_done = sem("turned_done"), sem("turned_ready"), sem("pv_done")
        o_hi_ready, o_ready = sem("o_hi_ready"), sem("o_ready")

        def flushed(rng):
            return steps[rng[1] - 1]["flush"] + 1

        load_const, load_x, load_mem = sem("load_const"), sem("load_x"), sem("load_mem")
        load_ctx, load_tab = sem("load_ctx"), sem("load_tables")
        ones_ready, tables_ready = sem("ones_ready"), sem("tables_ready")
        angle_ready = sem("angle_ready")
        silu_c_ready, mod_ready = sem("silu_c_ready"), sem("mod_ready")
        idx_done, relu_ready, idx_summed = sem("idx_done"), sem("relu_ready"), sem("idx_summed")
        conv_ready, silu_ready, g_ready = sem("conv_ready"), sem("silu_ready"), sem("g_ready")
        qkv_ready = sem("qkv_ready")
        f1_done, f1_ready, f2_done, f2_hi, four_ready = (sem(n) for n in (
            "f1_done", "f1_ready", "f2_done", "f2_hi_ready", "four_ready"))
        m_ready, m_hi, m_lo = sem("m_ready"), sem("m_hi_ready"), sem("m_lo_ready")
        vec_steps, act_steps = sem("vector_steps"), sem("scalar_steps")
        out_landed = sem("out_landed")

        block = ctx.enter_context(nc.Block())

        @block.sync
        def _(sp):
            def occupant_read(p):
                if p < 2:
                    return
                ph = max((q for q in order if q.land <= p - 2), key=lambda q: q.land)
                u = p - 2 - ph.land
                if ph.name == "mod":
                    sp.wait_ge(ph.done, u + 1)
                else:
                    sp.wait_ge(lo_ready, ph.split + u + 1)

            for ph in order:
                def load(i, j, ph=ph):
                    slot = (ph.land + j) % 2
                    if isinstance(i, int) and i == 0:
                        occupant_read(ph.land + j)
                    elif ph.name == "mod":
                        sp.wait_ge(ph.done, 2 * i + j - 1)
                    else:
                        sp.wait_ge(lo_ready, 2 * i + (j - 1 + ph.split))
                    u = 2 * i + j
                    src = wdram[ph.name][u] if isinstance(u, int) else \
                        wdram[ph.name][bass.ds(u, 1), :, :].rearrange("a p n -> p (a n)")
                    sp.dma_start(RAW[slot][:, 0:ph.size], src).then_inc(raw_landed[slot], 16)
                each_unit(sp, ph.n, load)
            for c in range(DC):
                sp.wait_ge(x_ready, XR["post2"] + c + 1)
                sp.dma_start(out_d[:, c, :], XT[:, c, :]).then_inc(out_landed, 16)
            sp.wait_ge(out_landed, 16 * DC)

        @block.gpsimd
        def _(pool):
            pool.memset(ONES[:], 1.0).then_inc(ones_ready, 1)
            for ph in split_order:
                def low(i, j, ph=ph):
                    slot = (ph.split + j) % 2
                    pool.wait_ge(hi_ready, 2 * i + (j + ph.split + 1))
                    nc.gpsimd.tensor_tensor(LO[slot][:, 0:ph.size], RAW[slot][:, 0:ph.size],
                                            HI[slot][:, 0:ph.size].bitcast(F32), ALU.subtract).then_inc(lo_ready, 1)
                each_unit(pool, ph.n, low)

        @block.scalar
        def _(act):
            chain = Chain(act, act_steps)

            def hi_unit(ph, i, j):
                slot = (ph.split + j) % 2
                act.wait_ge(raw_landed[slot], i * 16 + 16 * ((ph.land + j) // 2 + 1))
                if not isinstance(i, int) or i > 0:
                    act.wait_ge(ph.done, ph.before(2 * i + j - 1))
                elif ph.split + j >= 2:
                    g = ph.split + j - 2
                    q = max((q for q in split_order if q.split <= g), key=lambda q: q.split)
                    act.wait_ge(q.done, q.before(g - q.split + 1))
                nc.scalar.activation(HI[slot][:, 0:ph.size], RAW[slot][:, 0:ph.size], ACT.Copy).then_inc(hi_ready, 1)

            def next_hi(ph, i, j):
                if isinstance(i, int) and 2 * i + j == ph.n - 1:
                    k = split_order.index(ph) + 1
                    if ph.name != "a_in" and k < len(split_order):
                        hi_unit(split_order[k], 0, 0)
                elif j == 0:
                    hi_unit(ph, i, 1)
                else:
                    hi_unit(ph, i + 1, 0)

            def stream_only(ph):
                each_unit(act, ph.n, lambda i, j: next_hi(ph, i, j))

            def norm(name, src, ready, free=None, dst=(HH, HL), width=D, root_free=()):
                i, nch, rows, b, s = NORMS[name]
                for k in range(nch):
                    for w in ready(k):
                        act.wait_ge(*w)
                    if k >= 2:
                        act.wait_ge(square_used, b + k - 1)
                    nc.scalar.activation(T[:, k % 2, 0:rows], src(k), ACT.Square).then_inc(square_ready, 1)
                for w in root_free:
                    act.wait_ge(*w)
                act.wait_ge(square_used, b + nch)
                nc.scalar.activation(T[:, 2, 0:rows], bank(4, 0, rows), ACT.Sqrt, bias=cst("eps"),
                                     scale=1.0 / width).then_inc(root_ready, 1)
                if free is not None:
                    for w in free:
                        act.wait_ge(*w)
                    for k in range(nch):
                        act.wait_ge(scaled_ready, s + k + 1)
                        nc.scalar.activation(dst[0][:, k, 0:rows], T[:, 4 + k % 2, 0:rows], ACT.Copy).then_inc(h_hi_ready, 1)

            def attend(rng):
                lo, hi = rng

                def exps(s):
                    st, W = steps[s], steps[s]["nk"]
                    act.wait_ge(max_ready, s + 1)
                    if st["mask"] is None and s >= 2:
                        act.wait_ge(turned_done, s - 1)
                    for n in range(st["nh"]):
                        sm = TW[:, (s % 2) * 640 + n * W:(s % 2) * 640 + (n + 1) * W]
                        src = sm if st["mask"] is not None else ps[:, (s % 2) * 1024 + n * S:(s % 2) * 1024 + n * S + W]
                        last = nc.scalar.activation(sm, src, ACT.Exp, bias=ST[:, s % 2, 2 + n:3 + n], scale=st["scale"],
                                                    accum_out=ST[:, s % 2, 4 + n:5 + n])
                        if st["sink"] is not None:
                            last = nc.scalar.activation(ST[:, s % 2, 6 + n:7 + n], st["sink"][:, n:n + 1], ACT.Exp,
                                                        bias=ST[:, s % 2, 2 + n:3 + n])
                    last.then_inc(exp_done, 1)

                def turned(s):
                    W = steps[s]["nk"] * steps[s]["nh"]
                    act.wait_ge(turned_done, s + 1)
                    if s >= 2:
                        act.wait_ge(pv_done, s - 1)
                    b0 = (4 + s % 2) * S if W <= S and rng is not c_range else 4 * S
                    nc.scalar.activation(TW[:, 1280 + (s % 2) * 640:1280 + (s % 2) * 640 + W], ps[:, b0:b0 + W],
                                         ACT.Copy).then_inc(turned_ready, 1)

                def flush(s):
                    f = steps[s]["flush"]
                    act.wait_ge(pv_done, s + 1)
                    nc.scalar.activation(HH[:, flushes[f], :], bank(6 + f % 2), ACT.Copy).then_inc(o_hi_ready, 1)

                for s in range(lo, hi):
                    exps(s)
                    if s > lo:
                        turned(s - 1)
                    if s >= lo + 3 and steps[s - 3]["last"]:
                        flush(s - 3)
                turned(hi - 1)
                for s in range(max(lo, hi - 3), hi):
                    if steps[s]["last"]:
                        flush(s)

            def ffn_up(ph, first):
                def body(i, j):
                    next_hi(ph, i, j)
                    act.wait_ge(conv_ready, 2 * i + (j + 1 + first))
                    nc.scalar.activation(T[:, 2 + j, :], T[:, j, :], ACT.Silu).then_inc(silu_ready, 1)
                each_unit(act, ph.n, body)

            act.dma_start(MEMT[:], mem_d).then_inc(load_mem, 16)
            act.dma_start(CST[:], const_d).then_inc(load_const, 16)
            act.dma_start(PRM[:], params_d).then_inc(load_const, 16)
            act.dma_start(POS[:], pos_d.partition_broadcast(P)).then_inc(load_const, 16)
            act.dma_start(XT[:], x_d).then_inc(load_x, 16)

            act.wait_ge(load_const, 48)
            nc.scalar.activation(SV[:], par("cvec", 0, 16), ACT.Silu).then_inc(silu_c_ready, 1)
            for n, dst in enumerate((C32, S32, C16, S16)):
                act.wait_ge(angle_ready, n + 1)
                nc.scalar.activation(dst[:], T[:, 3 + n, :], ACT.Sin).then_inc(tables_ready, 1)
            act.wait_ge(tables_ready, 6)
            norm("mem", lambda k: MEMT[:, k, :], lambda k: [(load_mem, 16)], free=[])

            ph = PH["memkv"]
            hi_unit(ph, 0, 0)
            for u in range(4):
                next_hi(ph, u // 2, u % 2)
                l, v = u // 2, u % 2
                for c in range(2):
                    act.wait_ge(ph.done, 2 * u + c + 1)
                    b = (u % 2) * 2 + c
                    dst = MV[l][:, c, :] if v else MK[l][:, c, :]
                    nc.scalar.activation(dst, bank(b, 0, 256), ACT.Copy).then_inc(ph.free, 1)

            norm("mix0", lambda k: XT[:, k, :], lambda k: [(load_x, 16)], free=[(ph.done, ph.total)])

            ph = PH["a_in"]
            for u in range(11):
                next_hi(ph, u // 2, u % 2)
                if u == 0:
                    for c in range(2):
                        act.wait_ge(ph.done, c + 1)
                        nc.scalar.activation(CKV[:, c, :], bank(c), ACT.Copy).then_inc(ph.free, 1)
                if u == 1:
                    act.wait_ge(ph.done, ph.before(1) + 3)
                    nc.scalar.activation(WIDX[:], bank(5, 0, 64).rearrange("p (t h) -> p t h", h=16), ACT.Copy,
                                         scale=1.0 / 32).then_inc(qkv_ready, 1)
                if u == 2:
                    norm("ckv", lambda k: CKV[:, k, :], lambda k: [(ph.free, 2)], free=[], dst=(CH, CL), width=KV_RANK,
                         root_free=[(ph.free, 8)])
                if u == 10:
                    for c in range(2):
                        act.wait_ge(ph.done, ph.before(10) + c + 1)
                        nc.scalar.activation(QM[:, c, :], bank((u % 2) * 2 + c), ACT.Copy).then_inc(qkv_ready, 1)

            n = 0
            for t in range(1, ROWT):
                W = (t + 1) * P
                for h in range(IDX_HEADS):
                    act.wait_ge(idx_done, n + 1)
                    if n >= 2:
                        act.wait_ge(idx_summed, n - 1)
                    nc.scalar.activation(T[:, n % 2, 0:W], bank(4 + n % 3, 0, W), ACT.Relu).then_inc(relu_ready, 1)
                    n += 1

            uk, uv = PH["uk"], PH["uv"]
            hi_unit(uk, 0, 0)
            hi_unit(uv, 0, 0)
            for h in range(8):
                act.wait_ge(uk.done, h + 1)
                nc.scalar.activation(AK[:, h, :], bank(h % 4), ACT.Copy).then_inc(uk.free, 1)
                act.wait_ge(uk.free, h + 1)
                nc.scalar.activation(AK[0:32, h, :], KROPE[0:32, :], ACT.Copy).then_inc(qkv_ready, 1)
            act.wait_ge(qkv_ready, 11)
            for n in range(8):
                act.wait_ge(uv.done, n + 1)
                nc.scalar.activation(AV[:, n // 2, (n % 2) * S:(n % 2 + 1) * S], bank(n % 4), ACT.Copy).then_inc(uv.free, 1)
            hi_unit(PH["a_out"], 0, 0)
            attend(a_range)
            attend(am_range)
            stream_only(PH["a_out"])

            def ffn(l, first):
                for h in range(2):
                    ffn_up(PH[f"up{l}{h}"], first + h * HALF)
                    stream_only(PH[f"dn{l}{h}"])

            norm("ffn0", lambda k: XT[:, k, :], lambda k: [(PH["a_out"].free, k + 1)], free=[(PH["a_out"].done, 8)])
            ffn(0, 0)
            norm("mix1", lambda k: XT[:, k, :], lambda k: [(PH["dn01"].free, k + 1)], free=[(PH["up01"].done, 22)])

            ph = PH["b_in"]
            for u in range(7):
                next_hi(ph, u // 2, u % 2)
                if u == 5:
                    for t in range(ROWT):
                        act.wait_ge(ph.done, ph.before(5) + t + 1)
                        nc.scalar.activation(BV[:, t, :], bank(t, 0, 256), ACT.Copy).then_inc(qkv_ready, 1)
                if u == 6:
                    for c in range(2):
                        act.wait_ge(ph.done, ph.before(6) + c + 1)
                        nc.scalar.activation(QM[:, c, :], bank(c), ACT.Copy).then_inc(qkv_ready, 1)
            attend(b_range)
            attend(bm_range)
            stream_only(PH["b_out"])
            norm("ffn1", lambda k: XT[:, k, :], lambda k: [(PH["b_out"].free, k + 1)], free=[(PH["b_out"].done, 8)])
            ffn(1, 22)

            act.wait_ge(o_ready, flushed(bm_range))
            act.dma_start(AXC[:], axial_d[:, 0, :]).then_inc(load_tab, 16)
            act.dma_start(AXS[:], axial_d[:, 1, :]).then_inc(load_tab, 16)
            act.wait_ge(PH["dn11"].done, 8)
            act.dma_start(CTXT[:], ctx_d).then_inc(load_ctx, 16)
            norm("final", lambda k: XT[:, k, :], lambda k: [(PH["dn11"].free, k + 1)])
            norm("ctx", lambda k: CTXT[:, k, :], lambda k: [(load_ctx, 16), (x_ready, 8)], free=[])
            ph = PH["ctx"]
            next_hi(ph, 0, 0)
            act.wait_ge(ph.done, 1)
            nc.scalar.activation(CKX[:], bank(0, 0, MEM), ACT.Copy).then_inc(ph.free, 1)
            for t in range(2):
                act.wait_ge(ph.done, t + 2)
                nc.scalar.activation(CVX[:, t, :], bank(1 + t, 0, P), ACT.Copy).then_inc(ph.free, 1)
            norm("pre1", lambda k: XT[:, k, :], lambda k: [(x_ready, XR["final"] + k + 1)], free=[(ph.done, 3)])

            ph = PH["c_in"]
            for u in range(13):
                next_hi(ph, u // 2, u % 2)
                if u == 2:
                    for t in range(ROWT):
                        act.wait_ge(ph.done, ph.before(2) + t + 2)
                        nc.scalar.activation(CV[:, t, :], bank(4 + t, 0, P), ACT.Copy).then_inc(qkv_ready, 1)
                for c in range(2):
                    if u >= 3:
                        act.wait_ge(ph.done, ph.before(u) + c + 1)
                        b = (u % 2) * 2 + c
                        if u == 3 and c == 0:
                            act.wait_ge(ph.free, 5)
                        if u < 5:
                            nc.scalar.activation(FT[:, 2 * (u - 3) + c, :], bank(b), ACT.Copy).then_inc(ph.free, 1)
                        else:
                            dst = (GA if u < 9 else GF)[:, 2 * ((u - 5) % 4) + c, :]
                            nc.scalar.activation(dst, bank(b), ACT.Sigmoid).then_inc(ph.free, 1)
            act.wait_ge(PH["c_in"].free, PH["c_in"].total - 4)
            act.dma_start(DFT[:], rows_d).then_inc(load_tab, 16)
            attend(c_range)
            for g in range(4):
                for t2 in range(2):
                    act.wait_ge(f1_done, 2 * g + t2 + 1)
                    if g >= 2:
                        act.wait_ge(f2_done, g - 1)
                    nc.scalar.activation(F1[g % 2][:, 2 * t2:2 * t2 + 2, :],
                                         bank(t2).rearrange("p (t n) -> p t n", t=2), ACT.Copy).then_inc(f1_ready, 1)
                act.wait_ge(f2_done, g + 1)
                nc.scalar.activation(HH[:, 4 + g, :], bank(2 + g % 2), ACT.Copy).then_inc(f2_hi, 1)

            ph = PH["merge"]
            for u in range(4):
                next_hi(ph, u // 2, u % 2)
                for c in range(2):
                    m = 2 * u + c
                    act.wait_ge(m_ready, m + 1)
                    nc.scalar.activation(MH[:, m, :], T[:, 4 + m % 2, :], ACT.Copy).then_inc(m_hi, 1)
            stream_only(PH["c_out"])
            norm("post1", lambda k: Y[:, k, :], lambda k: [(PH["c_out"].free, k + 1)])
            norm("pre2", lambda k: XT[:, k, :], lambda k: [(x_ready, XR["post1"] + k + 1)], free=[(PH["c_out"].done, 8)])
            ffn(2, 44)
            norm("post2", lambda k: Y2[:, k, :], lambda k: [(PH["dn21"].free, k + 1)])

        @block.vector
        def _(v):
            chain = Chain(v, vec_steps)
            step = chain.step

            def norm(name, src, gain, shift=None, dst=(HH, HL), into=None):
                i, nch, rows, b, s = NORMS[name]
                v.wait_ge(root_ready, i + 1)
                step(nc.vector.reciprocal(T[:, 3, 0:rows], T[:, 2, 0:rows]))

                def low(k):
                    v.wait_ge(h_hi_ready, s + k + 1)
                    nc.vector.tensor_tensor(dst[1][:, k, 0:rows], T[:, 4 + k % 2, 0:rows],
                                            dst[0][:, k, 0:rows].bitcast(F32), ALU.subtract).then_inc(h_ready, 1)

                for k in range(nch):
                    if into is not None:
                        out = src(k) if into == "self" else T[:, 4 + k % 2, 0:rows]
                        ins = nc.vector.scalar_tensor_tensor(out=out, in0=src(k), scalar=gain(k), in1=T[:, 3, 0:rows],
                                                             op0=ALU.mult, op1=ALU.mult)
                        if into == "self":
                            ins.then_inc(x_ready, 1)
                        else:
                            step(ins)
                            nc.vector.tensor_tensor(XT[:, k, :], XT[:, k, :], out, ALU.add).then_inc(x_ready, 1)
                        continue
                    t = T[:, 4 + k % 2, 0:rows]
                    if k >= 2:
                        v.wait_ge(h_ready, s + k - 1)
                    ins = nc.vector.scalar_tensor_tensor(out=t, in0=src(k), scalar=gain(k), in1=T[:, 3, 0:rows],
                                                         op0=ALU.mult, op1=ALU.mult)
                    if shift is not None:
                        step(ins)
                        ins = nc.vector.tensor_scalar(t, t, shift(k), None, ALU.add)
                    ins.then_inc(scaled_ready, 1)
                    if k >= 1:
                        low(k - 1)
                if into is None:
                    low(nch - 1)

            ropes = []

            def rope(src, dst, cos, sin, half, done, count, n=P):
                sw = T[0:n, 2 + len(ropes) % 2, :]
                if len(ropes) >= 2:
                    v.wait_ge(*ropes[-2])
                ropes.append((done, count))
                mask = [i + half if i < half else i - half if i < 2 * half else i for i in range(32)]
                if half == 16:
                    mask = [(i + 16) % 32 for i in range(32)]
                step(nc.vector.stream_shuffle(sw, src, mask))
                step(nc.vector.tensor_tensor(sw, sw, sin[0:n, :], ALU.mult))
                step(nc.vector.tensor_tensor(dst, src, cos[0:n, :], ALU.mult))
                nc.vector.tensor_tensor(dst, dst, sw, ALU.add).then_inc(done, 1)

            def attend(rng):
                lo, hi = rng

                def maxes(s):
                    st, W = steps[s], steps[s]["nk"]
                    v.wait_ge(scores_done, s + 1)
                    if s >= 2:
                        v.wait_ge(turned_done, s - 1)
                        v.wait_ge(exp_done, s - 1)
                    o = ST[:, s % 2, :]
                    for n in range(st["nh"]):
                        src = ps[:, (s % 2) * 1024 + n * S:(s % 2) * 1024 + n * S + W]
                        if st["mask"] is None:
                            ins = nc.vector.tensor_reduce(o[:, n:n + 1], src, AX.X, ALU.max)
                        else:
                            ins = nc.vector.tensor_tensor_reduce(
                                TW[:, (s % 2) * 640 + n * W:(s % 2) * 640 + (n + 1) * W], src, st["mask"], 1.0, PICKED,
                                ALU.add, ALU.max, o[:, n:n + 1])
                    step(ins)
                    nh = st["nh"]
                    if st["sink"] is None:
                        nc.vector.tensor_scalar(o[:, 2:2 + nh], o[:, 0:nh], -st["scale"], None, ALU.mult).then_inc(max_ready, 1)
                    else:
                        step(nc.vector.scalar_tensor_tensor(out=o[:, 8:8 + nh], in0=o[:, 0:nh], scalar=st["scale"],
                                                            in1=st["sink"], op0=ALU.mult, op1=ALU.max))
                        nc.vector.tensor_scalar(o[:, 2:2 + nh], o[:, 8:8 + nh], -1.0, None, ALU.mult).then_inc(max_ready, 1)

                def probs(s):
                    st, W = steps[s], steps[s]["nk"]
                    nh, o = st["nh"], ST[:, s % 2, :]
                    v.wait_ge(exp_done, s + 1)
                    if st["sink"] is not None:
                        step(nc.vector.tensor_tensor(o[:, 4:4 + nh], o[:, 4:4 + nh], o[:, 6:6 + nh], ALU.add))
                    step(nc.vector.reciprocal(o[:, 10:10 + nh], o[:, 4:4 + nh]))
                    for n in range(nh):
                        sm = TW[:, (s % 2) * 640 + n * W:(s % 2) * 640 + (n + 1) * W]
                        ins = nc.vector.tensor_scalar(sm, sm, o[:, 10 + n:11 + n], None, ALU.mult)
                    ins.then_inc(p_ready, 1)

                def flush(s):
                    f = steps[s]["flush"]
                    v.wait_ge(o_hi_ready, f + 1)
                    nc.vector.tensor_tensor(HL[:, flushes[f], :], bank(6 + f % 2), HH[:, flushes[f], :].bitcast(F32),
                                            ALU.subtract).then_inc(o_ready, 1)

                maxes(lo)
                for s in range(lo, hi):
                    if s + 1 < hi:
                        maxes(s + 1)
                    probs(s)
                    if s - 2 >= lo and steps[s - 2]["last"]:
                        flush(s - 2)
                for s in range(max(lo, hi - 2), hi):
                    if steps[s]["last"]:
                        flush(s)

            def residual(ph, dst, mode):
                def body(i, j):
                    v.wait_ge(ph.done, 2 * i + j + 1)
                    c = 2 * i + j
                    d = dst[:, c, :] if isinstance(c, int) else dst[:, bass.ds(c, 1), :].rearrange("p a n -> p (a n)")
                    if mode == "add":
                        nc.vector.tensor_tensor(d, bank(j), d, ALU.add).then_inc(ph.free, 1)
                    else:
                        nc.vector.tensor_scalar(d, bank(j), 1.0, None, ALU.mult).then_inc(ph.free, 1)
                each_unit(v, ph.n, body)

            def ffn_up(ph, l, h, first, before):
                taps = [(0, 2), (1, 1), (2, 0)] if l < 2 else [(0, 1), (1, 0), (2, -1)]
                col = PCOL[f"conv{l}"] + 4 * h * HALF
                for w in before:
                    v.wait_ge(*w)

                def body(i, j):
                    u = 2 * i + j

                    def w(tap):
                        if isinstance(u, int):
                            return PRM[:, col + 4 * u + tap:col + 4 * u + tap + 1]
                        return PRM[:, bass.ds(u * 4 + (col + tap), 1)]

                    def chunk(buf):
                        return buf[:, u, :] if isinstance(u, int) else buf[:, bass.ds(u, 1), :].rearrange("p a n -> p (a n)")

                    a, b, t = bank(2 * j), bank(2 * j + 1), T[:, j, :]
                    mid = next(k for k, sft in taps if sft == 0)
                    v.wait_ge(ph.done, 2 * u + 1)
                    step(nc.vector.tensor_scalar(t, a, w(mid), w(3), ALU.mult, ALU.add))
                    rest = [x for x in taps if x[1] != 0]
                    for k, sft in rest:
                        o, s_ = (slice(sft, S), slice(0, S - sft)) if sft > 0 else (slice(0, S + sft), slice(-sft, S))
                        ins = nc.vector.scalar_tensor_tensor(out=t[:, o], in0=a[:, s_], scalar=w(k), in1=t[:, o],
                                                             op0=ALU.mult, op1=ALU.add)
                        if k == rest[-1][0]:
                            ins.then_inc(conv_ready, 1)
                        else:
                            step(ins)
                    v.wait_ge(ph.done, 2 * u + 2)
                    v.wait_ge(silu_ready, 2 * i + (j + 1 + first))
                    g = T[:, 4 + j, :]
                    nc.vector.tensor_tensor(g, b, T[:, 2 + j, :], ALU.mult).then_inc(ph.free, 1)
                    v.wait_ge(ph.free, u + 1)
                    step(nc.vector.tensor_scalar(chunk(GH), g, 1.0, None, ALU.mult))
                    nc.vector.tensor_tensor(chunk(GL), g, chunk(GH).bitcast(F32), ALU.subtract).then_inc(g_ready, 1)
                each_unit(v, ph.n, body, chain)

            def ffn(l, dst, modes):
                for h in range(2):
                    before = [(PH[f"dn{l}0"].done, 8)] if h else []
                    ffn_up(PH[f"up{l}{h}"], l, h, (2 * l + h) * HALF, before)
                    residual(PH[f"dn{l}{h}"], dst, modes[h])

            TWO_PI = 2 * math.pi
            C1 = 6.28125
            C2 = float(np.float32(round((TWO_PI - C1) * 2 ** 20) / 2 ** 20))
            C3 = TWO_PI - C1 - C2
            MAGIC = 1.5 * 2 ** 23
            PI = 3.1415925
            v.wait_ge(load_const, 48)
            step(nc.vector.tensor_copy(T[:, 0, :], POS[:]))
            for n, (name, quarter) in enumerate((("32", True), ("32", False), ("16", True), ("16", False))):
                ang, turns, red = T[:, 1, :], T[:, 2, :], T[:, 3 + n, :]
                step(nc.vector.tensor_scalar(ang, T[:, 0, :], cst("inv" + name), None, ALU.mult))
                step(nc.vector.tensor_scalar(turns, ang, 1 / TWO_PI, 0.25 if quarter else 0.0, ALU.mult, ALU.add))
                step(nc.vector.tensor_scalar(turns, turns, MAGIC, None, ALU.add))
                step(nc.vector.tensor_scalar(turns, turns, MAGIC, None, ALU.subtract))
                for k, c in enumerate((C1, C2, C3)):
                    step(nc.vector.scalar_tensor_tensor(out=red if k else red, in0=turns, scalar=-c, in1=red if k else ang,
                                                        op0=ALU.mult, op1=ALU.add))
                if quarter:
                    step(nc.vector.tensor_scalar(red, red, math.pi / 2, None, ALU.add))
                nc.vector.tensor_scalar(red, red, PI, -PI, ALU.min, ALU.max).then_inc(angle_ready, 1)
            v.wait_ge(tables_ready, 4)
            for k, (tab, name) in enumerate(((S32, "32"), (S16, "16"))):
                nc.vector.tensor_scalar(tab[:], tab[:], cst("sgn" + name), None, ALU.mult).then_inc(tables_ready, 1)
            v.wait_ge(tables_ready, 6)

            norm("mem", lambda k: MEMT[:, k, :], lambda k: par("g_mem", k))
            norm("mix0", lambda k: XT[:, k, :], lambda k: par("g_mix", k))

            ph = PH["a_in"]
            v.wait_ge(ph.free, 2)
            v.wait_ge(ph.done, ph.before(1) + 1)
            rope(bank(2)[0:32, :], KROPE[0:32, :], C32, S32, 16, ph.free, 3, 32)
            v.wait_ge(ph.done, ph.before(1) + 2)
            rope(bank(3), KIDX[:], C16, S16, 8, ph.free, 4)
            v.wait_ge(ph.free, 4)

            def q_unit(u, dst, n, cos, sin, half):
                for c in range(2):
                    v.wait_ge(ph.done, ph.before(u) + c + 1)
                    rope(bank((u % 2) * 2 + c), dst[:, n + c, :], cos, sin, half, ph.free, 2 * u + c + 1)

            for u in range(2, 6):
                q_unit(u, AQI, 2 * (u - 2), C16, S16, 8)
                if u == 3:
                    norm("ckv", lambda k: CKV[:, k, :], lambda k: par("kv_norm", k), dst=(CH, CL))
            for u in range(6, 10):
                q_unit(u, AQ, 2 * (u - 6), C32, S32, 16)

            for t in range(1, ROWT):
                acc = PICK[:, t - 1, :]
                step(nc.vector.memset(acc[:, 0:t * P], 0.0))
                step(nc.vector.tensor_copy(acc[:, t * P:(t + 1) * P], cst("le", P)))
            v.wait_ge(qkv_ready, 1)
            n = 0
            for t in range(1, ROWT):
                W = (t + 1) * P
                acc = PICK[:, t - 1, 0:W]
                for h in range(IDX_HEADS):
                    v.wait_ge(relu_ready, n + 1)
                    nc.vector.scalar_tensor_tensor(out=acc, in0=T[:, n % 2, 0:W], scalar=WIDX[:, t, h:h + 1], in1=acc,
                                                   op0=ALU.mult, op1=ALU.add).then_inc(idx_summed, 1)
                    n += 1
                    v.wait_ge(idx_summed, n)
            for t in range(1, ROWT):
                acc = PICK[:, t - 1, 0:(t + 1) * P]
                for _ in range(TOPK // 8):
                    step(nc.vector.max(M8[:], acc))
                    step(nc.vector.match_replace(acc, M8[:], acc, PICKED))
                step(nc.vector.tensor_scalar(acc, acc, PICKED / 2, NEG, ALU.is_gt, ALU.mult))

            v.wait_ge(PH["mod"].done, 24)
            for w in range(2):
                nc.vector.tensor_tensor(MODV[:, :, w], bank(7, 0, 96).rearrange("p (n w) -> p n w", w=2)[:, :, w],
                                        par("b_mod", 0, 48), ALU.add).then_inc(mod_ready, 1)
            v.wait_ge(mod_ready, 2)
            for n, (g, col, w, one) in enumerate((("g_pre1", 8, 0, 1), ("g_pre1", 8, 1, 1), ("g_post1", 16, 0, 0),
                                                  ("g_pre2", 32, 0, 1), ("g_post2", 40, 0, 0))):
                step(nc.vector.scalar_tensor_tensor(out=DER[:, n, :], in0=MODV[:, col:col + 8, w], scalar=float(one),
                                                    in1=par(g, 0, 8), op0=ALU.add, op1=ALU.mult))

            attend(a_range)
            attend(am_range)
            residual(PH["a_out"], XT, "add")

            norm("ffn0", lambda k: XT[:, k, :], lambda k: par("g_ffn", k))
            ffn(0, XT, ("add", "add"))
            norm("mix1", lambda k: XT[:, k, :], lambda k: par("g_mix", 8 + k))

            ph = PH["b_in"]
            for u in range(4):
                q_unit(u, BQ, 2 * u, C16, S16, 8)
            q_unit(4, BK, 0, C16, S16, 8)
            attend(b_range)
            attend(bm_range)
            residual(PH["b_out"], XT, "add")
            norm("ffn1", lambda k: XT[:, k, :], lambda k: par("g_ffn", 8 + k))
            ffn(1, XT, ("add", "add"))

            norm("final", lambda k: XT[:, k, :], lambda k: par("g_final", k), into="self")
            norm("ctx", lambda k: CTXT[:, k, :], lambda k: DER[:, 1, k:k + 1], shift=lambda k: MODV[:, k, 1:2])
            norm("pre1", lambda k: XT[:, k, :], lambda k: DER[:, 0, k:k + 1], shift=lambda k: MODV[:, k, 0:1])
            ph = PH["c_in"]
            v.wait_ge(load_tab, 32)
            for u in range(2):
                q_unit(u, CQ, 2 * u, AXC, AXS, 16)
            v.wait_ge(ph.done, ph.before(2) + 1)
            rope(bank(0), CK[:], AXC, AXS, 16, ph.free, 5)
            attend(c_range)
            for g in range(4):
                v.wait_ge(f2_hi, g + 1)
                nc.vector.tensor_tensor(HL[:, 4 + g, :], bank(2 + g % 2), HH[:, 4 + g, :].bitcast(F32),
                                        ALU.subtract).then_inc(four_ready, 1)
            ph = PH["merge"]
            for u in range(4):
                for c in range(2):
                    m = 2 * u + c
                    v.wait_ge(ph.done, 4 * u + c + 1)
                    step(nc.vector.tensor_tensor(T[:, c, :], bank(c), GA[:, m, :], ALU.mult))
                    v.wait_ge(ph.done, 4 * u + c + 3)
                    step(nc.vector.tensor_tensor(T[:, 2 + c, :], bank(2 + c), GF[:, m, :], ALU.mult))
                    t = T[:, 4 + m % 2, :]
                    nc.vector.tensor_tensor(t, T[:, c, :], T[:, 2 + c, :], ALU.add).then_inc(m_ready, 1)
                    v.wait_ge(m_hi, m + 1)
                    nc.vector.tensor_tensor(ML[:, m, :], t, MH[:, m, :].bitcast(F32), ALU.subtract).then_inc(m_lo, 1)
            ph = PH["c_out"]
            for u in range(4):
                for c in range(2):
                    v.wait_ge(ph.done, 2 * u + c + 1)
                    nc.vector.tensor_copy(Y[:, 2 * u + c, :], bank((u % 2) * 2 + c)).then_inc(ph.free, 1)
            norm("post1", lambda k: Y[:, k, :], lambda k: DER[:, 2, k:k + 1], into="x")
            norm("pre2", lambda k: XT[:, k, :], lambda k: DER[:, 3, k:k + 1], shift=lambda k: MODV[:, 24 + k, 0:1])
            ffn(2, Y2, ("copy", "add"))
            norm("post2", lambda k: Y2[:, k, :], lambda k: DER[:, 4, k:k + 1], into="x")

        @block.tensor
        def _(pe):
            last_read = {}

            def bank_free(b):
                if b in last_read:
                    pe.wait_ge(*last_read[b])

            def products(out, pairs):
                n = len(pairs)
                for k, (wh, wl, ah, al, swap, ready) in enumerate(pairs):
                    if ready is not None:
                        pe.wait_ge(*ready)
                    for m, (w, a) in enumerate(((wh, ah), (wh, al), (wl, ah))):
                        l, r = (a, w) if swap else (w, a)
                        ins = nc.tensor.matmul(out, l, r, start=(k == 0 and m == 0), stop=(k == n - 1 and m == 2))
                return ins

            def gemm(ph, kc, width, act_hi, act_lo, rows=S, ready=None, banks=None):
                t = ph.tiles
                period = 2 * t

                def body(i, j):
                    u = 2 * i + j
                    slot = (ph.split + j) % 2
                    pe.wait_ge(lo_ready, 2 * i + (j + ph.split + 1))
                    for c in range(t):
                        b = j * t + c
                        if isinstance(i, int) and i == 0:
                            bank_free(b)
                        elif ph.name.startswith("up"):
                            pe.wait_ge(ph.free, u - 1)
                        else:
                            pe.wait_ge(ph.free, u * t + (c + 1 - period))
                        products(bank(b, 0, rows), [
                            (HI[slot][:, k * width + c * P:k * width + (c + 1) * P],
                             LO[slot][:, k * width + c * P:k * width + (c + 1) * P],
                             act_hi[:, k, 0:rows], act_lo[:, k, 0:rows], False,
                             ready(k) if ready is not None and isinstance(u, int) and u == 0 and c == 0 else None)
                            for k in range(kc)]).then_inc(ph.done, 1)
                each_unit(pe, ph.n, body)
                for u in range(max(0, ph.n - 2), ph.n):
                    for c in range(t):
                        last_read[(u % 2) * t + c] = (ph.free, u + 1 if ph.name.startswith("up") else u * t + c + 1)

            def t_tiles(ph, u, cs, bs, width=256, rows=S, ah=HH, al=HL, kc=DC, ready=None):
                slot = (ph.split + u) % 2
                for n, (c, b) in enumerate(zip(cs, bs)):
                    bank_free(b)
                    products(bank(b, 0, rows), [
                        (HI[slot][:, k * width + c * P:k * width + (c + 1) * P],
                         LO[slot][:, k * width + c * P:k * width + (c + 1) * P], ah[:, k, 0:rows], al[:, k, 0:rows],
                         False, ready(k) if ready and n == 0 else None) for k in range(kc)]).then_inc(ph.done, 1)

            def r_tiles(ph, u, rts, bs, lo, n, width=256, kc=DC, ah=HH, al=HL):
                slot = (ph.split + u) % 2
                for rt, b in zip(rts, bs):
                    bank_free(b)
                    products(bank(b, 0, n), [
                        (HI[slot][:, k * width + lo:k * width + lo + n], LO[slot][:, k * width + lo:k * width + lo + n],
                         ah[:, k, rt * P:(rt + 1) * P], al[:, k, rt * P:(rt + 1) * P], True, None)
                        for k in range(kc)]).then_inc(ph.done, 1)

            def unit_ready(ph, u):
                pe.wait_ge(lo_ready, ph.split + u + 1)

            def norm(name):
                i, nch, rows, b, s = NORMS[name]
                bank_free(4)
                for k in range(nch):
                    pe.wait_ge(square_ready, b + k + 1)
                    nc.tensor.matmul(bank(4, 0, rows), ONES[:], T[:, k % 2, 0:rows], start=(k == 0),
                                     stop=(k == nch - 1)).then_inc(square_used, 1)
                last_read[4] = (root_ready, i + 1)

            def h_chunk(name):
                s = NORMS[name][4]
                return lambda k: (h_ready, s + k + 1)

            def attend(rng):
                lo, hi = rng

                def scores(s):
                    st = steps[s]
                    b0 = (s % 2) * 1024
                    if s < lo + 2:
                        bank_free((s % 2) * 2)
                        bank_free((s % 2) * 2 + 1)
                    for off, q, k in st["qk"]:
                        n = k.shape[-1]
                        ins = nc.tensor.matmul(ps[:, b0 + off:b0 + off + n], q, k, start=True, stop=True)
                    ins.then_inc(scores_done, 1)

                def turn(s):
                    st = steps[s]
                    W = st["nk"] * st["nh"]
                    wide = rng is c_range
                    b0 = 4 * S if wide else (4 + s % 2) * S
                    pe.wait_ge(p_ready, s + 1)
                    back = 1 if wide else 2
                    if s >= lo + back:
                        pe.wait_ge(turned_ready, s + 1 - back)
                    else:
                        bank_free(4)
                        bank_free(5)
                    for n in range(W // P):
                        ins = nc.tensor.transpose(ps[:, b0 + n * P:b0 + (n + 1) * P],
                                                  TW[:, (s % 2) * 640 + n * P:(s % 2) * 640 + (n + 1) * P], cst("ident", P))
                    ins.then_inc(turned_done, 1)

                def values(s):
                    st = steps[s]
                    f = st["flush"]
                    pe.wait_ge(turned_ready, s + 1)
                    if st["first"]:
                        if f >= 2 and f - 2 >= steps[lo]["flush"]:
                            pe.wait_ge(o_ready, f - 1)
                        else:
                            bank_free(6 + f % 2)
                    kb_n = st["nk"] // P
                    for n in range(st["nh"]):
                        p0, m, t = st["out"][n]
                        for b in range(kb_n):
                            c0 = 1280 + (s % 2) * 640 + (n * kb_n + b) * P
                            ins = nc.tensor.matmul(ps[p0:p0 + m, (6 + f % 2) * S + t * P:(6 + f % 2) * S + (t + 1) * P],
                                                   st["pv"][n][b], TW[:, c0:c0 + P], start=(b == 0), stop=(b == kb_n - 1))
                    ins.then_inc(pv_done, 1)
                    if st["last"]:
                        last_read[6 + f % 2] = (o_ready, f + 1)

                scores(lo)
                scores(lo + 1)
                for s in range(lo, hi):
                    turn(s)
                    if s + 2 < hi:
                        scores(s + 2)
                    values(s)
                for b in range(4):
                    last_read[b] = (exp_done, hi)
                last_read[4] = last_read[5] = (turned_ready, hi)

            pe.wait_ge(ones_ready, 1)
            norm("mem")
            ph = PH["memkv"]
            for u in range(4):
                unit_ready(ph, u)
                b = (u % 2) * 2
                if u >= 2:
                    last_read[b], last_read[b + 1] = (ph.free, 2 * u - 3), (ph.free, 2 * u - 2)
                if u % 2 == 0:
                    t_tiles(ph, u, (0, 1), (b, b + 1), rows=MEM, ready=h_chunk("mem") if u == 0 else None)
                else:
                    r_tiles(ph, u, (0, 1), (b, b + 1), 0, 256)
            for b in range(4):
                last_read[b] = (ph.free, 5 + b)

            norm("mix0")
            ph = PH["a_in"]
            for u in range(11):
                unit_ready(ph, u)
                b = (u % 2) * 2
                t_tiles(ph, u, (0, 1), (b, b + 1), ready=h_chunk("mix0") if u == 0 else None)
                last_read[b], last_read[b + 1] = (ph.free, 2 * u + 1), (ph.free, 2 * u + 2)
                if u == 1:
                    slot = (ph.split + u) % 2
                    bank_free(5)
                    for rt in range(ROWT):
                        ins = products(bank(5, rt * 16, rt * 16 + 16), [
                            (HI[slot][:, k * 256 + 32:k * 256 + 48], LO[slot][:, k * 256 + 32:k * 256 + 48],
                             HH[:, k, rt * P:(rt + 1) * P], HL[:, k, rt * P:(rt + 1) * P], True, None)
                            for k in range(DC)])
                    ins.then_inc(ph.done, 1)
                    last_read[5] = (qkv_ready, 1)
                if u == 3:
                    norm("ckv")
            for b in (0, 1):
                last_read[b] = (qkv_ready, 2 + b)

            n = 0
            pe.wait_ge(ph.free, 20)
            for t in range(1, ROWT):
                for h in range(IDX_HEADS):
                    b = 4 + n % 3
                    if n >= 3:
                        pe.wait_ge(relu_ready, n - 2)
                    else:
                        bank_free(b)
                    j = h % 2
                    nc.tensor.matmul(bank(b, 0, (t + 1) * P), AQI[64 * j:64 * j + 64, h // 2, t * P:(t + 1) * P],
                                     KIDX[64 * j:64 * j + 64, 0:(t + 1) * P], start=True, stop=True).then_inc(idx_done, 1)
                    n += 1
            for b in (4, 5, 6):
                last_read[b] = (relu_ready, n)

            ph = PH["mod"]
            pe.wait_ge(silu_c_ready, 1)

            def mod_unit(i, j):
                slot = (ph.land + j) % 2
                pe.wait_ge(raw_landed[slot], i * 16 + 16 * ((ph.land + j) // 2 + 1))
                for c in range(2):
                    col = (2 * i + j) * 4 + 2 * c
                    out = bank(7, col, col + 2) if isinstance(col, int) else ps[:, bass.ds(col + 7 * S, 2)]
                    for k in range(DC):
                        ins = nc.tensor.matmul(out, RAW[slot][:, k * 256 + c * P:k * 256 + (c + 1) * P],
                                               SV[:, 2 * k:2 * k + 2], start=(k == 0), stop=(k == DC - 1))
                ins.then_inc(ph.done, 1)
            each_unit(pe, ph.n, mod_unit)

            ph = PH["uk"]
            unit_ready(ph, 0)
            pe.wait_ge(h_ready, NORMS["ckv"][4] + 2)
            for h in range(8):
                if h >= 4:
                    last_read[h % 4] = (ph.free, h - 3)
                t_tiles(ph, 0, (h,), (h % 4,), width=1024, ah=CH, al=CL, kc=2)
            for b in range(4):
                last_read[b] = (ph.free, 5 + b)
            ph = PH["uv"]
            unit_ready(ph, 0)
            for n in range(8):
                if n >= 4:
                    last_read[n % 4] = (ph.free, n - 3)
                r_tiles(ph, 0, (n // 2,), (n % 4,), (n % 2) * S, S, width=1024, kc=2, ah=CH, al=CL)
            for b in range(4):
                last_read[b] = (ph.free, 5 + b)
            pe.wait_ge(ph.free, 8)
            last_read[7] = (mod_ready, 2)
            attend(a_range)
            attend(am_range)
            gemm(PH["a_out"], 10, P, HH, HL, ready=lambda k: (o_ready, flushed(am_range)))

            def ffn(l, name):
                for h in range(2):
                    gemm(PH[f"up{l}{h}"], DC, 256, HH, HL, ready=h_chunk(name) if h == 0 else None)
                    gemm(PH[f"dn{l}{h}"], HALF, P, GH, GL, ready=lambda k: (g_ready, (2 * l + h) * HALF + k + 1))

            norm("ffn0")
            ffn(0, "ffn0")
            norm("mix1")
            ph = PH["b_in"]
            for u in range(7):
                unit_ready(ph, u)
                b = (u % 2) * 2
                if u == 5:
                    last_read.update({2: (ph.free, 7), 3: (ph.free, 8), 0: (ph.free, 9), 1: (ph.free, 10)})
                    r_tiles(ph, u, range(4), range(4), 0, 256)
                    for t in range(4):
                        last_read[t] = (qkv_ready, 11 + t + 1)
                else:
                    t_tiles(ph, u, (0, 1), (b, b + 1), ready=h_chunk("mix1") if u == 0 else None)
                    if u < 5:
                        last_read[b], last_read[b + 1] = (ph.free, 2 * u + 1), (ph.free, 2 * u + 2)
            for b in (0, 1):
                last_read[b] = (qkv_ready, 16 + b)
            pe.wait_ge(qkv_ready, 17)
            pe.wait_ge(ph.free, 10)
            attend(b_range)
            attend(bm_range)
            gemm(PH["b_out"], 10, P, HH, HL, ready=lambda k: (o_ready, flushed(bm_range)))
            norm("ffn1")
            ffn(1, "ffn1")

            norm("final")
            norm("ctx")
            ph = PH["ctx"]
            unit_ready(ph, 0)
            t_tiles(ph, 0, (0,), (0,), rows=MEM, ready=h_chunk("ctx"))
            r_tiles(ph, 0, (0, 1), (1, 2), P, P)
            for b in range(3):
                last_read[b] = (ph.free, b + 1)
            norm("pre1")
            ph = PH["c_in"]
            for u in range(13):
                unit_ready(ph, u)
                b = (u % 2) * 2
                if u == 2:
                    t_tiles(ph, u, (0,), (0,))
                    last_read[0] = (ph.free, 5)
                    last_read[1] = (ph.free, 2)
                    last_read[4] = (root_ready, NORMS["pre1"][0] + 1)
                    r_tiles(ph, u, range(4), range(4, 8), P, P)
                    for t in range(4):
                        last_read[4 + t] = (qkv_ready, 17 + t + 1)
                    continue
                t_tiles(ph, u, (0, 1), (b, b + 1), ready=h_chunk("pre1") if u == 0 else None)
                n = 2 * u + 1 if u < 2 else 2 * u
                last_read[b], last_read[b + 1] = (ph.free, n), (ph.free, n + 1)
            pe.wait_ge(qkv_ready, 21)
            pe.wait_ge(ph.free, 5)
            attend(c_range)
            pe.wait_ge(load_tab, 48)
            for g in range(4):
                for t2 in range(2):
                    if g:
                        pe.wait_ge(f1_ready, 2 * g - 1 + t2)
                    else:
                        bank_free(t2)
                    for t in range(2):
                        rt = 2 * t2 + t
                        ins = nc.tensor.matmul(bank(t2, t * 256, t * 256 + 256), FT[:, g, rt * P:(rt + 1) * P],
                                               cst("dft_c", 256), start=True, stop=True)
                    ins.then_inc(f1_done, 1)
                pe.wait_ge(f1_ready, 2 * g + 2)
                if g >= 2:
                    pe.wait_ge(four_ready, g - 1)
                for n in range(8):
                    rt, part = n // 2, n % 2
                    ins = nc.tensor.matmul(bank(2 + g % 2), F1[g % 2][:, rt, part * P:(part + 1) * P],
                                           DFT[:, rt, part * S:(part + 1) * S], start=(n == 0), stop=(n == 7))
                ins.then_inc(f2_done, 1)

            last_read.update({0: (f1_ready, 7), 1: (f1_ready, 8), 2: (four_ready, 3), 3: (four_ready, 4)})
            ph = PH["merge"]
            pe.wait_ge(o_ready, flushed(c_range))
            pe.wait_ge(four_ready, 4)
            for u in range(4):
                unit_ready(ph, u)
                slot = (ph.split + u) % 2
                for part in range(2):
                    for c in range(2):
                        b = 2 * part + c
                        bank_free(b)
                        products(bank(b), [
                            (HI[slot][:, 1024 * part + k * 256 + c * P:1024 * part + k * 256 + (c + 1) * P],
                             LO[slot][:, 1024 * part + k * 256 + c * P:1024 * part + k * 256 + (c + 1) * P],
                             HH[:, 4 * part + k, :], HL[:, 4 * part + k, :], False, None)
                            for k in range(4)]).then_inc(ph.done, 1)
                        last_read[b] = (m_ready, 2 * u + c + 1)
            gemm(PH["c_out"], DC, 256, MH, ML, ready=lambda k: (m_lo, k + 1))
            norm("post1")
            norm("pre2")
            ffn(2, "pre2")
            norm("post2")


def kernel(**inputs):
    import numpy as _np
    import concourse.bacc as _bacc
    from concourse.bass_utils import run_bass_kernel_spmd as _run

    x = {k: _np.asarray(a) for k, a in inputs.items()}
    weights, params, x_t, mem_t, ctx_t = lay_out(x)
    const, axial, rows = constants()
    nc = _bacc.Bacc("TRN2", target_bir_lowering=False, num_devices=1)
    arrays = {}

    def given(name, a):
        a = _np.ascontiguousarray(a)
        arrays[name] = a
        return nc.dram_tensor(name, a.shape, mybir.dt.from_np(a.dtype), kind="ExternalInput").ap()

    wd = {k: given(f"w_{k}", a) for k, a in weights.items()}
    others = [given(n, a) for n, a in (("params", params), ("constants", const), ("axial", axial), ("dft", rows),
                                       ("x_t", x_t), ("mem_t", mem_t), ("ctx_t", ctx_t), ("positions", x["positions"]))]
    out = nc.dram_tensor("out_t", (P, DC, S), F32, kind="ExternalOutput").ap()
    program(nc, wd, *others, out)
    r = _run(nc, [arrays], core_ids=[0])
    got = r.results[0]["out_t"]
    return _np.ascontiguousarray(got.transpose(2, 1, 0).reshape(1, S, D))
```

```python
import math
from contextlib import ExitStack

import numpy as np

import concourse.bass as bass
from concourse import mybir

F32 = mybir.dt.float32
F32R = mybir.dt.float32r
I32 = mybir.dt.int32
ALU = mybir.AluOpType
ACT = mybir.ActivationFunctionType
AX = mybir.AxisListType

P = 128
S = 512
ROWT = S // P
D = 1024
DC = D // P
MEM = 256
FF = 2816
FC = FF // P
HALF = FC // 2
KB = 1024
EPS = 1e-6
NEG = -1e30
PICKED = -3e38
TOPK = 128
A_HEADS = 8
IDX_HEADS = 16
KV_RANK = 256

PARAMS = [("g_mix", 16), ("g_ffn", 16), ("g_mem", 8), ("g_final", 8), ("g_pre1", 8), ("g_post1", 8),
          ("g_pre2", 8), ("g_post2", 8), ("kv_norm", 2), ("conv0", 4 * FC), ("conv1", 4 * FC),
          ("conv2", 4 * FC), ("b_mod", 48), ("cvec", 16), ("sink_b", 16), ("sink_c", 8)]
PCOL, _n = {}, 0
for _name, _w in PARAMS:
    PCOL[_name] = _n
    _n += _w
NPARAM = _n

CONSTS = [("ge", P), ("z0", P), ("le", P), ("z1", P), ("z2", P), ("z3", P), ("ge2", P), ("gt", P), ("le2", P),
          ("ident", P), ("dft_c", 2 * P), ("inv32", 1), ("inv16", 1), ("sgn32", 1), ("sgn16", 1), ("eps", 1)]
CCOL, _n = {}, 0
for _name, _w in CONSTS:
    CCOL[_name] = _n
    _n += _w
NCONST = _n


def constants():
    q, k = np.arange(P)[:, None], np.arange(P)[None, :]
    c = np.zeros((P, NCONST), np.float32)

    def put(name, a):
        c[:, CCOL[name]:CCOL[name] + a.shape[1]] = a

    ge, le, gt = (np.where(ok, 0.0, NEG).astype(np.float32) for ok in (k >= q, k <= q, k > q))
    for name, a in (("ge", ge), ("ge2", ge), ("le", le), ("le2", le), ("gt", gt)):
        put(name, a)
    put("ident", np.eye(P, dtype=np.float32))
    ang = 2 * np.pi * ((q * k) % P) / P
    put("dft_c", np.concatenate([np.cos(ang), np.sin(ang)], 1).astype(np.float32))
    p = np.arange(P)
    for name, head, rot in (("32", 128, 32), ("16", 64, 16)):
        d, half = p % head, rot // 2
        inv = np.float32(500000.0) ** (-(2.0 * (d % half)).astype(np.float32) / np.float32(rot))
        put("inv" + name, np.where(d < rot, inv, 0.0).astype(np.float32)[:, None])
        put("sgn" + name, np.where(d < half, -1.0, 1.0).astype(np.float32)[:, None])
    put("eps", np.full((P, 1), EPS, np.float32))
    s = np.arange(S)
    d = p % 64
    inv = np.float32(10000.0) ** (-(2.0 * (d % 16)).astype(np.float32) / np.float32(32))
    at = np.where((d < 32)[:, None], (s // 64)[None, :], (s % 64)[None, :]).astype(np.float32)
    ang = at * inv[:, None]
    sgn = np.where(d % 32 < 16, -1.0, 1.0)[:, None]
    axial = np.stack([np.cos(ang), np.sin(ang) * sgn], 1).astype(np.float32)
    i = np.arange(S)
    ang = 2 * np.pi * ((i[:, None] * i[None, :]) % S) / S
    rows = np.concatenate([np.cos(ang), -np.sin(ang)], 1) / math.sqrt(S * P)
    rows = rows.astype(np.float32).reshape(ROWT, P, 2 * S).transpose(1, 0, 2)
    return c, axial, np.ascontiguousarray(rows)


STREAM = [("memkv", 4, 2048, [2, 2, 2, 2]),
          ("a_in", 11, 2048, [2, 3, 2, 2, 2, 2, 2, 2, 2, 2, 2]),
          ("uk", 1, 2048, 8), ("uv", 1, 2048, 8), ("mod", 24, 2048, 1),
          ("a_out", 8, 1280, 1),
          ("up00", HALF, 2048, 2), ("dn00", 8, HALF * P, 1), ("up01", HALF, 2048, 2), ("dn01", 8, HALF * P, 1),
          ("b_in", 7, 2048, [2, 4, 2, 2, 2, 2, 2]), ("b_out", 8, 1280, 1),
          ("up10", HALF, 2048, 2), ("dn10", 8, HALF * P, 1), ("up11", HALF, 2048, 2), ("dn11", 8, HALF * P, 1),
          ("ctx", 1, 2048, 3),
          ("c_in", 13, 2048, [2, 2, 5] + [2] * 10),
          ("merge", 4, 2048, 4), ("c_out", 4, 2048, 2),
          ("up20", HALF, 2048, 2), ("dn20", 8, HALF * P, 1), ("up21", HALF, 2048, 2), ("dn21", 8, HALF * P, 1)]


def units(w, width):
    k, n = w.shape
    return w.reshape(k // P, P, n // width, width).transpose(2, 1, 0, 3).reshape(n // width, P, -1)


def lay_out(x):
    w = {}
    kv = x["w_mem_kv"]
    w["memkv"] = np.concatenate([units(kv[0], 256), units(kv[1], 256)])
    a = x["a_w_in"][0]
    q, ckv, kr, qi, ki, wi, qm = np.split(a, np.cumsum([1024, 256, 32, 1024, 64, 16]).tolist(), axis=1)
    misc = np.concatenate([kr, wi, np.zeros((D, 80), np.float32), ki, ki], 1)
    w["a_in"] = units(np.concatenate([ckv, misc, qi, q, qm], 1), 256)
    w["mod"] = units(x["w_mod_2"][0], 256)
    uk = x["a_w_uk"][0]
    w["uk"] = units(np.concatenate([np.zeros((KV_RANK, 8, 32), np.float32), uk], 2).reshape(KV_RANK, 1024), 1024)
    w["uv"] = units(x["a_w_uv"][0].reshape(KV_RANK, 1024), 1024)
    w["a_out"] = units(x["a_w_out"][0], P)
    pair8 = [h for c in range(4) for h in (c, c + 4)]
    pair16 = pair8 + [h + 8 for h in pair8]
    b = x["b_w_in"][0]
    bq = b[:, :1024].reshape(D, 16, 64)[:, pair16].reshape(D, 1024)
    w["b_in"] = units(np.concatenate([b[:, 1024:1536], bq, b[:, 1536:]], 1), 256)
    bo = x["b_w_out"][0]
    w["b_out"] = units(np.concatenate([bo[:1024].reshape(16, 64, D)[pair16].reshape(1024, D), bo[1024:]]), P)
    ups = [x["f_w_up"][0], x["f_w_up"][1], x["w_up_2"][0]]
    downs = [x["f_w_down"][0], x["f_w_down"][1], x["w_down_2"][0]]
    for l in range(3):
        up = ups[l].reshape(DC, P, 2, FC, P).transpose(3, 1, 0, 2, 4).reshape(FC, P, 2048)
        down = downs[l].reshape(2, HALF, P, DC, P).transpose(0, 3, 2, 1, 4).reshape(2, DC, P, HALF * P)
        for h in range(2):
            w[f"up{l}{h}"] = up[h * HALF:(h + 1) * HALF]
            w[f"dn{l}{h}"] = down[h]
    c = x["w_in_2"][0]
    w["ctx"] = units(c[:, 512:768], 256)
    cq = c[:, :512].reshape(D, 8, 64)[:, pair8].reshape(D, 512)
    w["c_in"] = units(np.concatenate([cq, c[:, 512:]], 1), 256)
    pa = x["w_pa_2"][0].reshape(8, 64, D)[pair8].reshape(512, D)
    w["merge"] = np.concatenate([units(pa, 256), units(x["w_pf_2"][0], 256)], 2)
    w["c_out"] = units(x["w_out_2"][0], 256)
    w["up"] = None
    del w["up"]

    def cols(v):
        return v.reshape(-1, P).T

    def conv(cw, cb):
        return np.stack([cols(cw[0]), cols(cw[1]), cols(cw[2]), cols(cb)], 2).reshape(P, 4 * FC)

    sink_b = np.broadcast_to(x["b_sinks"][0][pair16], (P, 16))
    sink_c = np.broadcast_to(x["sink_2"][0][pair8], (P, 8))
    cvec = np.stack([cols(x["c_2"]), cols(x["c_ctx_2"])], 2).reshape(P, 16)
    params = np.concatenate([
        cols(x["g_mix"]), cols(x["g_ffn"]), cols(x["g_mem"]), cols(x["g_final"]), cols(x["g_pre1_2"]),
        cols(x["g_post1_2"]), cols(x["g_pre2_2"]), cols(x["g_post2_2"]), cols(x["a_kv_norm"]),
        conv(x["f_conv_w"][0], x["f_conv_b"][0]), conv(x["f_conv_w"][1], x["f_conv_b"][1]),
        conv(x["conv_w_2"][0], x["conv_b_2"][0]), cols(x["b_mod_2"]), cvec, sink_b, sink_c], 1)

    def turned(t):
        n = t.shape[1]
        return t[0].reshape(n, DC, P).transpose(2, 1, 0)

    return w, params, turned(x["x"]), turned(x["mem"]), turned(x["ctx_2"])


class Phase:

    def __init__(self, name, n, size, tiles, land, split):
        self.name, self.n, self.size, self.tiles = name, n, size, tiles
        self.land = land
        self.split = split
        self.done = None
        self.free = None

    def before(self, u):
        return sum(self.tiles[:u]) if isinstance(self.tiles, list) else u * self.tiles

    @property
    def total(self):
        return self.before(self.n)


class Chain:

    def __init__(self, eng, sem):
        self.eng, self.sem, self.n, self.off = eng, sem, 0, 0

    def step(self, ins):
        ins.then_inc(self.sem, 1)
        self.n += 1
        self.eng.wait_ge(self.sem, self.off + self.n)


def each_unit(eng, n, body, chain=None):
    if n < 8:
        for u in range(n):
            body(u // 2, u % 2)
        return
    at = chain.n if chain else 0
    body(0, 0)
    body(0, 1)
    per = chain.n - at if chain else 0
    last = (n - 1) // 2
    with eng.Fori(1, last) as i:
        if chain:
            chain.off = i * per - per
        body(i, 0)
        body(i, 1)
    if chain:
        chain.off = 0
        chain.n = at + per * last
    for u in range(2 * last, n):
        body(u // 2, u % 2)


def program(nc, wdram, params_d, const_d, axial_d, rows_d, x_d, mem_d, ctx_d, pos_d, out_d):
    ctx = ExitStack()
    with ctx:
        def sem(name):
            return ctx.enter_context(nc.semaphore(name))

        base = (nc.sbuf_base + 63) // 64 * 64

        def at(name, kb, shape, dt=F32):
            return nc.alloc_sbuf_tensor_at(name, [P] + shape, dt, offset=base + int(kb * KB))

        XT = at("xT", 0, [DC, S])
        HH, HL = at("h_hi", 16, [10, S], F32R), at("h_lo", 36, [10, S], F32R)
        RAW = [at(f"raw{i}", 56 + 8 * i, [2048]) for i in range(2)]
        HI = [at(f"w_hi{i}", 72 + 8 * i, [2048], F32R) for i in range(2)]
        LO = [at(f"w_lo{i}", 88 + 8 * i, [2048], F32R) for i in range(2)]
        R = 104
        MEMT = at("memT", R, [DC, MEM])
        MEMH, MEML = at("mem_hi", R + 16, [DC, MEM], F32R), at("mem_lo", R + 24, [DC, MEM], F32R)
        AQ = at("a_q", R, [8, S])
        AQI, AK = at("a_q_idx", R + 16, [8, S]), at("a_k", R + 16, [8, S])
        CKV, KIDX, KROPE = at("c_kv", R + 32, [2, S]), at("k_idx", R + 36, [S]), at("k_rope", R + 38, [S])
        AV = at("a_v", R + 32, [ROWT, 1024])
        PICK = at("picked", R + 48, [3, S])
        CH, CL = at("c_hi", R + 56, [2, S], F32R), at("c_lo", R + 60, [2, S], F32R)
        WIDX = at("w_idx", R + 54, [ROWT, IDX_HEADS])
        QM = at("q_mem", R + 184 - 104 + 10, [2, S])
        GH, GL = at("g_hi", R, [HALF, S], F32R), at("g_lo", R + 22, [HALF, S], F32R)
        BQ, BK, BV = at("b_q", R, [8, S]), at("b_k", R + 16, [2, S]), at("b_v", R + 20, [ROWT, 256])
        BO = at("b_o_hi", R + 24, [8, S], F32R), at("b_o_lo", R + 40, [8, S], F32R)
        BSW = at("b_swapped", R + 56, [2, S])
        CTXT = at("ctxT", R + 48, [DC, MEM])
        GA, GF = at("gate_a", R, [8, S]), at("gate_f", R + 16, [8, S])
        CQ, FT = at("c_q", R + 32, [4, S]), at("f_t", R + 40, [4, S])
        CO = at("c_o_hi", R + 48, [4, S], F32R), at("c_o_lo", R + 56, [4, S], F32R)
        MH, ML = at("m_hi", R + 32, [8, S], F32R), at("m_lo", R + 64, [8, S], F32R)
        F1 = [at(f"f_rows{i}", 16 + 4 * i, [ROWT, 256]) for i in range(2)]
        Y = at("y", R, [DC, S])
        Y2 = at("y2", R + 44, [DC, S])
        C32, S32, C16, S16 = (at(n, R + 64 + 2 * i, [S]) for i, n in enumerate(("cos32", "sin32", "cos16", "sin16")))
        MK = [at(f"mem_k{l}", R + 72 + 4 * l, [2, MEM]) for l in range(2)]
        MV = [at(f"mem_v{l}", R + 74 + 4 * l, [2, 256]) for l in range(2)]
        DFT = at("dft_rows", R + 64, [ROWT, 1024])
        T = at("work", R + 80, [7, S])
        TW = at("work_flat", R + 80, [7 * S])
        small = [R + 94.0]

        def after(name, shape):
            t = at(name, small[0], shape)
            small[0] += -(-4 * math.prod(shape) // 32) * 32 / KB
            return t

        CST, PRM, ONES = after("const", [NCONST]), after("params", [NPARAM]), after("ones", [P])
        MODV, DER, SV = after("mod", [48, 2]), after("derived", [5, 8]), after("silu_c", [16])
        ST, M8 = after("stats", [2, 12]), after("top8", [8])
        CKX, CVX = at("ctx_k", 32, [MEM]), at("ctx_v", 33, [2, P])
        CK, CV = at("c_k", 34, [S]), at("c_v", 52, [ROWT, P])
        assert base + small[0] * KB <= nc.sbuf_usable_end
        AXC, AXS = C16, S16
        POS = at("positions", R + 70, [S], I32)

        ps = ctx.enter_context(nc.psum_tensor("psum", [P, 8 * S], F32))

        def bank(b, a=0, z=S):
            return ps[:, b * S + a:b * S + z]

        def par(name, k, n=1):
            return PRM[:, PCOL[name] + k:PCOL[name] + k + n]

        def cst(name, n=1, off=0):
            return CST[:, CCOL[name] + off:CCOL[name] + off + n]

        PH, land, split = {}, 0, 0
        for name, n, size, tiles in STREAM:
            ph = PH[name] = Phase(name, n, size, tiles, land, split)
            ph.done, ph.free = sem(f"{name}_done"), sem(f"{name}_read")
            land += n
            if name != "mod":
                split += n
        order = [PH[s[0]] for s in STREAM]
        split_order = [p for p in order if p.name != "mod"]

        raw_landed = [sem("raw_landed0"), sem("raw_landed1")]
        hi_ready, lo_ready = sem("w_hi_ready"), sem("w_lo_ready")

        NORMS = {}
        nb = sc = 0
        for i, (name, nch, rows, splits) in enumerate([
                ("mem", 8, MEM, True), ("mix0", 8, S, True), ("ckv", 2, S, True), ("ffn0", 8, S, True),
                ("mix1", 8, S, True), ("ffn1", 8, S, True), ("final", 8, S, False), ("ctx", 8, MEM, True),
                ("pre1", 8, S, True), ("post1", 8, S, False), ("pre2", 8, S, True), ("post2", 8, S, False)]):
            NORMS[name] = (i, nch, rows, nb, sc)
            nb += nch
            sc += nch if splits else 0
        square_ready, square_used, root_ready = sem("square_ready"), sem("square_used"), sem("root_ready")
        scaled_ready, h_hi_ready, h_ready = sem("scaled_ready"), sem("h_hi_ready"), sem("h_ready")
        x_ready = sem("x_ready")
        XR = {"final": 0, "post1": 8, "post2": 16}

        steps, flushes = [], []

        def add_steps(group, last_of, targets):
            for n, s in enumerate(group):
                s["flush"] = len(flushes) + n // last_of
                s["first"] = n % last_of == 0
                s["last"] = n % last_of == last_of - 1
            flushes.extend(targets)
            lo = len(steps)
            steps.extend(group)
            return lo, len(steps)

        def whole(c, out=(HH, HL)):
            return out[0][:, c, :], out[1][:, c, :]

        def heads_of_tile(t, h4):
            return tuple(buf[:, 4 * h4:4 * h4 + 4, t * P:(t + 1) * P] for buf in (HH, HL))

        def q_tile(buf, c, j, t):
            return buf[64 * j:64 * j + 64, c, t * P:(t + 1) * P]

        def mem_steps(l):
            return [dict(nh=2, nk=256, mask=None, scale=0.125, sink=None,
                         qk=[(j * S, q_tile(QM, c, j, t), MK[l][64 * j:64 * j + 64, c, :]) for j in range(2)],
                         pv=[[(MV[l][:, kb_, (2 * c + j) * 64:(2 * c + j + 1) * 64]) for kb_ in range(2)] for j in range(2)],
                         out=[(64 * j, 64, t) for j in range(2)])
                    for c in range(2) for t in range(ROWT)]

        a_range = add_steps(
            [dict(nh=1, nk=(t + 1) * P, mask=cst("le", P) if t == 0 else PICK[:, t - 1, 0:(t + 1) * P],
                  scale=128 ** -0.5, sink=None,
                  qk=[(0, AQ[:, h, t * P:(t + 1) * P], AK[:, h, 0:(t + 1) * P])],
                  pv=[[AV[:, kb_, h * P:(h + 1) * P] for kb_ in range(t + 1)]], out=[(0, P, h % 4)])
             for t in range(ROWT) for h in range(A_HEADS)], 4, [heads_of_tile(t, h4) for t in range(ROWT) for h4 in range(2)])
        am_range = add_steps(mem_steps(0), ROWT, [whole(8), whole(9)])
        b_range = add_steps(
            [dict(nh=2, nk=min(t + 1, 2) * P, mask=cst("le", P) if t == 0 else cst("gt", 2 * P), scale=0.125,
                  sink=par("sink_b", 2 * c, 2),
                  qk=[(j * S, q_tile(BQ, c, j, t),
                       BK[64 * j:64 * j + 64, c // 4, max(t - 1, 0) * P:(t + 1) * P]) for j in range(2)],
                  pv=[[BV[:, kb_, (2 * (c // 4) + j) * 64:(2 * (c // 4) + j + 1) * 64]
                       for kb_ in range(max(t - 1, 0), t + 1)] for j in range(2)],
                  out=[(64 * j, 64, t) for j in range(2)])
             for c in range(8) for t in range(ROWT)], ROWT, [whole(c, BO) for c in range(8)])
        bm_range = add_steps(mem_steps(1), ROWT, [whole(8), whole(9)])

        def c_step(c, j, t):
            rows = slice(64 * j, 64 * j + 64)
            q = q_tile(CQ, c, j, t)
            k = [CK[rows, b * P:(b + 1) * P] for b in range(ROWT)]
            v = [CV[:, b, 64 * j:64 * j + 64] for b in range(ROWT)]
            kx = [CKX[rows, b * P:(b + 1) * P] for b in range(2)]
            vx = [CVX[:, b, 64 * j:64 * j + 64] for b in range(2)]
            if t == 0:
                mask, ks, vs = "z0", [k[0], k[1], *kx], [v[0], v[1], *vx]
            elif t == ROWT - 1:
                mask, ks, vs = "z1", [k[t], *kx, k[t - 1]], [v[t], *vx, v[t - 1]]
            else:
                mask, ks, vs = "ge", [*k[t - 1:t + 2], *kx], [*v[t - 1:t + 2], *vx]
            n = len(ks)
            return dict(nh=1, nk=n * P, mask=cst(mask, n * P), scale=0.125, sink=par("sink_c", 2 * c + j, 1),
                        qk=[(b * P, q, ks[b]) for b in range(n)], pv=[vs], out=[(64 * j, 64, t)])

        c_range = add_steps([c_step(c, j, t) for c in range(4) for j in range(2) for t in range(ROWT)],
                            2 * ROWT, [whole(c, CO) for c in range(4)])
        a_all, b_all = (a_range[0], am_range[1]), (b_range[0], bm_range[1])

        def scores_at(s, n):
            return (2 + 2 * (s % 2) + n) * S

        def wide(s):
            return 640 if s >= c_range[0] else S

        def probs_at(s):
            return (s % 3) * wide(s)

        def turned_at(s):
            return (3 + s % 2) * wide(s)

        def finished(rate, k):
            return rate * k // 24

        FILL_IDX, FILL_B, FILL_C = 5, 7, 15

        scores_done, max_ready, exp_done, p_ready = sem("scores_done"), sem("max_ready"), sem("exp_done"), sem("p_ready")
        turned_done, turned_ready, pv_done = sem("turned_done"), sem("turned_ready"), sem("pv_done")
        o_hi_ready, o_ready = sem("o_hi_ready"), sem("o_ready")

        def flushed(rng):
            return steps[rng[1] - 1]["flush"] + 1

        load_const, load_x, load_mem = sem("load_const"), sem("load_x"), sem("load_mem")
        load_ctx, load_tab = sem("load_ctx"), sem("load_tables")
        ones_ready, tables_ready = sem("ones_ready"), sem("tables_ready")
        angle_ready = sem("angle_ready")
        silu_c_ready, mod_ready = sem("silu_c_ready"), sem("mod_ready")
        idx_done, relu_ready, idx_summed = sem("idx_done"), sem("relu_ready"), sem("idx_summed")
        conv_ready, silu_ready, g_ready = sem("conv_ready"), sem("silu_ready"), sem("g_ready")
        qkv_ready = sem("qkv_ready")
        f1_done, f1_ready, f2_done, f2_hi, four_ready = (sem(n) for n in (
            "f1_done", "f1_ready", "f2_done", "f2_hi_ready", "four_ready"))
        gates_ready = sem("gates_ready")
        m_ready, m_hi, m_lo = sem("m_ready"), sem("m_hi_ready"), sem("m_lo_ready")
        vec_steps, act_steps = sem("vector_steps"), sem("scalar_steps")
        out_landed = sem("out_landed")

        block = ctx.enter_context(nc.Block())

        @block.sync
        def _(sp):
            def occupant_read(p):
                if p < 2:
                    return
                ph = max((q for q in order if q.land <= p - 2), key=lambda q: q.land)
                u = p - 2 - ph.land
                if ph.name == "mod":
                    sp.wait_ge(ph.done, u + 1)
                else:
                    sp.wait_ge(lo_ready, ph.split + u + 1)

            for ph in order:
                def load(i, j, ph=ph):
                    slot = (ph.land + j) % 2
                    if isinstance(i, int) and i == 0:
                        occupant_read(ph.land + j)
                    elif ph.name == "mod":
                        sp.wait_ge(ph.done, 2 * i + j - 1)
                    else:
                        sp.wait_ge(lo_ready, 2 * i + (j - 1 + ph.split))
                    u = 2 * i + j
                    src = wdram[ph.name][u] if isinstance(u, int) else \
                        wdram[ph.name][bass.ds(u, 1), :, :].rearrange("a p n -> p (a n)")
                    sp.dma_start(RAW[slot][:, 0:ph.size], src).then_inc(raw_landed[slot], 16)
                each_unit(sp, ph.n, load)
            for c in range(DC):
                sp.wait_ge(x_ready, XR["post2"] + c + 1)
                sp.dma_start(out_d[:, c, :], XT[:, c, :]).then_inc(out_landed, 16)
            sp.wait_ge(out_landed, 16 * DC)

        @block.gpsimd
        def _(pool):
            pool.memset(ONES[:], 1.0).then_inc(ones_ready, 1)
            for ph in split_order:
                def low(i, j, ph=ph):
                    slot = (ph.split + j) % 2
                    pool.wait_ge(hi_ready, 2 * i + (j + ph.split + 1))
                    nc.gpsimd.tensor_tensor(LO[slot][:, 0:ph.size], RAW[slot][:, 0:ph.size],
                                            HI[slot][:, 0:ph.size].bitcast(F32), ALU.subtract).then_inc(lo_ready, 1)
                each_unit(pool, ph.n, low)

        @block.scalar
        def _(act):
            chain = Chain(act, act_steps)

            def hi_unit(ph, i, j):
                slot = (ph.split + j) % 2
                act.wait_ge(raw_landed[slot], i * 16 + 16 * ((ph.land + j) // 2 + 1))
                if not isinstance(i, int) or i > 0:
                    act.wait_ge(ph.done, ph.before(2 * i + j - 1))
                elif ph.split + j >= 2:
                    g = ph.split + j - 2
                    q = max((q for q in split_order if q.split <= g), key=lambda q: q.split)
                    act.wait_ge(q.done, q.before(g - q.split + 1))
                nc.scalar.activation(HI[slot][:, 0:ph.size], RAW[slot][:, 0:ph.size], ACT.Copy).then_inc(hi_ready, 1)

            def next_hi(ph, i, j):
                if isinstance(i, int) and 2 * i + j == ph.n - 1:
                    k = split_order.index(ph) + 1
                    if ph.name != "a_in" and k < len(split_order):
                        hi_unit(split_order[k], 0, 0)
                elif j == 0:
                    hi_unit(ph, i, 1)
                else:
                    hi_unit(ph, i + 1, 0)

            def stream_only(ph):
                each_unit(act, ph.n, lambda i, j: next_hi(ph, i, j))

            def norm(name, src, ready, free=None, dst=(HH, HL), width=D, root_free=()):
                i, nch, rows, b, s = NORMS[name]
                for k in range(nch):
                    for w in ready(k):
                        act.wait_ge(*w)
                    if k >= 2:
                        act.wait_ge(square_used, b + k - 1)
                    nc.scalar.activation(T[:, k % 2, 0:rows], src(k), ACT.Square).then_inc(square_ready, 1)
                for w in root_free:
                    act.wait_ge(*w)
                act.wait_ge(square_used, b + nch)
                nc.scalar.activation(T[:, 2, 0:rows], bank(4, 0, rows), ACT.Sqrt, bias=cst("eps"),
                                     scale=1.0 / width).then_inc(root_ready, 1)
                if free is not None:
                    for w in free:
                        act.wait_ge(*w)
                    for k in range(nch):
                        act.wait_ge(scaled_ready, s + k + 1)
                        nc.scalar.activation(dst[0][:, k, 0:rows], T[:, 4 + k % 2, 0:rows], ACT.Copy).then_inc(h_hi_ready, 1)

            def hi_split(g):
                q = max((q for q in split_order if q.split <= g), key=lambda q: q.split)
                hi_unit(q, (g - q.split) // 2, (g - q.split) % 2)

            def attend(rng, between=None):
                lo, hi = rng

                def exps(s):
                    st, W = steps[s], steps[s]["nk"]
                    act.wait_ge(max_ready, s + 1)
                    if st["mask"] is None and s >= 3:
                        act.wait_ge(turned_done, s - 2)
                    for n in range(st["nh"]):
                        sm = TW[:, probs_at(s) + n * W:probs_at(s) + (n + 1) * W]
                        src = sm if st["mask"] is not None else ps[:, scores_at(s, n):scores_at(s, n) + W]
                        last = nc.scalar.activation(sm, src, ACT.Exp, bias=ST[:, s % 2, 2 + n:3 + n], scale=st["scale"],
                                                    accum_out=ST[:, s % 2, 4 + n:5 + n])
                        if st["sink"] is not None:
                            last = nc.scalar.activation(ST[:, s % 2, 6 + n:7 + n], st["sink"][:, n:n + 1], ACT.Exp,
                                                        bias=ST[:, s % 2, 2 + n:3 + n])
                    last.then_inc(exp_done, 1)

                def turned(s):
                    W = steps[s]["nk"] * steps[s]["nh"]
                    act.wait_ge(turned_done, s + 1)
                    if s >= 2:
                        act.wait_ge(pv_done, s - 1)
                    d = turned_at(s)
                    ins = nc.scalar.activation(TW[:, d:d + min(W, S)], bank(6, 0, min(W, S)), ACT.Copy)
                    if W > S:
                        a0 = scores_at(s, 1) + S - P
                        ins = nc.scalar.activation(TW[:, d + S:d + W], ps[:, a0:a0 + P], ACT.Copy)
                    ins.then_inc(turned_ready, 1)

                def flush(s):
                    f = steps[s]["flush"]
                    act.wait_ge(pv_done, s + 1)
                    out = flushes[f][0]
                    src = bank(7) if len(out.shape) == 2 else bank(7).rearrange("p (h n) -> p h n", h=4)
                    nc.scalar.activation(out, src, ACT.Copy).then_inc(o_hi_ready, 1)

                for s in range(lo, hi):
                    exps(s)
                    if s > lo:
                        turned(s - 1)
                    if s >= lo + 2 and steps[s - 2]["last"]:
                        flush(s - 2)
                    if between:
                        between(s - lo)
                turned(hi - 1)
                for s in range(hi - 2, hi):
                    if steps[s]["last"]:
                        flush(s)

            def ffn_up(ph, first):
                def body(i, j):
                    next_hi(ph, i, j)
                    act.wait_ge(conv_ready, 2 * i + (j + 1 + first))
                    nc.scalar.activation(T[:, 2 + j, :], T[:, j, :], ACT.Silu).then_inc(silu_ready, 1)
                each_unit(act, ph.n, body)

            act.dma_start(MEMT[:], mem_d).then_inc(load_mem, 16)
            act.dma_start(CST[:], const_d).then_inc(load_const, 16)
            act.dma_start(PRM[:], params_d).then_inc(load_const, 16)
            act.dma_start(XT[:], x_d).then_inc(load_x, 16)
            act.dma_start(POS[:], pos_d.partition_broadcast(P)).then_inc(load_const, 16)

            norm("mem", lambda k: MEMT[:, k, :], lambda k: [(load_mem, 16), (load_const, 48)], free=[], dst=(MEMH, MEML))
            ph = PH["memkv"]
            hi_unit(ph, 0, 0)
            norm("mix0", lambda k: XT[:, k, :], lambda k: [(load_x, 16)], free=[])
            for u in range(4):
                next_hi(ph, u // 2, u % 2)
                l, v = u // 2, u % 2
                for c in range(2):
                    act.wait_ge(ph.done, 2 * u + c + 1)
                    b = (u % 2) * 2 + c
                    dst = MV[l][:, c, :] if v else MK[l][:, c, :]
                    nc.scalar.activation(dst, bank(b, 0, 256), ACT.Copy).then_inc(ph.free, 1)
            for n, dst in enumerate((C32, S32, C16, S16)):
                act.wait_ge(angle_ready, n + 1)
                nc.scalar.activation(dst[:], T[:, 3 + n, :], ACT.Sin).then_inc(tables_ready, 1)

            ph = PH["a_in"]
            for u in range(6):
                next_hi(ph, u // 2, u % 2)
                if u == 0:
                    for c in range(2):
                        act.wait_ge(ph.done, c + 1)
                        nc.scalar.activation(CKV[:, c, :], bank(c), ACT.Copy).then_inc(ph.free, 1)
                if u == 1:
                    act.wait_ge(ph.done, ph.before(1) + 3)
                    nc.scalar.activation(WIDX[:], bank(5, 0, 64).rearrange("p (t h) -> p t h", h=16), ACT.Copy,
                                         scale=1.0 / 32).then_inc(qkv_ready, 1)
                if u == 2:
                    norm("ckv", lambda k: CKV[:, k, :], lambda k: [(ph.free, 2), (tables_ready, 6)], free=[], dst=(CH, CL),
                         width=KV_RANK, root_free=[(ph.free, 8)])

            hi_split(ph.split + 7)
            n = 0
            for t in range(1, ROWT):
                W = (t + 1) * P
                for h in range(IDX_HEADS):
                    act.wait_ge(idx_done, n + 1)
                    if n >= 2:
                        act.wait_ge(idx_summed, n - 1)
                    nc.scalar.activation(T[:, n % 2, 0:W], bank(4 + n % 3, 0, W), ACT.Relu).then_inc(relu_ready, 1)
                    for tile in range(finished(FILL_IDX, n - 1) if n else 0, finished(FILL_IDX, n)):
                        if tile % 2:
                            hi_split(ph.split + 8 + tile // 2)
                    n += 1
            for c in range(2):
                act.wait_ge(ph.done, ph.before(10) + c + 1)
                nc.scalar.activation(QM[:, c, :], bank(c), ACT.Copy).then_inc(qkv_ready, 1)
            hi_split(ph.split + 12)
            nc.scalar.activation(SV[:], par("cvec", 0, 16), ACT.Silu).then_inc(silu_c_ready, 1)

            uk, uv = PH["uk"], PH["uv"]
            for h in range(8):
                act.wait_ge(uk.done, h + 1)
                nc.scalar.activation(AK[:, h, :], bank(h % 4), ACT.Copy).then_inc(uk.free, 1)
                act.wait_ge(uk.free, h + 1)
                nc.scalar.activation(AK[0:32, h, :], KROPE[0:32, :], ACT.Copy).then_inc(qkv_ready, 1)
            act.wait_ge(qkv_ready, 11)
            for n in range(8):
                act.wait_ge(uv.done, n + 1)
                nc.scalar.activation(AV[:, n // 2, (n % 2) * S:(n % 2 + 1) * S], bank(n % 4), ACT.Copy).then_inc(uv.free, 1)
            attend(a_all, lambda k: hi_unit(PH["a_out"], 0, 0) if k == 30 else None)
            stream_only(PH["a_out"])

            def ffn(l, first):
                for h in range(2):
                    ffn_up(PH[f"up{l}{h}"], first + h * HALF)
                    stream_only(PH[f"dn{l}{h}"])

            norm("ffn0", lambda k: XT[:, k, :], lambda k: [(PH["a_out"].free, k + 1)], free=[(PH["a_out"].done, 8)])
            ffn(0, 0)
            norm("mix1", lambda k: XT[:, k, :], lambda k: [(PH["dn01"].free, k + 1)], free=[(PH["up01"].done, 22)])

            ph = PH["b_in"]
            for u in range(3):
                next_hi(ph, u // 2, u % 2)
                if u == 1:
                    for t in range(ROWT):
                        act.wait_ge(ph.done, ph.before(1) + t + 1)
                        nc.scalar.activation(BV[:, t, :], bank(4 + t, 0, 256), ACT.Copy).then_inc(qkv_ready, 1)
            hi_split(ph.split + 4)

            def b_between(k):
                for tile in range(min(finished(FILL_B, k - 1) if k else 0, 8), min(finished(FILL_B, k), 8)):
                    if tile >= 6:
                        act.wait_ge(ph.done, ph.before(6) + tile - 5)
                        nc.scalar.activation(QM[:, tile - 6, :], bank(tile - 6), ACT.Copy).then_inc(qkv_ready, 1)
                    if tile % 2 and tile < 6:
                        hi_split(ph.split + 5 + tile // 2)
            attend(b_all, b_between)
            stream_only(PH["b_out"])
            norm("ffn1", lambda k: XT[:, k, :], lambda k: [(PH["b_out"].free, k + 1)], free=[(PH["b_out"].done, 8)])
            ffn(1, 22)

            act.wait_ge(o_ready, flushed(bm_range))
            act.dma_start(AXC[:], axial_d[:, 0, :]).then_inc(load_tab, 16)
            act.dma_start(AXS[:], axial_d[:, 1, :]).then_inc(load_tab, 16)
            act.wait_ge(PH["dn11"].done, 8)
            act.dma_start(CTXT[:], ctx_d).then_inc(load_ctx, 16)
            norm("final", lambda k: XT[:, k, :], lambda k: [(PH["dn11"].free, k + 1)])
            norm("ctx", lambda k: CTXT[:, k, :], lambda k: [(load_ctx, 16), (x_ready, 8)], free=[])
            ph = PH["ctx"]
            next_hi(ph, 0, 0)
            act.wait_ge(ph.done, 1)
            nc.scalar.activation(CKX[:], bank(0, 0, MEM), ACT.Copy).then_inc(ph.free, 1)
            for t in range(2):
                act.wait_ge(ph.done, t + 2)
                nc.scalar.activation(CVX[:, t, :], bank(1 + t, 0, P), ACT.Copy).then_inc(ph.free, 1)
            norm("pre1", lambda k: XT[:, k, :], lambda k: [(x_ready, XR["final"] + k + 1)], free=[(ph.done, 3)])

            ph = PH["c_in"]
            for u in range(3):
                next_hi(ph, u // 2, u % 2)
                if u == 2:
                    for t in range(ROWT):
                        act.wait_ge(ph.done, ph.before(2) + t + 2)
                        nc.scalar.activation(CV[:, t, :], bank(4 + t, 0, P), ACT.Copy).then_inc(qkv_ready, 1)
            hi_split(ph.split + 4)
            act.wait_ge(ph.free, 5)

            def c_between(k):
                for tile in range(finished(FILL_C, k - 1) if k else 0, finished(FILL_C, k)):
                    act.wait_ge(ph.done, ph.before(3) + tile + 1)
                    if tile < 4:
                        dst = FT[:, tile, :]
                    else:
                        dst = (GA if tile < 12 else GF)[:, (tile - 4) % 8, :]
                    nc.scalar.activation(dst, bank(tile % 2), ACT.Copy).then_inc(ph.free, 1)
                    if tile % 2 and tile // 2 < 9:
                        hi_split(ph.split + 5 + tile // 2)
            attend(c_range, c_between)
            c_between(32)
            act.wait_ge(turned_done, c_range[1])
            act.dma_start(DFT[:], rows_d).then_inc(load_tab, 16)
            act.wait_ge(ph.free, ph.total - 4)
            for n, gate in enumerate((GA, GF)):
                nc.scalar.activation(gate[:], gate[:], ACT.Sigmoid).then_inc(gates_ready, 1)
            for g in range(4):
                for t2 in range(2):
                    act.wait_ge(f1_done, 2 * g + t2 + 1)
                    if g >= 2:
                        act.wait_ge(f2_done, g - 1)
                    nc.scalar.activation(F1[g % 2][:, 2 * t2:2 * t2 + 2, :],
                                         bank(t2).rearrange("p (t n) -> p t n", t=2), ACT.Copy).then_inc(f1_ready, 1)
                act.wait_ge(f2_done, g + 1)
                nc.scalar.activation(HH[:, 4 + g, :], bank(2 + g % 2), ACT.Copy).then_inc(f2_hi, 1)

            ph = PH["merge"]
            for u in range(4):
                next_hi(ph, u // 2, u % 2)
                for c in range(2):
                    m = 2 * u + c
                    act.wait_ge(m_ready, m + 1)
                    nc.scalar.activation(MH[:, m, :], T[:, 4 + m % 2, :], ACT.Copy).then_inc(m_hi, 1)
            stream_only(PH["c_out"])
            norm("post1", lambda k: Y[:, k, :], lambda k: [(PH["c_out"].free, k + 1)])
            norm("pre2", lambda k: XT[:, k, :], lambda k: [(x_ready, XR["post1"] + k + 1)], free=[(PH["c_out"].done, 8)])
            ffn(2, 44)
            norm("post2", lambda k: Y2[:, k, :], lambda k: [(PH["dn21"].free, k + 1)])

        @block.vector
        def _(v):
            chain = Chain(v, vec_steps)
            step = chain.step

            def norm(name, src, gain, shift=None, dst=(HH, HL), into=None):
                i, nch, rows, b, s = NORMS[name]
                v.wait_ge(root_ready, i + 1)
                step(nc.vector.reciprocal(T[:, 3, 0:rows], T[:, 2, 0:rows]))

                def low(k):
                    v.wait_ge(h_hi_ready, s + k + 1)
                    nc.vector.tensor_tensor(dst[1][:, k, 0:rows], T[:, 4 + k % 2, 0:rows],
                                            dst[0][:, k, 0:rows].bitcast(F32), ALU.subtract).then_inc(h_ready, 1)

                for k in range(nch):
                    if into is not None:
                        out = src(k) if into == "self" else T[:, 4 + k % 2, 0:rows]
                        ins = nc.vector.scalar_tensor_tensor(out=out, in0=src(k), scalar=gain(k), in1=T[:, 3, 0:rows],
                                                             op0=ALU.mult, op1=ALU.mult)
                        if into == "self":
                            ins.then_inc(x_ready, 1)
                        else:
                            step(ins)
                            nc.vector.tensor_tensor(XT[:, k, :], XT[:, k, :], out, ALU.add).then_inc(x_ready, 1)
                        continue
                    t = T[:, 4 + k % 2, 0:rows]
                    if k >= 2:
                        v.wait_ge(h_ready, s + k - 1)
                    ins = nc.vector.scalar_tensor_tensor(out=t, in0=src(k), scalar=gain(k), in1=T[:, 3, 0:rows],
                                                         op0=ALU.mult, op1=ALU.mult)
                    if shift is not None:
                        step(ins)
                        ins = nc.vector.tensor_scalar(t, t, shift(k), None, ALU.add)
                    ins.then_inc(scaled_ready, 1)
                    if k >= 1:
                        low(k - 1)
                if into is None:
                    low(nch - 1)

            ropes = []

            def rope(src, dst, cos, sin, half, done, count, n=P, swapped=None):
                sw = T[0:n, 2 + len(ropes) % 2, :] if swapped is None else swapped[0:n, len(ropes) % 2, :]
                if len(ropes) >= 2:
                    v.wait_ge(*ropes[-2])
                ropes.append((done, count))
                mask = [i + half if i < half else i - half if i < 2 * half else i for i in range(32)]
                if half == 16:
                    mask = [(i + 16) % 32 for i in range(32)]
                step(nc.vector.stream_shuffle(sw, src, mask))
                step(nc.vector.tensor_tensor(sw, sw, sin[0:n, :], ALU.mult))
                step(nc.vector.tensor_tensor(dst, src, cos[0:n, :], ALU.mult))
                nc.vector.tensor_tensor(dst, dst, sw, ALU.add).then_inc(done, 1)

            def attend(rng, between=None):
                lo, hi = rng

                def maxes(s):
                    st, W = steps[s], steps[s]["nk"]
                    v.wait_ge(scores_done, s + 1)
                    if s >= 2:
                        v.wait_ge(p_ready, s - 1)
                    if s >= 3:
                        v.wait_ge(turned_done, s - 2)
                    o = ST[:, s % 2, :]
                    for n in range(st["nh"]):
                        src = ps[:, scores_at(s, n):scores_at(s, n) + W]
                        if st["mask"] is None:
                            ins = nc.vector.tensor_reduce(o[:, n:n + 1], src, AX.X, ALU.max)
                        else:
                            ins = nc.vector.tensor_tensor_reduce(
                                TW[:, probs_at(s) + n * W:probs_at(s) + (n + 1) * W], src, st["mask"], 1.0, PICKED,
                                ALU.add, ALU.max, o[:, n:n + 1])
                    step(ins)
                    nh = st["nh"]
                    if st["sink"] is None:
                        nc.vector.tensor_scalar(o[:, 2:2 + nh], o[:, 0:nh], -st["scale"], None, ALU.mult).then_inc(max_ready, 1)
                    else:
                        step(nc.vector.scalar_tensor_tensor(out=o[:, 8:8 + nh], in0=o[:, 0:nh], scalar=st["scale"],
                                                            in1=st["sink"], op0=ALU.mult, op1=ALU.max))
                        nc.vector.tensor_scalar(o[:, 2:2 + nh], o[:, 8:8 + nh], -1.0, None, ALU.mult).then_inc(max_ready, 1)

                def probs(s):
                    st, W = steps[s], steps[s]["nk"]
                    nh, o = st["nh"], ST[:, s % 2, :]
                    v.wait_ge(exp_done, s + 1)
                    if st["sink"] is not None:
                        step(nc.vector.tensor_tensor(o[:, 4:4 + nh], o[:, 4:4 + nh], o[:, 6:6 + nh], ALU.add))
                    step(nc.vector.reciprocal(o[:, 10:10 + nh], o[:, 4:4 + nh]))
                    for n in range(nh):
                        sm = TW[:, probs_at(s) + n * W:probs_at(s) + (n + 1) * W]
                        ins = nc.vector.tensor_scalar(sm, sm, o[:, 10 + n:11 + n], None, ALU.mult)
                    ins.then_inc(p_ready, 1)

                def flush(s):
                    f = steps[s]["flush"]
                    v.wait_ge(o_hi_ready, f + 1)
                    hi_part, out = flushes[f]
                    src = bank(7) if len(out.shape) == 2 else bank(7).rearrange("p (h n) -> p h n", h=4)
                    nc.vector.tensor_tensor(out, src, hi_part.bitcast(F32), ALU.subtract).then_inc(o_ready, 1)

                maxes(lo)
                for s in range(lo, hi):
                    if s + 1 < hi:
                        maxes(s + 1)
                    probs(s)
                    if s - 2 >= lo and steps[s - 2]["last"]:
                        flush(s - 2)
                    if between:
                        between(s - lo)
                for s in range(hi - 2, hi):
                    if steps[s]["last"]:
                        flush(s)

            def residual(ph, dst, mode):
                def body(i, j):
                    v.wait_ge(ph.done, 2 * i + j + 1)
                    c = 2 * i + j
                    d = dst[:, c, :] if isinstance(c, int) else dst[:, bass.ds(c, 1), :].rearrange("p a n -> p (a n)")
                    if mode == "add":
                        nc.vector.tensor_tensor(d, bank(j), d, ALU.add).then_inc(ph.free, 1)
                    else:
                        nc.vector.tensor_scalar(d, bank(j), 1.0, None, ALU.mult).then_inc(ph.free, 1)
                each_unit(v, ph.n, body)

            def ffn_up(ph, l, h, first, before):
                taps = [(0, 2), (1, 1), (2, 0)] if l < 2 else [(0, 1), (1, 0), (2, -1)]
                col = PCOL[f"conv{l}"] + 4 * h * HALF
                for w in before:
                    v.wait_ge(*w)

                def body(i, j):
                    u = 2 * i + j

                    def w(tap):
                        if isinstance(u, int):
                            return PRM[:, col + 4 * u + tap:col + 4 * u + tap + 1]
                        return PRM[:, bass.ds(u * 4 + (col + tap), 1)]

                    def chunk(buf):
                        return buf[:, u, :] if isinstance(u, int) else buf[:, bass.ds(u, 1), :].rearrange("p a n -> p (a n)")

                    a, b, t = bank(2 * j), bank(2 * j + 1), T[:, j, :]
                    mid = next(k for k, sft in taps if sft == 0)
                    v.wait_ge(ph.done, 2 * u + 1)
                    step(nc.vector.tensor_scalar(t, a, w(mid), w(3), ALU.mult, ALU.add))
                    rest = [x for x in taps if x[1] != 0]
                    for k, sft in rest:
                        o, s_ = (slice(sft, S), slice(0, S - sft)) if sft > 0 else (slice(0, S + sft), slice(-sft, S))
                        ins = nc.vector.scalar_tensor_tensor(out=t[:, o], in0=a[:, s_], scalar=w(k), in1=t[:, o],
                                                             op0=ALU.mult, op1=ALU.add)
                        if k == rest[-1][0]:
                            ins.then_inc(conv_ready, 1)
                        else:
                            step(ins)
                    v.wait_ge(ph.done, 2 * u + 2)
                    v.wait_ge(silu_ready, 2 * i + (j + 1 + first))
                    g = T[:, 4 + j, :]
                    nc.vector.tensor_tensor(g, b, T[:, 2 + j, :], ALU.mult).then_inc(ph.free, 1)
                    v.wait_ge(ph.free, u + 1)
                    step(nc.vector.tensor_scalar(chunk(GH), g, 1.0, None, ALU.mult))
                    nc.vector.tensor_tensor(chunk(GL), g, chunk(GH).bitcast(F32), ALU.subtract).then_inc(g_ready, 1)
                each_unit(v, ph.n, body, chain)

            def ffn(l, dst, modes):
                for h in range(2):
                    before = [(PH[f"dn{l}0"].done, 8)] if h else []
                    ffn_up(PH[f"up{l}{h}"], l, h, (2 * l + h) * HALF, before)
                    residual(PH[f"dn{l}{h}"], dst, modes[h])

            norm("mem", lambda k: MEMT[:, k, :], lambda k: par("g_mem", k), dst=(MEMH, MEML))
            norm("mix0", lambda k: XT[:, k, :], lambda k: par("g_mix", k))

            TWO_PI = 2 * math.pi
            C1 = 6.28125
            C2 = float(np.float32(round((TWO_PI - C1) * 2 ** 20) / 2 ** 20))
            C3 = TWO_PI - C1 - C2
            MAGIC = 1.5 * 2 ** 23
            PI = 3.1415925
            v.wait_ge(h_ready, 16)
            step(nc.vector.tensor_copy(T[:, 0, :], POS[:]))
            for n, (name, quarter) in enumerate((("32", True), ("32", False), ("16", True), ("16", False))):
                ang, turns, red = T[:, 1, :], T[:, 2, :], T[:, 3 + n, :]
                step(nc.vector.tensor_scalar(ang, T[:, 0, :], cst("inv" + name), None, ALU.mult))
                step(nc.vector.tensor_scalar(turns, ang, 1 / TWO_PI, 0.25 if quarter else 0.0, ALU.mult, ALU.add))
                step(nc.vector.tensor_scalar(turns, turns, MAGIC, None, ALU.add))
                step(nc.vector.tensor_scalar(turns, turns, MAGIC, None, ALU.subtract))
                for k, c in enumerate((C1, C2, C3)):
                    step(nc.vector.scalar_tensor_tensor(out=red if k else red, in0=turns, scalar=-c, in1=red if k else ang,
                                                        op0=ALU.mult, op1=ALU.add))
                if quarter:
                    step(nc.vector.tensor_scalar(red, red, math.pi / 2, None, ALU.add))
                nc.vector.tensor_scalar(red, red, PI, -PI, ALU.min, ALU.max).then_inc(angle_ready, 1)
            v.wait_ge(tables_ready, 4)
            for k, (tab, name) in enumerate(((S32, "32"), (S16, "16"))):
                nc.vector.tensor_scalar(tab[:], tab[:], cst("sgn" + name), None, ALU.mult).then_inc(tables_ready, 1)
            v.wait_ge(tables_ready, 6)

            ph = PH["a_in"]
            v.wait_ge(ph.free, 2)
            v.wait_ge(ph.done, ph.before(1) + 1)
            rope(bank(2)[0:32, :], KROPE[0:32, :], C32, S32, 16, ph.free, 3, 32)
            v.wait_ge(ph.done, ph.before(1) + 2)
            rope(bank(3), KIDX[:], C16, S16, 8, ph.free, 4)
            v.wait_ge(ph.free, 4)

            def q_unit(u, dst, n, cos, sin, half):
                for c in range(2):
                    v.wait_ge(ph.done, ph.before(u) + c + 1)
                    rope(bank((u % 2) * 2 + c), dst[:, n + c, :], cos, sin, half, ph.free, 2 * u + c + 1)

            for u in range(2, 6):
                q_unit(u, AQI, 2 * (u - 2), C16, S16, 8)
                if u == 3:
                    norm("ckv", lambda k: CKV[:, k, :], lambda k: par("kv_norm", k), dst=(CH, CL))
            for t in range(1, ROWT):
                acc = PICK[:, t - 1, :]
                step(nc.vector.memset(acc[:, 0:t * P], 0.0))
                step(nc.vector.tensor_copy(acc[:, t * P:(t + 1) * P], cst("le", P)))

            def pick_eight(t, last):
                acc = PICK[:, t - 1, 0:(t + 1) * P]
                step(nc.vector.max(M8[:], acc))
                step(nc.vector.match_replace(acc, M8[:], acc, PICKED))
                if last:
                    step(nc.vector.tensor_scalar(acc, acc, PICKED / 2, NEG, ALU.is_gt, ALU.mult))

            def q_rope(tile):
                u, c = 6 + tile // 2, tile % 2
                v.wait_ge(ph.done, ph.before(u) + c + 1)
                rope(bank((u % 2) * 2 + c), AQ[:, tile, :], C32, S32, 16, ph.free, 2 * u + c + 1)

            v.wait_ge(qkv_ready, 1)
            n = 0
            for t in range(1, ROWT):
                W = (t + 1) * P
                acc = PICK[:, t - 1, 0:W]
                for h in range(IDX_HEADS):
                    v.wait_ge(relu_ready, n + 1)
                    nc.vector.scalar_tensor_tensor(out=acc, in0=T[:, n % 2, 0:W], scalar=WIDX[:, t, h:h + 1], in1=acc,
                                                   op0=ALU.mult, op1=ALU.add).then_inc(idx_summed, 1)
                    v.wait_ge(idx_summed, n + 1)
                    if t > 1:
                        pick_eight(t - 1, h == TOPK // 8 - 1)
                    for tile in range(min(finished(FILL_IDX, n - 1) if n else 0, 8), min(finished(FILL_IDX, n), 8)):
                        q_rope(tile)
                    n += 1
            for h in range(TOPK // 8):
                pick_eight(ROWT - 1, h == TOPK // 8 - 1)
            attend(a_all)

            v.wait_ge(PH["mod"].done, 24)
            for w in range(2):
                nc.vector.tensor_tensor(MODV[:, :, w], bank(0, 0, 96).rearrange("p (n w) -> p n w", w=2)[:, :, w],
                                        par("b_mod", 0, 48), ALU.add).then_inc(mod_ready, 1)
            v.wait_ge(mod_ready, 2)
            for n, (g, col, w, one) in enumerate((("g_pre1", 8, 0, 1), ("g_pre1", 8, 1, 1), ("g_post1", 16, 0, 0),
                                                  ("g_pre2", 32, 0, 1), ("g_post2", 40, 0, 0))):
                step(nc.vector.scalar_tensor_tensor(out=DER[:, n, :], in0=MODV[:, col:col + 8, w], scalar=float(one),
                                                    in1=par(g, 0, 8), op0=ALU.add, op1=ALU.mult))

            residual(PH["a_out"], XT, "add")

            norm("ffn0", lambda k: XT[:, k, :], lambda k: par("g_ffn", k))
            ffn(0, XT, ("add", "add"))
            norm("mix1", lambda k: XT[:, k, :], lambda k: par("g_mix", 8 + k))

            ph = PH["b_in"]

            def b_tile(u, c, dst, count):
                v.wait_ge(ph.done, ph.before(u) + c + 1)
                rope(bank((u % 2) * 2 + c if u < 3 else c), dst, C16, S16, 8, ph.free, count, swapped=BSW)

            for c in range(2):
                b_tile(0, c, BK[:, c, :], c + 1)
            for c in range(2):
                b_tile(2, c, BQ[:, c, :], c + 3)

            def b_between(k):
                for tile in range(min(finished(FILL_B, k - 1) if k else 0, 6), min(finished(FILL_B, k), 6)):
                    b_tile(3 + tile // 2, tile % 2, BQ[:, 2 + tile, :], 5 + tile)
            attend(b_all, b_between)
            residual(PH["b_out"], XT, "add")
            norm("ffn1", lambda k: XT[:, k, :], lambda k: par("g_ffn", 8 + k))
            ffn(1, XT, ("add", "add"))

            norm("final", lambda k: XT[:, k, :], lambda k: par("g_final", k), into="self")
            norm("ctx", lambda k: CTXT[:, k, :], lambda k: DER[:, 1, k:k + 1], shift=lambda k: MODV[:, k, 1:2])
            norm("pre1", lambda k: XT[:, k, :], lambda k: DER[:, 0, k:k + 1], shift=lambda k: MODV[:, k, 0:1])
            ph = PH["c_in"]
            v.wait_ge(load_tab, 32)
            for u in range(2):
                q_unit(u, CQ, 2 * u, AXC, AXS, 16)
            v.wait_ge(ph.done, ph.before(2) + 1)
            rope(bank(0), CK[:], AXC, AXS, 16, ph.free, 5)
            attend(c_range)
            for g in range(4):
                v.wait_ge(f2_hi, g + 1)
                nc.vector.tensor_tensor(HL[:, 4 + g, :], bank(2 + g % 2), HH[:, 4 + g, :].bitcast(F32),
                                        ALU.subtract).then_inc(four_ready, 1)
            ph = PH["merge"]
            for u in range(4):
                for c in range(2):
                    m = 2 * u + c
                    v.wait_ge(gates_ready, 2)
                    v.wait_ge(ph.done, 4 * u + c + 1)
                    step(nc.vector.tensor_tensor(T[:, c, :], bank(c), GA[:, m, :], ALU.mult))
                    v.wait_ge(ph.done, 4 * u + c + 3)
                    step(nc.vector.tensor_tensor(T[:, 2 + c, :], bank(2 + c), GF[:, m, :], ALU.mult))
                    t = T[:, 4 + m % 2, :]
                    nc.vector.tensor_tensor(t, T[:, c, :], T[:, 2 + c, :], ALU.add).then_inc(m_ready, 1)
                    v.wait_ge(m_hi, m + 1)
                    nc.vector.tensor_tensor(ML[:, m, :], t, MH[:, m, :].bitcast(F32), ALU.subtract).then_inc(m_lo, 1)
            ph = PH["c_out"]
            for u in range(4):
                for c in range(2):
                    v.wait_ge(ph.done, 2 * u + c + 1)
                    nc.vector.tensor_copy(Y[:, 2 * u + c, :], bank((u % 2) * 2 + c)).then_inc(ph.free, 1)
            norm("post1", lambda k: Y[:, k, :], lambda k: DER[:, 2, k:k + 1], into="x")
            norm("pre2", lambda k: XT[:, k, :], lambda k: DER[:, 3, k:k + 1], shift=lambda k: MODV[:, 24 + k, 0:1])
            ffn(2, Y2, ("copy", "add"))
            norm("post2", lambda k: Y2[:, k, :], lambda k: DER[:, 4, k:k + 1], into="x")

        @block.tensor
        def _(pe):
            last_read = {}

            def bank_free(b):
                if b in last_read:
                    pe.wait_ge(*last_read[b])

            def products(out, pairs, done=None):
                n = len(pairs)
                for k, (wh, wl, ah, al, swap, ready) in enumerate(pairs):
                    if ready is not None:
                        pe.wait_ge(*ready)
                    for m, (w, a) in enumerate(((wh, ah), (wh, al), (wl, ah))):
                        l, r = (a, w) if swap else (w, a)
                        ins = nc.tensor.matmul(out, l, r, start=(k == 0 and m == 0), stop=(k == n - 1 and m == 2))
                        if k == n - 1 and m == 2 and done is not None:
                            ins.then_inc(done, 1)
                        yield

            def advance(work, count=None):
                while count is None or count > 0:
                    if next(work, True):
                        return
                    count = count and count - 1

            def gemm(ph, kc, width, act_hi, act_lo, rows=S, ready=None, first8=None):
                t = ph.tiles
                period = 2 * t

                def body(i, j):
                    u = 2 * i + j
                    slot = (ph.split + j) % 2
                    pe.wait_ge(lo_ready, 2 * i + (j + ph.split + 1))
                    for c in range(t):
                        b = j * t + c
                        if isinstance(i, int) and i == 0:
                            bank_free(b)
                        elif ph.name.startswith("up"):
                            pe.wait_ge(ph.free, u - 1)
                        else:
                            pe.wait_ge(ph.free, u * t + (c + 1 - period))
                        advance(products(bank(b, 0, rows), [
                            (HI[slot][:, k * width + c * P:k * width + (c + 1) * P],
                             LO[slot][:, k * width + c * P:k * width + (c + 1) * P],
                             (first8[0] if first8 and k < 8 else act_hi)[:, k, 0:rows],
                             (first8[1] if first8 and k < 8 else act_lo)[:, k, 0:rows], False,
                             ready(k) if ready is not None and isinstance(u, int) and u == 0 and c == 0 else None)
                            for k in range(kc)], ph.done))
                each_unit(pe, ph.n, body)
                for u in range(max(0, ph.n - 2), ph.n):
                    for c in range(t):
                        last_read[(u % 2) * t + c] = (ph.free, u + 1 if ph.name.startswith("up") else u * t + c + 1)

            def t_tiles(ph, u, cs, bs, width=256, rows=S, ah=HH, al=HL, kc=DC, ready=None):
                slot = (ph.split + u) % 2
                for n, (c, b) in enumerate(zip(cs, bs)):
                    bank_free(b)
                    yield from products(bank(b, 0, rows), [
                        (HI[slot][:, k * width + c * P:k * width + (c + 1) * P],
                         LO[slot][:, k * width + c * P:k * width + (c + 1) * P], ah[:, k, 0:rows], al[:, k, 0:rows],
                         False, ready(k) if ready and n == 0 else None) for k in range(kc)], ph.done)

            def r_tiles(ph, u, rts, bs, lo, n, width=256, kc=DC, ah=HH, al=HL):
                slot = (ph.split + u) % 2
                for rt, b in zip(rts, bs):
                    bank_free(b)
                    yield from products(bank(b, 0, n), [
                        (HI[slot][:, k * width + lo:k * width + lo + n], LO[slot][:, k * width + lo:k * width + lo + n],
                         ah[:, k, rt * P:(rt + 1) * P], al[:, k, rt * P:(rt + 1) * P], True, None)
                        for k in range(kc)], ph.done)

            def unit_ready(ph, u):
                pe.wait_ge(lo_ready, ph.split + u + 1)

            def norm(name):
                i, nch, rows, b, s = NORMS[name]
                bank_free(4)
                for k in range(nch):
                    pe.wait_ge(square_ready, b + k + 1)
                    nc.tensor.matmul(bank(4, 0, rows), ONES[:], T[:, k % 2, 0:rows], start=(k == 0),
                                     stop=(k == nch - 1)).then_inc(square_used, 1)
                last_read[4] = (root_ready, i + 1)

            def h_chunk(name):
                s = NORMS[name][4]
                return lambda k: (h_ready, s + k + 1)

            def attend(rng, between=None):
                lo, hi = rng

                def scores(s):
                    st = steps[s]
                    if s < lo + 2:
                        for b in (2, 3):
                            bank_free(b + 2 * (s % 2))
                    else:
                        pe.wait_ge(max_ready if steps[s - 2]["mask"] is not None else exp_done, s - 1)
                        if s - 2 >= c_range[0]:
                            pe.wait_ge(turned_ready, s - 2)
                    for off, q, k in st["qk"]:
                        n = k.shape[-1]
                        ins = nc.tensor.matmul(ps[:, scores_at(s, 0) + off:scores_at(s, 0) + off + n], q, k,
                                               start=True, stop=True)
                    ins.then_inc(scores_done, 1)

                def turn(s):
                    st = steps[s]
                    pe.wait_ge(p_ready, s + 1)
                    if s > lo:
                        pe.wait_ge(turned_ready, s)
                    else:
                        bank_free(6)
                    for n in range(st["nk"] * st["nh"] // P):
                        a0 = 6 * S + n * P if n < 4 else scores_at(s, 1) + S - P
                        ins = nc.tensor.transpose(ps[:, a0:a0 + P], TW[:, probs_at(s) + n * P:probs_at(s) + (n + 1) * P],
                                                  cst("ident", P))
                    ins.then_inc(turned_done, 1)

                def values(s):
                    st = steps[s]
                    f = st["flush"]
                    pe.wait_ge(turned_ready, s + 1)
                    if st["first"]:
                        if s > lo:
                            pe.wait_ge(o_ready, f)
                        else:
                            bank_free(7)
                    kb_n = st["nk"] // P
                    for n in range(st["nh"]):
                        p0, m, col = st["out"][n]
                        for b in range(kb_n):
                            c0 = turned_at(s) + (n * kb_n + b) * P
                            ins = nc.tensor.matmul(ps[p0:p0 + m, 7 * S + col * P:7 * S + (col + 1) * P],
                                                   st["pv"][n][b], TW[:, c0:c0 + P], start=(b == 0), stop=(b == kb_n - 1))
                    ins.then_inc(pv_done, 1)

                scores(lo)
                scores(lo + 1)
                for s in range(lo, hi):
                    if between:
                        between(s - lo, True)
                    turn(s)
                    if s + 2 < hi:
                        scores(s + 2)
                    if s > lo:
                        values(s - 1)
                    if between:
                        between(s - lo, False)
                values(hi - 1)
                for b in range(2, 6):
                    last_read[b] = (exp_done, hi)
                last_read[6] = (turned_ready, hi)
                last_read[7] = (o_ready, steps[hi - 1]["flush"] + 1)

            pe.wait_ge(ones_ready, 1)
            norm("mem")
            norm("mix0")
            ph = PH["memkv"]
            for u in range(4):
                unit_ready(ph, u)
                b = (u % 2) * 2
                if u >= 2:
                    last_read[b], last_read[b + 1] = (ph.free, 2 * u - 3), (ph.free, 2 * u - 2)
                if u % 2 == 0:
                    advance(t_tiles(ph, u, (0, 1), (b, b + 1), rows=MEM, ah=MEMH, al=MEML,
                                    ready=h_chunk("mem") if u == 0 else None))
                else:
                    advance(r_tiles(ph, u, (0, 1), (b, b + 1), 0, 256, ah=MEMH, al=MEML))
            for b in range(4):
                last_read[b] = (ph.free, 5 + b)

            ph = PH["a_in"]
            for u in range(6):
                unit_ready(ph, u)
                b = (u % 2) * 2
                advance(t_tiles(ph, u, (0, 1), (b, b + 1), ready=h_chunk("mix0") if u == 0 else None))
                last_read[b], last_read[b + 1] = (ph.free, 2 * u + 1), (ph.free, 2 * u + 2)
                if u == 1:
                    slot = (ph.split + u) % 2
                    bank_free(5)
                    for rt in range(ROWT):
                        advance(products(bank(5, rt * 16, rt * 16 + 16), [
                            (HI[slot][:, k * 256 + 32:k * 256 + 48], LO[slot][:, k * 256 + 32:k * 256 + 48],
                             HH[:, k, rt * P:(rt + 1) * P], HL[:, k, rt * P:(rt + 1) * P], True, None)
                            for k in range(DC)], ph.done if rt == ROWT - 1 else None))
                    last_read[5] = (qkv_ready, 1)
                if u == 3:
                    norm("ckv")

            def a_rest():
                for u in range(6, 11):
                    unit_ready(ph, u)
                    b = (u % 2) * 2
                    yield from t_tiles(ph, u, (0, 1), (b, b + 1))
                    last_read[b], last_read[b + 1] = (ph.free, 2 * u + 1), (ph.free, 2 * u + 2)

            rest = a_rest()
            n = 0
            pe.wait_ge(ph.free, 12)
            for t in range(1, ROWT):
                for h in range(IDX_HEADS):
                    b = 4 + n % 3
                    if n >= 3:
                        pe.wait_ge(relu_ready, n - 2)
                    else:
                        bank_free(b)
                    j = h % 2
                    nc.tensor.matmul(bank(b, 0, (t + 1) * P), AQI[64 * j:64 * j + 64, h // 2, t * P:(t + 1) * P],
                                     KIDX[64 * j:64 * j + 64, 0:(t + 1) * P], start=True, stop=True).then_inc(idx_done, 1)
                    advance(rest, FILL_IDX)
                    n += 1
            advance(rest)
            for b in (4, 5, 6):
                last_read[b] = (relu_ready, n)
            last_read[0], last_read[1] = (qkv_ready, 2), (qkv_ready, 3)

            def mod_unit(k, first):
                ph = PH["mod"]
                if k >= ph.n or first:
                    return
                if k == 0:
                    pe.wait_ge(silu_c_ready, 1)
                    bank_free(0)
                slot = (ph.land + k) % 2
                pe.wait_ge(raw_landed[slot], 16 * ((ph.land + k) // 2 + 1))
                for c in range(2):
                    col = 4 * k + 2 * c
                    for m in range(DC):
                        ins = nc.tensor.matmul(bank(0, col, col + 2), RAW[slot][:, m * 256 + c * P:m * 256 + (c + 1) * P],
                                               SV[:, 2 * m:2 * m + 2], start=(m == 0), stop=(m == DC - 1))
                ins.then_inc(ph.done, 1)

            ph = PH["uk"]
            unit_ready(ph, 0)
            pe.wait_ge(h_ready, NORMS["ckv"][4] + 2)
            for h in range(8):
                if h >= 4:
                    last_read[h % 4] = (ph.free, h - 3)
                advance(t_tiles(ph, 0, (h,), (h % 4,), width=1024, ah=CH, al=CL, kc=2))
            for b in range(4):
                last_read[b] = (ph.free, 5 + b)
            ph = PH["uv"]
            unit_ready(ph, 0)
            for n in range(8):
                if n >= 4:
                    last_read[n % 4] = (ph.free, n - 3)
                advance(r_tiles(ph, 0, (n // 2,), (n % 4,), (n % 2) * S, S, width=1024, kc=2, ah=CH, al=CL))
            for b in range(4):
                last_read[b] = (ph.free, 5 + b)
            pe.wait_ge(ph.free, 8)
            attend(a_all, mod_unit)
            last_read[0] = (mod_ready, 2)
            gemm(PH["a_out"], 10, P, HH, HL, ready=lambda k: (o_ready, flushed(am_range)))

            def ffn(l, name):
                for h in range(2):
                    gemm(PH[f"up{l}{h}"], DC, 256, HH, HL, ready=h_chunk(name) if h == 0 else None)
                    gemm(PH[f"dn{l}{h}"], HALF, P, GH, GL, ready=lambda k: (g_ready, (2 * l + h) * HALF + k + 1))

            norm("ffn0")
            ffn(0, "ffn0")
            norm("mix1")
            ph = PH["b_in"]
            for u in range(3):
                unit_ready(ph, u)
                b = (u % 2) * 2
                if u == 1:
                    last_read[4] = (root_ready, NORMS["mix1"][0] + 1)
                    advance(r_tiles(ph, u, range(4), range(4, 8), 0, 256))
                    for t in range(4):
                        last_read[4 + t] = (qkv_ready, 11 + t + 1)
                else:
                    advance(t_tiles(ph, u, (0, 1), (b, b + 1), ready=h_chunk("mix1") if u == 0 else None))
                    last_read[b], last_read[b + 1] = (ph.free, u + 1), (ph.free, u + 2)

            def b_rest():
                for u in range(3, 7):
                    unit_ready(ph, u)
                    yield from t_tiles(ph, u, (0, 1), (0, 1))
                    last_read[0], last_read[1] = (ph.free, 2 * u - 1), (ph.free, 2 * u)
                last_read[0], last_read[1] = (qkv_ready, 16), (qkv_ready, 17)

            rest = b_rest()

            def b_between(k, first):
                if first:
                    group = (k + 2) // 4
                    if k % 4 == 2 and 2 <= group < 8:
                        pe.wait_ge(ph.free, 3 + group)
                    elif k % 4 == 2 and group == 8:
                        pe.wait_ge(qkv_ready, 17)
                else:
                    advance(rest, FILL_B)
            pe.wait_ge(qkv_ready, 15)
            pe.wait_ge(ph.free, 4)
            attend(b_all, b_between)
            advance(rest)
            gemm(PH["b_out"], 10, P, HH, HL, ready=lambda k: (o_ready, flushed(bm_range)), first8=BO)
            norm("ffn1")
            ffn(1, "ffn1")

            norm("final")
            norm("ctx")
            ph = PH["ctx"]
            unit_ready(ph, 0)
            advance(t_tiles(ph, 0, (0,), (0,), rows=MEM, ready=h_chunk("ctx")))
            advance(r_tiles(ph, 0, (0, 1), (1, 2), P, P))
            for b in range(3):
                last_read[b] = (ph.free, b + 1)
            norm("pre1")
            ph = PH["c_in"]
            for u in range(3):
                unit_ready(ph, u)
                b = (u % 2) * 2
                if u == 2:
                    advance(t_tiles(ph, u, (0,), (0,)))
                    last_read[0] = (ph.free, 5)
                    last_read[4] = (root_ready, NORMS["pre1"][0] + 1)
                    advance(r_tiles(ph, u, range(4), range(4, 8), P, P))
                    for t in range(4):
                        last_read[4 + t] = (qkv_ready, 17 + t + 1)
                else:
                    advance(t_tiles(ph, u, (0, 1), (b, b + 1), ready=h_chunk("pre1") if u == 0 else None))
                    last_read[b], last_read[b + 1] = (ph.free, 2 * u + 1), (ph.free, 2 * u + 2)

            def c_rest():
                for u in range(3, 13):
                    unit_ready(ph, u)
                    yield from t_tiles(ph, u, (0, 1), (0, 1))
                    last_read[0], last_read[1] = (ph.free, 2 * u), (ph.free, 2 * u + 1)

            rest = c_rest()
            pe.wait_ge(qkv_ready, 21)
            pe.wait_ge(ph.free, 5)
            attend(c_range, lambda k, first: None if first else advance(rest, FILL_C))
            advance(rest)
            pe.wait_ge(load_tab, 48)
            for g in range(4):
                for t2 in range(2):
                    if g:
                        pe.wait_ge(f1_ready, 2 * g - 1 + t2)
                    else:
                        bank_free(t2)
                        bank_free(2 + t2)
                    for t in range(2):
                        rt = 2 * t2 + t
                        ins = nc.tensor.matmul(bank(t2, t * 256, t * 256 + 256), FT[:, g, rt * P:(rt + 1) * P],
                                               cst("dft_c", 256), start=True, stop=True)
                    ins.then_inc(f1_done, 1)
                pe.wait_ge(f1_ready, 2 * g + 2)
                if g >= 2:
                    pe.wait_ge(four_ready, g - 1)
                for n in range(8):
                    rt, part = n // 2, n % 2
                    ins = nc.tensor.matmul(bank(2 + g % 2), F1[g % 2][:, rt, part * P:(part + 1) * P],
                                           DFT[:, rt, part * S:(part + 1) * S], start=(n == 0), stop=(n == 7))
                ins.then_inc(f2_done, 1)

            last_read.update({0: (f1_ready, 7), 1: (f1_ready, 8), 2: (four_ready, 3), 3: (four_ready, 4)})
            ph = PH["merge"]
            pe.wait_ge(o_ready, flushed(c_range))
            pe.wait_ge(four_ready, 4)
            for u in range(4):
                unit_ready(ph, u)
                slot = (ph.split + u) % 2
                for part in range(2):
                    for c in range(2):
                        b = 2 * part + c
                        bank_free(b)
                        advance(products(bank(b), [
                            (HI[slot][:, 1024 * part + k * 256 + c * P:1024 * part + k * 256 + (c + 1) * P],
                             LO[slot][:, 1024 * part + k * 256 + c * P:1024 * part + k * 256 + (c + 1) * P],
                             HH[:, 4 + k, :] if part else CO[0][:, k, :],
                             HL[:, 4 + k, :] if part else CO[1][:, k, :], False, None)
                            for k in range(4)], ph.done))
                        last_read[b] = (m_ready, 2 * u + c + 1)
            gemm(PH["c_out"], DC, 256, MH, ML, ready=lambda k: (m_lo, k + 1))
            norm("post1")
            norm("pre2")
            ffn(2, "pre2")
            norm("post2")


def kernel(**inputs):
    import numpy as _np
    import concourse.bacc as _bacc
    from concourse.bass_utils import run_bass_kernel_spmd as _run

    x = {k: _np.asarray(a) for k, a in inputs.items()}
    weights, params, x_t, mem_t, ctx_t = lay_out(x)
    const, axial, rows = constants()
    nc = _bacc.Bacc("TRN2", target_bir_lowering=False, num_devices=1)
    arrays = {}

    def given(name, a):
        a = _np.ascontiguousarray(a)
        arrays[name] = a
        return nc.dram_tensor(name, a.shape, mybir.dt.from_np(a.dtype), kind="ExternalInput").ap()

    wd = {k: given(f"w_{k}", a) for k, a in weights.items()}
    others = [given(n, a) for n, a in (("params", params), ("constants", const), ("axial", axial), ("dft", rows),
                                       ("x_t", x_t), ("mem_t", mem_t), ("ctx_t", ctx_t), ("positions", x["positions"]))]
    out = nc.dram_tensor("out_t", (P, DC, S), F32, kind="ExternalOutput").ap()
    program(nc, wd, *others, out)
    r = _run(nc, [arrays], core_ids=[0])
    got = r.results[0]["out_t"]
    return _np.ascontiguousarray(got.transpose(2, 1, 0).reshape(1, S, D))
```

```python
import math
from contextlib import ExitStack

import numpy as np

import concourse.bass as bass
from concourse import mybir

F32 = mybir.dt.float32
F32R = mybir.dt.float32r
I32 = mybir.dt.int32
ALU = mybir.AluOpType
ACT = mybir.ActivationFunctionType
AX = mybir.AxisListType

P = 128
S = 512
ROWT = S // P
D = 1024
DC = D // P
MEM = 256
FF = 2816
FC = FF // P
HALF = FC // 2
KB = 1024
EPS = 1e-6
NEG = -1e30
PICKED = -3e38
TOPK = 128
A_HEADS = 8
IDX_HEADS = 16
KV_RANK = 256

PARAMS = [("g_mix", 16), ("g_ffn", 16), ("g_mem", 8), ("g_final", 8), ("g_pre1", 8), ("g_post1", 8),
          ("g_pre2", 8), ("g_post2", 8), ("kv_norm", 2), ("conv0", 4 * FC), ("conv1", 4 * FC),
          ("conv2", 4 * FC), ("b_mod", 48), ("sink_b", 16), ("sink_c", 8)]
PCOL, _n = {}, 0
for _name, _w in PARAMS:
    PCOL[_name] = _n
    _n += _w
NPARAM = _n

CONSTS = [("ge", P), ("z0", P), ("le", P), ("z1", P), ("z2", P), ("z3", P), ("ge2", P), ("gt", P), ("le2", P),
          ("ident", P), ("dft_c", 2 * P), ("inv32", 1), ("inv16", 1), ("sgn32", 1), ("sgn16", 1), ("eps", 1)]
CCOL, _n = {}, 0
for _name, _w in CONSTS:
    CCOL[_name] = _n
    _n += _w
NCONST = _n


def constants():
    q, k = np.arange(P)[:, None], np.arange(P)[None, :]
    c = np.zeros((P, NCONST), np.float32)

    def put(name, a):
        c[:, CCOL[name]:CCOL[name] + a.shape[1]] = a

    ge, le, gt = (np.where(ok, 0.0, NEG).astype(np.float32) for ok in (k >= q, k <= q, k > q))
    for name, a in (("ge", ge), ("ge2", ge), ("le", le), ("le2", le), ("gt", gt)):
        put(name, a)
    put("ident", np.eye(P, dtype=np.float32))
    ang = 2 * np.pi * ((q * k) % P) / P
    put("dft_c", np.concatenate([np.cos(ang), np.sin(ang)], 1).astype(np.float32))
    p = np.arange(P)
    for name, head, rot in (("32", 128, 32), ("16", 64, 16)):
        d, half = p % head, rot // 2
        inv = np.float32(500000.0) ** (-(2.0 * (d % half)).astype(np.float32) / np.float32(rot))
        put("inv" + name, np.where(d < rot, inv, 0.0).astype(np.float32)[:, None])
        put("sgn" + name, np.where(d < half, -1.0, 1.0).astype(np.float32)[:, None])
    put("eps", np.full((P, 1), EPS, np.float32))
    s = np.arange(S)
    d = p % 64
    inv = np.float32(10000.0) ** (-(2.0 * (d % 16)).astype(np.float32) / np.float32(32))
    at = np.where((d < 32)[:, None], (s // 64)[None, :], (s % 64)[None, :]).astype(np.float32)
    ang = at * inv[:, None]
    sgn = np.where(d % 32 < 16, -1.0, 1.0)[:, None]
    axial = np.stack([np.cos(ang), np.sin(ang) * sgn], 1).astype(np.float32)
    i = np.arange(S)
    ang = 2 * np.pi * ((i[:, None] * i[None, :]) % S) / S
    rows = np.concatenate([np.cos(ang), -np.sin(ang)], 1) / math.sqrt(S * P)
    rows = rows.astype(np.float32).reshape(ROWT, P, 2 * S).transpose(1, 0, 2)
    return c, axial, np.ascontiguousarray(rows)


STREAM = [("memkv", 4, 2048, [2, 2, 2, 2]),
          ("a_in", 11, 2048, 2),
          ("uk", 1, 2048, 8), ("uv", 1, 2048, 8),
          ("a_out", 8, 1280, 1),
          ("up00", HALF, 2048, 2), ("dn00", 8, HALF * P, 1), ("up01", HALF, 2048, 2), ("dn01", 8, HALF * P, 1),
          ("b_in", 7, 2048, [2, 4, 2, 2, 2, 2, 2]), ("b_out", 8, 1280, 1),
          ("up10", HALF, 2048, 2), ("dn10", 8, HALF * P, 1), ("up11", HALF, 2048, 2), ("dn11", 8, HALF * P, 1),
          ("ctx", 1, 2048, 3),
          ("c_in", 13, 2048, [2, 2, 5] + [2] * 10),
          ("merge", 4, 2048, 4), ("c_out", 4, 2048, 2),
          ("up20", HALF, 2048, 2), ("dn20", 8, HALF * P, 1), ("up21", HALF, 2048, 2), ("dn21", 8, HALF * P, 1)]


def units(w, width):
    k, n = w.shape
    return w.reshape(k // P, P, n // width, width).transpose(2, 1, 0, 3).reshape(n // width, P, -1)


def lay_out(x):
    w = {}
    kv = x["w_mem_kv"]
    w["memkv"] = np.concatenate([units(kv[0], 256), units(kv[1], 256)])
    a = x["a_w_in"][0]
    q, ckv, kr, qi, ki, wi, qm = np.split(a, np.cumsum([1024, 256, 32, 1024, 64, 16]).tolist(), axis=1)
    misc = np.concatenate([kr, wi, np.zeros((D, 80), np.float32), ki, ki], 1)
    w["a_in"] = units(np.concatenate([ckv, misc, qi, q, qm], 1), 256)
    w["mod"] = x["w_mod_2"][0].T.reshape(24, 2, P, D).transpose(0, 2, 1, 3).reshape(24, P, 2 * D)
    uk = x["a_w_uk"][0]
    w["uk"] = units(np.concatenate([np.zeros((KV_RANK, 8, 32), np.float32), uk], 2).reshape(KV_RANK, 1024), 1024)
    w["uv"] = units(x["a_w_uv"][0].reshape(KV_RANK, 1024), 1024)
    w["a_out"] = units(x["a_w_out"][0], P)
    pair8 = [h for c in range(4) for h in (c, c + 4)]
    pair16 = pair8 + [h + 8 for h in pair8]
    b = x["b_w_in"][0]
    bq = b[:, :1024].reshape(D, 16, 64)[:, pair16].reshape(D, 1024)
    w["b_in"] = units(np.concatenate([b[:, 1024:1536], bq, b[:, 1536:]], 1), 256)
    bo = x["b_w_out"][0]
    w["b_out"] = units(np.concatenate([bo[:1024].reshape(16, 64, D)[pair16].reshape(1024, D), bo[1024:]]), P)
    ups = [x["f_w_up"][0], x["f_w_up"][1], x["w_up_2"][0]]
    downs = [x["f_w_down"][0], x["f_w_down"][1], x["w_down_2"][0]]
    for l in range(3):
        up = ups[l].reshape(DC, P, 2, FC, P).transpose(3, 1, 0, 2, 4).reshape(FC, P, 2048)
        down = downs[l].reshape(2, HALF, P, DC, P).transpose(0, 3, 2, 1, 4).reshape(2, DC, P, HALF * P)
        for h in range(2):
            w[f"up{l}{h}"] = up[h * HALF:(h + 1) * HALF]
            w[f"dn{l}{h}"] = down[h]
    c = x["w_in_2"][0]
    w["ctx"] = units(c[:, 512:768], 256)
    cq = c[:, :512].reshape(D, 8, 64)[:, pair8].reshape(D, 512)
    w["c_in"] = units(np.concatenate([cq, c[:, 512:]], 1), 256)
    pa = x["w_pa_2"][0].reshape(8, 64, D)[pair8].reshape(512, D)
    w["merge"] = np.concatenate([units(pa, 256), units(x["w_pf_2"][0], 256)], 2)
    w["c_out"] = units(x["w_out_2"][0], 256)

    def cols(v):
        return v.reshape(-1, P).T

    def conv(cw, cb):
        return np.stack([cols(cw[0]), cols(cw[1]), cols(cw[2]), cols(cb)], 2).reshape(P, 4 * FC)

    sink_b = np.broadcast_to(x["b_sinks"][0][pair16], (P, 16))
    sink_c = np.broadcast_to(x["sink_2"][0][pair8], (P, 8))
    params = np.concatenate([
        cols(x["g_mix"]), cols(x["g_ffn"]), cols(x["g_mem"]), cols(x["g_final"]), cols(x["g_pre1_2"]),
        cols(x["g_post1_2"]), cols(x["g_pre2_2"]), cols(x["g_post2_2"]), cols(x["a_kv_norm"]),
        conv(x["f_conv_w"][0], x["f_conv_b"][0]), conv(x["f_conv_w"][1], x["f_conv_b"][1]),
        conv(x["conv_w_2"][0], x["conv_b_2"][0]), cols(x["b_mod_2"]), sink_b, sink_c], 1)

    def turned(t):
        n = t.shape[1]
        return t[0].reshape(n, DC, P).transpose(2, 1, 0)

    conds = np.concatenate([x["c_2"].reshape(1, D), x["c_ctx_2"].reshape(1, D)], 1)
    return w, params, turned(x["x"]), turned(x["mem"]), turned(x["ctx_2"]), conds


class Phase:

    def __init__(self, name, n, size, tiles, land, split):
        self.name, self.n, self.size, self.tiles = name, n, size, tiles
        self.land = land
        self.split = split
        self.done = None
        self.free = None

    def before(self, u):
        return sum(self.tiles[:u]) if isinstance(self.tiles, list) else u * self.tiles

    @property
    def total(self):
        return self.before(self.n)


class Chain:

    def __init__(self, eng, sem):
        self.eng, self.sem, self.n, self.off = eng, sem, 0, 0

    def step(self, ins):
        ins.then_inc(self.sem, 1)
        self.n += 1
        self.eng.wait_ge(self.sem, self.off + self.n)


def each_unit(eng, n, body, chain=None):
    if n < 8:
        for u in range(n):
            body(u // 2, u % 2)
        return
    at = chain.n if chain else 0
    body(0, 0)
    body(0, 1)
    per = chain.n - at if chain else 0
    last = (n - 1) // 2
    with eng.Fori(1, last) as i:
        if chain:
            chain.off = i * per - per
        body(i, 0)
        body(i, 1)
    if chain:
        chain.off = 0
        chain.n = at + per * last
    for u in range(2 * last, n):
        body(u // 2, u % 2)


def program(nc, wdram, params_d, const_d, axial_d, rows_d, x_d, mem_d, ctx_d, cond_d, pos_d, out_d):
    ctx = ExitStack()
    with ctx:
        def sem(name):
            return ctx.enter_context(nc.semaphore(name))

        base = (nc.sbuf_base + 63) // 64 * 64

        def at(name, kb, shape, dt=F32):
            return nc.alloc_sbuf_tensor_at(name, [P] + shape, dt, offset=base + int(kb * KB))

        XT = at("xT", 0, [DC, S])
        HH, HL = at("h_hi", 16, [10, S], F32R), at("h_lo", 36, [10, S], F32R)
        RAW = [at(f"raw{i}", 56 + 8 * i, [2048]) for i in range(2)]
        HI = [at(f"w_hi{i}", 72 + 8 * i, [2048], F32R) for i in range(2)]
        LO = [at(f"w_lo{i}", 88 + 8 * i, [2048], F32R) for i in range(2)]
        R = 104
        MEMT = at("memT", R, [DC, MEM])
        MEMH, MEML = at("mem_hi", R + 16, [DC, MEM], F32R), at("mem_lo", R + 24, [DC, MEM], F32R)
        AQ = at("a_q", R, [8, S])
        AQI, AK = at("a_q_idx", R + 16, [8, S]), at("a_k", R + 16, [8, S])
        CKV, KIDX, KROPE = at("c_kv", R + 32, [2, S]), at("k_idx", R + 36, [S]), at("k_rope", R + 38, [S])
        AV = at("a_v", R + 32, [ROWT, 1024])
        PICK = at("picked", R + 48, [3, S])
        CH, CL = at("c_hi", R + 56, [2, S], F32R), at("c_lo", R + 60, [2, S], F32R)
        WIDX = at("w_idx", R + 54, [ROWT, IDX_HEADS])
        QM = at("q_mem", R + 184 - 104 + 10, [2, S])
        GH, GL = at("g_hi", R, [HALF, S], F32R), at("g_lo", R + 22, [HALF, S], F32R)
        MODW, COND = [at(f"mod_w{i}", R + 44 + 8 * i, [2, D]) for i in range(2)], at("conditions", R + 60, [2, D])
        BQ, BK, BV = at("b_q", R, [8, S]), at("b_k", R + 16, [2, S]), at("b_v", R + 20, [ROWT, 256])
        BO = at("b_o_hi", R + 24, [8, S], F32R), at("b_o_lo", R + 40, [8, S], F32R)
        BSW = at("b_swapped", R + 56, [2, S])
        CTXT = at("ctxT", R + 48, [DC, MEM])
        GA, GF = at("gate_a", R, [8, S]), at("gate_f", R + 16, [8, S])
        CQ, FT = at("c_q", R + 32, [4, S]), at("f_t", R + 40, [4, S])
        CO = at("c_o_hi", R + 48, [4, S], F32R), at("c_o_lo", R + 56, [4, S], F32R)
        MH, ML = at("m_hi", R + 32, [8, S], F32R), at("m_lo", R + 64, [8, S], F32R)
        F1 = [at(f"f_rows{i}", 16 + 4 * i, [ROWT, 256]) for i in range(2)]
        Y = at("y", R, [DC, S])
        Y2 = at("y2", R + 44, [DC, S])
        C32, S32, C16, S16 = (at(n, R + 64 + 2 * i, [S]) for i, n in enumerate(("cos32", "sin32", "cos16", "sin16")))
        MK = [at(f"mem_k{l}", R + 72 + 4 * l, [2, MEM]) for l in range(2)]
        MV = [at(f"mem_v{l}", R + 74 + 4 * l, [2, 256]) for l in range(2)]
        DFT = at("dft_rows", R + 64, [ROWT, 1024])
        T = at("work", R + 80, [7, S])
        TW = at("work_flat", R + 80, [7 * S])
        small = [R + 94.0]

        def after(name, shape):
            t = at(name, small[0], shape)
            small[0] += -(-4 * math.prod(shape) // 32) * 32 / KB
            return t

        CST, PRM, ONES = after("const", [NCONST]), after("params", [NPARAM]), after("ones", [P])
        MODV, DER = after("mod", [48, 2]), after("derived", [5, 8])
        ST, M8, WARM = after("stats", [2, 12]), after("top8", [8]), after("tables_warm", [16])
        CKX, CVX = at("ctx_k", 32, [MEM]), at("ctx_v", 33, [2, P])
        CK, CV = at("c_k", 34, [S]), at("c_v", 52, [ROWT, P])
        assert base + small[0] * KB <= nc.sbuf_usable_end
        AXC, AXS = C16, S16
        POS = at("positions", R + 70, [S], I32)

        ps = ctx.enter_context(nc.psum_tensor("psum", [P, 8 * S], F32))

        def bank(b, a=0, z=S):
            return ps[:, b * S + a:b * S + z]

        def par(name, k, n=1):
            return PRM[:, PCOL[name] + k:PCOL[name] + k + n]

        def cst(name, n=1, off=0):
            return CST[:, CCOL[name] + off:CCOL[name] + off + n]

        PH, land, split = {}, 0, 0
        for name, n, size, tiles in STREAM:
            ph = PH[name] = Phase(name, n, size, tiles, land, split)
            ph.done, ph.free = sem(f"{name}_done"), sem(f"{name}_read")
            land += n
            split += n
        order = [PH[s[0]] for s in STREAM]
        MOD_PHASES = ["dn00", "dn01", "dn10"]

        raw_landed = [sem("raw_landed0"), sem("raw_landed1")]
        hi_ready, lo_ready = sem("w_hi_ready"), sem("w_lo_ready")

        SPREAD = ["ffn0", "mix1", "ffn1", "final", "post1", "post2"]
        NORMS = {}
        nb = sc = 0
        for i, (name, nch, rows, splits) in enumerate([
                ("mem", 8, MEM, True), ("mix0", 8, S, True), ("ckv", 2, S, True), ("ffn0", 8, S, True),
                ("mix1", 8, S, True), ("ffn1", 8, S, True), ("final", 8, S, False), ("ctx", 8, MEM, True),
                ("pre1", 8, S, True), ("post1", 8, S, False), ("pre2", 8, S, True), ("post2", 8, S, False)]):
            NORMS[name] = (i, nch, rows, nb, sc)
            nb += 1 if name in SPREAD else nch
            sc += nch if splits else 0
        square_ready, square_used, root_ready = sem("square_ready"), sem("square_used"), sem("root_ready")
        sum_ready = sem("sum_ready")
        scaled_ready, h_hi_ready, h_ready = sem("scaled_ready"), sem("h_hi_ready"), sem("h_ready")
        x_ready = sem("x_ready")
        XR = {"final": 0, "post1": 8, "post2": 16}

        steps, flushes = [], []

        def add_steps(group, last_of, targets):
            for n, s in enumerate(group):
                s["flush"] = len(flushes) + n // last_of
                s["first"] = n % last_of == 0
                s["last"] = n % last_of == last_of - 1
            flushes.extend(targets)
            lo = len(steps)
            steps.extend(group)
            return lo, len(steps)

        def whole(c, out=(HH, HL)):
            return out[0][:, c, :], out[1][:, c, :]

        def heads_of_tile(t, h4):
            return tuple(buf[:, 4 * h4:4 * h4 + 4, t * P:(t + 1) * P] for buf in (HH, HL))

        def q_tile(buf, c, j, t):
            return buf[64 * j:64 * j + 64, c, t * P:(t + 1) * P]

        def mem_steps(l):
            return [dict(nh=2, nk=256, mask=None, scale=0.125, sink=None,
                         qk=[(j * S, q_tile(QM, c, j, t), MK[l][64 * j:64 * j + 64, c, :]) for j in range(2)],
                         pv=[[(MV[l][:, kb_, (2 * c + j) * 64:(2 * c + j + 1) * 64]) for kb_ in range(2)] for j in range(2)],
                         out=[(64 * j, 64, t) for j in range(2)])
                    for c in range(2) for t in range(ROWT)]

        a_range = add_steps(
            [dict(nh=1, nk=(t + 1) * P, mask=cst("le", P) if t == 0 else PICK[:, t - 1, 0:(t + 1) * P],
                  scale=128 ** -0.5, sink=None,
                  qk=[(0, AQ[:, h, t * P:(t + 1) * P], AK[:, h, 0:(t + 1) * P])],
                  pv=[[AV[:, kb_, h * P:(h + 1) * P] for kb_ in range(t + 1)]], out=[(0, P, h % 4)])
             for t in range(ROWT) for h in range(A_HEADS)], 4, [heads_of_tile(t, h4) for t in range(ROWT) for h4 in range(2)])
        am_range = add_steps(mem_steps(0), ROWT, [whole(8), whole(9)])
        b_range = add_steps(
            [dict(nh=2, nk=min(t + 1, 2) * P, mask=cst("le", P) if t == 0 else cst("gt", 2 * P), scale=0.125,
                  sink=par("sink_b", 2 * c, 2),
                  qk=[(j * S, q_tile(BQ, c, j, t),
                       BK[64 * j:64 * j + 64, c // 4, max(t - 1, 0) * P:(t + 1) * P]) for j in range(2)],
                  pv=[[BV[:, kb_, (2 * (c // 4) + j) * 64:(2 * (c // 4) + j + 1) * 64]
                       for kb_ in range(max(t - 1, 0), t + 1)] for j in range(2)],
                  out=[(64 * j, 64, t) for j in range(2)])
             for c in range(8) for t in range(ROWT)], ROWT, [whole(c, BO) for c in range(8)])
        bm_range = add_steps(mem_steps(1), ROWT, [whole(8), whole(9)])

        def c_step(c, j, t):
            rows = slice(64 * j, 64 * j + 64)
            q = q_tile(CQ, c, j, t)
            k = [CK[rows, b * P:(b + 1) * P] for b in range(ROWT)]
            v = [CV[:, b, 64 * j:64 * j + 64] for b in range(ROWT)]
            kx = [CKX[rows, b * P:(b + 1) * P] for b in range(2)]
            vx = [CVX[:, b, 64 * j:64 * j + 64] for b in range(2)]
            if t == 0:
                mask, ks, vs = "z0", [k[0], k[1], *kx], [v[0], v[1], *vx]
            elif t == ROWT - 1:
                mask, ks, vs = "z1", [k[t], *kx, k[t - 1]], [v[t], *vx, v[t - 1]]
            else:
                mask, ks, vs = "ge", [*k[t - 1:t + 2], *kx], [*v[t - 1:t + 2], *vx]
            n = len(ks)
            return dict(nh=1, nk=n * P, mask=cst(mask, n * P), scale=0.125, sink=par("sink_c", 2 * c + j, 1),
                        qk=[(b * P, q, ks[b]) for b in range(n)], pv=[vs], out=[(64 * j, 64, t)])

        c_range = add_steps([c_step(c, j, t) for c in range(4) for j in range(2) for t in range(ROWT)],
                            2 * ROWT, [whole(c, CO) for c in range(4)])
        a_all, b_all = (a_range[0], am_range[1]), (b_range[0], bm_range[1])

        def scores_at(s, n):
            return (2 + 2 * (s % 2) + n) * S

        def wide(s):
            return 640 if s >= c_range[0] else S

        def probs_at(s):
            return (s % 3) * wide(s)

        def turned_at(s):
            return (3 + s % 2) * wide(s)

        def finished(rate, k):
            return rate * k // 24

        FILL_IDX, FILL_B, FILL_C = 5, 7, 15

        scores_done, max_ready, exp_done, p_ready = sem("scores_done"), sem("max_ready"), sem("exp_done"), sem("p_ready")
        turned_done, turned_ready, pv_done = sem("turned_done"), sem("turned_ready"), sem("pv_done")
        o_hi_ready, o_ready = sem("o_hi_ready"), sem("o_ready")

        def flushed(rng):
            return steps[rng[1] - 1]["flush"] + 1

        load_const, load_x, load_mem = sem("load_const"), sem("load_x"), sem("load_mem")
        load_ctx, load_tab = sem("load_ctx"), sem("load_tables")
        ones_ready, tables_ready = sem("ones_ready"), sem("tables_ready")
        angle_ready = sem("angle_ready")
        load_cond, cond_ready = sem("load_cond"), sem("cond_ready")
        mod_landed, mod_used = [sem("mod_landed0"), sem("mod_landed1")], sem("mod_used")
        misc_ready, misc_turned = sem("misc_ready"), sem("misc_turned")
        idx_done, relu_ready, idx_summed = sem("idx_done"), sem("relu_ready"), sem("idx_summed")
        conv_ready, silu_ready, g_ready = sem("conv_ready"), sem("silu_ready"), sem("g_ready")
        qkv_ready = sem("qkv_ready")
        f1_done, f1_ready, f2_done, f2_hi, four_ready = (sem(n) for n in (
            "f1_done", "f1_ready", "f2_done", "f2_hi_ready", "four_ready"))
        gates_ready = sem("gates_ready")
        m_ready, m_hi, m_lo = sem("m_ready"), sem("m_hi_ready"), sem("m_lo_ready")
        vec_steps = sem("vector_steps")
        out_landed = sem("out_landed")

        block = ctx.enter_context(nc.Block())

        @block.sync
        def _(sp):
            def occupant_read(p):
                if p < 2:
                    return
                sp.wait_ge(lo_ready, p - 1)

            for ph in order:
                def load(i, j, ph=ph):
                    slot = (ph.land + j) % 2
                    if isinstance(i, int) and i == 0:
                        occupant_read(ph.land + j)
                    else:
                        sp.wait_ge(lo_ready, 2 * i + (j - 1 + ph.split))
                    u = 2 * i + j
                    src = wdram[ph.name][u] if isinstance(u, int) else \
                        wdram[ph.name][bass.ds(u, 1), :, :].rearrange("a p n -> p (a n)")
                    sp.dma_start(RAW[slot][:, 0:ph.size], src).then_inc(raw_landed[slot], 16)
                each_unit(sp, ph.n, load)
            for c in range(DC):
                sp.wait_ge(x_ready, XR["post2"] + c + 1)
                sp.dma_start(out_d[:, c, :], XT[:, c, :]).then_inc(out_landed, 16)
            sp.wait_ge(out_landed, 16 * DC)

        @block.gpsimd
        def _(pool):
            pool.memset(ONES[:], 1.0).then_inc(ones_ready, 1)
            for ph in order:
                def low(i, j, ph=ph):
                    slot = (ph.split + j) % 2
                    pool.wait_ge(hi_ready, 2 * i + (j + ph.split + 1))
                    nc.gpsimd.tensor_tensor(LO[slot][:, 0:ph.size], RAW[slot][:, 0:ph.size],
                                            HI[slot][:, 0:ph.size].bitcast(F32), ALU.subtract).then_inc(lo_ready, 1)
                each_unit(pool, ph.n, low)

        @block.scalar
        def _(act):
            def hi_unit(ph, i, j):
                slot = (ph.split + j) % 2
                act.wait_ge(raw_landed[slot], i * 16 + 16 * ((ph.land + j) // 2 + 1))
                if not isinstance(i, int) or i > 0:
                    act.wait_ge(ph.done, ph.before(2 * i + j - 1))
                elif ph.split + j >= 2:
                    g = ph.split + j - 2
                    q = max((q for q in order if q.split <= g), key=lambda q: q.split)
                    act.wait_ge(q.done, q.before(g - q.split + 1))
                nc.scalar.activation(HI[slot][:, 0:ph.size], RAW[slot][:, 0:ph.size], ACT.Copy).then_inc(hi_ready, 1)

            AFTER_NORM = ["up00", "b_in", "up10", "c_in", "up20"]

            def second_unit(name):
                return lambda: hi_unit(PH[name], 0, 1)

            def next_hi(ph, i, j):
                if isinstance(i, int) and 2 * i + j == ph.n - 1:
                    k = order.index(ph) + 1
                    if ph.name != "a_in" and k < len(order):
                        hi_unit(order[k], 0, 0)
                elif j == 0:
                    if not (isinstance(i, int) and i == 0 and ph.name in AFTER_NORM):
                        hi_unit(ph, i, 1)
                else:
                    hi_unit(ph, i + 1, 0)

            def stream_only(ph):
                each_unit(act, ph.n, lambda i, j: next_hi(ph, i, j))

            def norm(name, src, ready, free=None, dst=(HH, HL), width=D, root_free=(), beside=None, after_root=None,
                     parts="squares root"):
                i, nch, rows, b, s = NORMS[name]
                if "squares" in parts and name not in SPREAD:
                    squares(range(nch), rows, b, src, ready)
                if "root" not in parts:
                    return
                for w in root_free:
                    act.wait_ge(*w)
                if name in SPREAD:
                    nc.scalar.activation(WARM[:, i:i + 1], cst("eps"), ACT.Sqrt)
                act.wait_ge(square_used, b + (1 if name in SPREAD else nch))
                nc.scalar.activation(T[:, 2, 0:rows], bank(4, 0, rows), ACT.Sqrt, bias=cst("eps"),
                                     scale=1.0 / width).then_inc(root_ready, 1)
                if after_root:
                    after_root()
                if free is not None:
                    for w in free:
                        act.wait_ge(*w)
                    for k in range(nch):
                        if beside:
                            beside(k)
                        act.wait_ge(scaled_ready, s + k + 1)
                        nc.scalar.activation(dst[0][:, k, 0:rows], T[:, 4 + k % 2, 0:rows], ACT.Copy).then_inc(h_hi_ready, 1)

            def squares(chunks, rows, b, src, ready):
                for k in chunks:
                    for w in ready(k):
                        act.wait_ge(*w)
                    if k >= 2:
                        act.wait_ge(square_used, b + k - 1)
                    nc.scalar.activation(T[:, k % 2, 0:rows], src(k), ACT.Square).then_inc(square_ready, 1)

            def hi_split(g):
                q = max((q for q in order if q.split <= g), key=lambda q: q.split)
                hi_unit(q, (g - q.split) // 2, (g - q.split) % 2)

            def attend(rng, between=None):
                lo, hi = rng

                def exps(s):
                    st, W = steps[s], steps[s]["nk"]
                    act.wait_ge(max_ready, s + 1)
                    if st["mask"] is None and s >= 3:
                        act.wait_ge(turned_done, s - 2)
                    for n in range(st["nh"]):
                        sm = TW[:, probs_at(s) + n * W:probs_at(s) + (n + 1) * W]
                        src = sm if st["mask"] is not None else ps[:, scores_at(s, n):scores_at(s, n) + W]
                        last = nc.scalar.activation(sm, src, ACT.Exp, bias=ST[:, s % 2, 2 + n:3 + n], scale=st["scale"],
                                                    accum_out=ST[:, s % 2, 4 + n:5 + n])
                        if st["sink"] is not None:
                            last = nc.scalar.activation(ST[:, s % 2, 6 + n:7 + n], st["sink"][:, n:n + 1], ACT.Exp,
                                                        bias=ST[:, s % 2, 2 + n:3 + n])
                    last.then_inc(exp_done, 1)

                def turned(s):
                    W = steps[s]["nk"] * steps[s]["nh"]
                    act.wait_ge(turned_done, s + 1)
                    if s >= 2:
                        act.wait_ge(pv_done, s - 1)
                    d = turned_at(s)
                    ins = nc.scalar.activation(TW[:, d:d + min(W, S)], bank(6, 0, min(W, S)), ACT.Copy)
                    if W > S:
                        a0 = scores_at(s, 1) + S - P
                        ins = nc.scalar.activation(TW[:, d + S:d + W], ps[:, a0:a0 + P], ACT.Copy)
                    ins.then_inc(turned_ready, 1)

                def flush(s):
                    f = steps[s]["flush"]
                    act.wait_ge(pv_done, s + 1)
                    out = flushes[f][0]
                    src = bank(7) if len(out.shape) == 2 else bank(7).rearrange("p (h n) -> p h n", h=4)
                    nc.scalar.activation(out, src, ACT.Copy).then_inc(o_hi_ready, 1)

                for s in range(lo, hi):
                    exps(s)
                    if s > lo:
                        turned(s - 1)
                    if s >= lo + 2 and steps[s - 2]["last"]:
                        flush(s - 2)
                    if between:
                        between(s - lo)
                turned(hi - 1)
                for s in range(hi - 2, hi):
                    if steps[s]["last"]:
                        flush(s)

            def ffn_up(ph, first):
                def body(i, j):
                    next_hi(ph, i, j)
                    act.wait_ge(conv_ready, 2 * i + (j + 1 + first))
                    nc.scalar.activation(T[:, 2 + j, :], T[:, j, :], ACT.Silu).then_inc(silu_ready, 1)
                each_unit(act, ph.n, body)

            act.dma_start(MEMT[:], mem_d).then_inc(load_mem, 16)
            act.dma_start(CST[:], const_d).then_inc(load_const, 16)
            act.dma_start(PRM[:], params_d).then_inc(load_const, 16)
            act.dma_start(POS[:], pos_d.partition_broadcast(P)).then_inc(load_const, 16)
            act.dma_start(XT[:], x_d).then_inc(load_x, 16)

            norm("mem", lambda k: MEMT[:, k, :], lambda k: [(load_mem, 16)], free=[], dst=(MEMH, MEML),
                 root_free=[(load_const, 48)],
                 beside=lambda k: squares([k], S, NORMS["mix0"][3], lambda k: XT[:, k, :], lambda k: [(load_x, 16)]))
            ph = PH["memkv"]
            hi_unit(ph, 0, 0)
            def mem_copies(u):
                l, v = u // 2, u % 2
                for c in range(2):
                    act.wait_ge(ph.done, 2 * u + c + 1)
                    b = (u % 2) * 2 + c
                    dst = MV[l][:, c, :] if v else MK[l][:, c, :]
                    nc.scalar.activation(dst, bank(b, 0, 256), ACT.Copy).then_inc(ph.free, 1)

            def first_mem_unit():
                mem_copies(0)
                hi_split(2)

            norm("mix0", None, None, free=[], parts="root", after_root=lambda: hi_unit(ph, 0, 1),
                 beside=lambda k: first_mem_unit() if k == 4 else None)
            for u in range(1, 4):
                hi_split(u + 2)
                mem_copies(u)
            for n, dst in enumerate((C32, S32, C16, S16)):
                act.wait_ge(angle_ready, n + 1)
                nc.scalar.activation(dst[:], T[:, 3 + n, :], ACT.Sin).then_inc(tables_ready, 1)

            ph = PH["a_in"]
            for c in range(2):
                act.wait_ge(ph.done, c + 1)
                nc.scalar.activation(CKV[:, c, :], bank(c), ACT.Copy).then_inc(ph.free, 1)
            act.wait_ge(tables_ready, 6)
            ckv_norm = dict(src=lambda k: CKV[:, k, :], ready=lambda k: [(ph.free, 2)], free=[], dst=(CH, CL),
                            width=KV_RANK, root_free=[(ph.free, 4)])
            norm("ckv", parts="squares", **ckv_norm)
            hi_split(ph.split + 2)
            act.wait_ge(ph.done, 3)
            nc.scalar.activation(PICK[:, 0, :], bank(2), ACT.Copy).then_inc(misc_ready, 1)
            hi_split(ph.split + 3)
            norm("ckv", parts="root", **ckv_norm)
            act.wait_ge(misc_turned, 1)
            nc.scalar.activation(WIDX[:], bank(5).rearrange("p (t h) -> p t h", h=P)[:, :, 32:48], ACT.Copy,
                                 scale=1.0 / 32).then_inc(qkv_ready, 1)
            for u in range(4, 7):
                hi_split(ph.split + u)

            hi_split(ph.split + 7)
            n = 0
            for t in range(1, ROWT):
                W = (t + 1) * P
                for h in range(IDX_HEADS):
                    act.wait_ge(idx_done, n + 1)
                    if n >= 2:
                        act.wait_ge(idx_summed, n - 1)
                    nc.scalar.activation(T[:, n % 2, 0:W], bank(4 + n % 3, 0, W), ACT.Relu).then_inc(relu_ready, 1)
                    for tile in range(finished(FILL_IDX, n - 1) if n else 0, finished(FILL_IDX, n)):
                        if tile % 2:
                            hi_split(ph.split + 8 + tile // 2)
                    n += 1
            for c in range(2):
                act.wait_ge(ph.done, ph.before(10) + c + 1)
                nc.scalar.activation(QM[:, c, :], bank(c), ACT.Copy).then_inc(qkv_ready, 1)
            hi_split(ph.split + 12)

            uk, uv = PH["uk"], PH["uv"]
            for h in range(8):
                act.wait_ge(uk.done, h + 1)
                nc.scalar.activation(AK[:, h, :], bank(h % 4), ACT.Copy).then_inc(uk.free, 1)
                act.wait_ge(uk.free, h + 1)
                nc.scalar.activation(AK[0:32, h, :], KROPE[0:32, :], ACT.Copy).then_inc(qkv_ready, 1)
            act.wait_ge(qkv_ready, 11)
            for n in range(8):
                act.wait_ge(uv.done, n + 1)
                nc.scalar.activation(AV[:, n // 2, (n % 2) * S:(n % 2 + 1) * S], bank(n % 4), ACT.Copy).then_inc(uv.free, 1)
            attend(a_all, lambda k: hi_unit(PH["a_out"], 0, 0) if k == 30 else None)
            stream_only(PH["a_out"])

            def load_mod(u):
                act.dma_start(MODW[u % 2][:], wdram["mod"][u].rearrange("p (c n) -> p c n", c=2)).then_inc(
                    mod_landed[u % 2], 16)

            def ffn(l, first):
                for h in range(2):
                    name = f"dn{l}{h}"
                    mod = 8 * MOD_PHASES.index(name) if name in MOD_PHASES else None
                    if mod is not None:
                        if mod:
                            act.wait_ge(mod_used, mod)
                        load_mod(mod)
                        load_mod(mod + 1)
                    ffn_up(PH[f"up{l}{h}"], first + h * HALF)
                    if mod is None:
                        stream_only(PH[name])
                        continue
                    for u in range(8):
                        next_hi(PH[name], u // 2, u % 2)
                        if 2 <= u + 1 < 8:
                            act.wait_ge(mod_used, mod + u)
                            load_mod(mod + u + 1)

            norm("ffn0", lambda k: XT[:, k, :], lambda k: [(PH["a_out"].free, k + 1)], free=[(PH["a_out"].done, 8)], after_root=second_unit("up00"))
            act.dma_start(COND[:], cond_d.partition_broadcast(P)).then_inc(load_cond, 16)
            act.wait_ge(load_cond, 16)
            nc.scalar.activation(COND[:], COND[:], ACT.Silu).then_inc(cond_ready, 1)
            ffn(0, 0)
            norm("mix1", lambda k: XT[:, k, :], lambda k: [(PH["dn01"].free, k + 1)], free=[(PH["up01"].done, 22)], after_root=second_unit("b_in"))

            ph = PH["b_in"]
            for u in range(3):
                next_hi(ph, u // 2, u % 2)
                if u == 1:
                    for t in range(ROWT):
                        act.wait_ge(ph.done, ph.before(1) + t + 1)
                        nc.scalar.activation(BV[:, t, :], bank(4 + t, 0, 256), ACT.Copy).then_inc(qkv_ready, 1)
            hi_split(ph.split + 4)

            def b_between(k):
                for tile in range(min(finished(FILL_B, k - 1) if k else 0, 8), min(finished(FILL_B, k), 8)):
                    if tile >= 6:
                        act.wait_ge(ph.done, ph.before(6) + tile - 5)
                        nc.scalar.activation(QM[:, tile - 6, :], bank(tile - 6), ACT.Copy).then_inc(qkv_ready, 1)
                    if tile % 2 and tile < 6:
                        hi_split(ph.split + 5 + tile // 2)
            attend(b_all, b_between)
            stream_only(PH["b_out"])
            norm("ffn1", lambda k: XT[:, k, :], lambda k: [(PH["b_out"].free, k + 1)], free=[(PH["b_out"].done, 8)], after_root=second_unit("up10"))
            ffn(1, 22)

            act.wait_ge(o_ready, flushed(bm_range))
            act.dma_start(AXC[:], axial_d[:, 0, :]).then_inc(load_tab, 16)
            act.dma_start(AXS[:], axial_d[:, 1, :]).then_inc(load_tab, 16)
            act.wait_ge(PH["dn11"].done, 8)
            act.dma_start(CTXT[:], ctx_d).then_inc(load_ctx, 16)
            norm("final", lambda k: XT[:, k, :], lambda k: [(PH["dn11"].free, k + 1)])
            norm("ctx", lambda k: CTXT[:, k, :], lambda k: [(load_ctx, 16), (x_ready, 8)], free=[])
            ph = PH["ctx"]
            next_hi(ph, 0, 0)
            act.wait_ge(ph.done, 1)
            nc.scalar.activation(CKX[:], bank(0, 0, MEM), ACT.Copy).then_inc(ph.free, 1)
            for t in range(2):
                act.wait_ge(ph.done, t + 2)
                nc.scalar.activation(CVX[:, t, :], bank(1 + t, 0, P), ACT.Copy).then_inc(ph.free, 1)
            norm("pre1", lambda k: XT[:, k, :], lambda k: [(x_ready, XR["final"] + k + 1)], free=[(ph.done, 3)], after_root=second_unit("c_in"))

            ph = PH["c_in"]
            for u in range(3):
                next_hi(ph, u // 2, u % 2)
                if u == 2:
                    for t in range(ROWT):
                        act.wait_ge(ph.done, ph.before(2) + t + 2)
                        nc.scalar.activation(CV[:, t, :], bank(4 + t, 0, P), ACT.Copy).then_inc(qkv_ready, 1)
            hi_split(ph.split + 4)
            act.wait_ge(ph.free, 5)
            act.dma_start(DFT[:], rows_d).then_inc(load_tab, 16)

            def c_between(k):
                for tile in range(finished(FILL_C, k - 1) if k else 0, finished(FILL_C, k)):
                    act.wait_ge(ph.done, ph.before(3) + tile + 1)
                    if tile < 4:
                        dst = FT[:, tile, :]
                    else:
                        dst = (GA if tile < 12 else GF)[:, (tile - 4) % 8, :]
                    nc.scalar.activation(dst, bank(tile % 2), ACT.Copy).then_inc(ph.free, 1)
                    if tile % 2 and tile // 2 < 9:
                        hi_split(ph.split + 5 + tile // 2)
            attend(c_range, c_between)
            c_between(32)
            act.wait_ge(ph.free, ph.total - 4)
            def by_channel(g):
                for t2 in range(2):
                    act.wait_ge(f1_done, 2 * g + t2 + 1)
                    if g >= 2:
                        act.wait_ge(f2_done, g - 1)
                    nc.scalar.activation(F1[g % 2][:, 2 * t2:2 * t2 + 2, :],
                                         bank(t2).rearrange("p (t n) -> p t n", t=2), ACT.Copy).then_inc(f1_ready, 1)

            by_channel(0)
            for g in range(4):
                if g < 3:
                    by_channel(g + 1)
                if g in (1, 2):
                    gate = (GA, GF)[g - 1]
                    nc.scalar.activation(gate[:], gate[:], ACT.Sigmoid).then_inc(gates_ready, 1)
                act.wait_ge(f2_done, g + 1)
                nc.scalar.activation(HH[:, 4 + g, :], bank(2 + g % 2), ACT.Copy).then_inc(f2_hi, 1)

            ph = PH["merge"]
            for u in range(4):
                next_hi(ph, u // 2, u % 2)
                for c in range(2):
                    m = 2 * u + c
                    act.wait_ge(m_ready, m + 1)
                    nc.scalar.activation(MH[:, m, :], T[:, 4 + m % 2, :], ACT.Copy).then_inc(m_hi, 1)
            stream_only(PH["c_out"])
            norm("post1", lambda k: Y[:, k, :], lambda k: [(PH["c_out"].free, k + 1)])
            norm("pre2", lambda k: XT[:, k, :], lambda k: [(x_ready, XR["post1"] + k + 1)], free=[(PH["c_out"].done, 8)], after_root=second_unit("up20"))
            ffn(2, 44)
            norm("post2", lambda k: Y2[:, k, :], lambda k: [(PH["dn21"].free, k + 1)])

        @block.vector
        def _(v):
            chain = Chain(v, vec_steps)
            step = chain.step

            def norm(name, src, gain, shift=None, dst=(HH, HL), into=None):
                i, nch, rows, b, s = NORMS[name]
                v.wait_ge(root_ready, i + 1)
                step(nc.vector.reciprocal(T[:, 3, 0:rows], T[:, 2, 0:rows]))

                def low(k):
                    v.wait_ge(h_hi_ready, s + k + 1)
                    nc.vector.tensor_tensor(dst[1][:, k, 0:rows], T[:, 4 + k % 2, 0:rows],
                                            dst[0][:, k, 0:rows].bitcast(F32), ALU.subtract).then_inc(h_ready, 1)

                for k in range(nch):
                    if into is not None:
                        out = src(k) if into == "self" else T[:, 4 + k % 2, 0:rows]
                        ins = nc.vector.scalar_tensor_tensor(out=out, in0=src(k), scalar=gain(k), in1=T[:, 3, 0:rows],
                                                             op0=ALU.mult, op1=ALU.mult)
                        if into == "self":
                            ins.then_inc(x_ready, 1)
                        else:
                            step(ins)
                            nc.vector.tensor_tensor(XT[:, k, :], XT[:, k, :], out, ALU.add).then_inc(x_ready, 1)
                        continue
                    t = T[:, 4 + k % 2, 0:rows]
                    if k >= 2:
                        v.wait_ge(h_ready, s + k - 1)
                    ins = nc.vector.scalar_tensor_tensor(out=t, in0=src(k), scalar=gain(k), in1=T[:, 3, 0:rows],
                                                         op0=ALU.mult, op1=ALU.mult)
                    if shift is not None:
                        step(ins)
                        ins = nc.vector.tensor_scalar(t, t, shift(k), None, ALU.add)
                    ins.then_inc(scaled_ready, 1)
                    if k >= 1:
                        low(k - 1)
                if into is None:
                    low(nch - 1)

            ropes = []

            def rope(src, dst, cos, sin, half, done, count, n=P, swapped=None):
                sw = T[0:n, 2 + len(ropes) % 2, :] if swapped is None else swapped[0:n, len(ropes) % 2, :]
                if len(ropes) >= 2:
                    v.wait_ge(*ropes[-2])
                ropes.append((done, count))
                mask = [i + half if i < half else i - half if i < 2 * half else i for i in range(32)]
                if half == 16:
                    mask = [(i + 16) % 32 for i in range(32)]
                step(nc.vector.stream_shuffle(sw, src, mask))
                step(nc.vector.tensor_tensor(sw, sw, sin[0:n, :], ALU.mult))
                step(nc.vector.tensor_tensor(dst, src, cos[0:n, :], ALU.mult))
                nc.vector.tensor_tensor(dst, dst, sw, ALU.add).then_inc(done, 1)

            def attend(rng, between=None):
                lo, hi = rng

                def maxes(s):
                    st, W = steps[s], steps[s]["nk"]
                    v.wait_ge(scores_done, s + 1)
                    if s >= 2:
                        v.wait_ge(p_ready, s - 1)
                    if s >= 3:
                        v.wait_ge(turned_done, s - 2)
                    o = ST[:, s % 2, :]
                    for n in range(st["nh"]):
                        src = ps[:, scores_at(s, n):scores_at(s, n) + W]
                        if st["mask"] is None:
                            ins = nc.vector.tensor_reduce(o[:, n:n + 1], src, AX.X, ALU.max)
                        else:
                            ins = nc.vector.tensor_tensor_reduce(
                                TW[:, probs_at(s) + n * W:probs_at(s) + (n + 1) * W], src, st["mask"], 1.0, PICKED,
                                ALU.add, ALU.max, o[:, n:n + 1])
                    step(ins)
                    nh = st["nh"]
                    if st["sink"] is None:
                        nc.vector.tensor_scalar(o[:, 2:2 + nh], o[:, 0:nh], -st["scale"], None, ALU.mult).then_inc(max_ready, 1)
                    else:
                        step(nc.vector.scalar_tensor_tensor(out=o[:, 8:8 + nh], in0=o[:, 0:nh], scalar=st["scale"],
                                                            in1=st["sink"], op0=ALU.mult, op1=ALU.max))
                        nc.vector.tensor_scalar(o[:, 2:2 + nh], o[:, 8:8 + nh], -1.0, None, ALU.mult).then_inc(max_ready, 1)

                def probs(s):
                    st, W = steps[s], steps[s]["nk"]
                    nh, o = st["nh"], ST[:, s % 2, :]
                    v.wait_ge(exp_done, s + 1)
                    if st["sink"] is not None:
                        step(nc.vector.tensor_tensor(o[:, 4:4 + nh], o[:, 4:4 + nh], o[:, 6:6 + nh], ALU.add))
                    step(nc.vector.reciprocal(o[:, 10:10 + nh], o[:, 4:4 + nh]))
                    for n in range(nh):
                        sm = TW[:, probs_at(s) + n * W:probs_at(s) + (n + 1) * W]
                        ins = nc.vector.tensor_scalar(sm, sm, o[:, 10 + n:11 + n], None, ALU.mult)
                    ins.then_inc(p_ready, 1)

                def flush(s):
                    f = steps[s]["flush"]
                    v.wait_ge(o_hi_ready, f + 1)
                    hi_part, out = flushes[f]
                    src = bank(7) if len(out.shape) == 2 else bank(7).rearrange("p (h n) -> p h n", h=4)
                    nc.vector.tensor_tensor(out, src, hi_part.bitcast(F32), ALU.subtract).then_inc(o_ready, 1)

                maxes(lo)
                for s in range(lo, hi):
                    if s + 1 < hi:
                        maxes(s + 1)
                    probs(s)
                    if s - 2 >= lo and steps[s - 2]["last"]:
                        flush(s - 2)
                    if between:
                        between(s - lo)
                for s in range(hi - 2, hi):
                    if steps[s]["last"]:
                        flush(s)

            def mod_unit(u):
                if u == 0:
                    v.wait_ge(cond_ready, 1)
                v.wait_ge(mod_landed[u % 2], 16 * (u // 2 + 1))
                for c in range(2):
                    for w in range(2 if u < 8 else 1):
                        ins = nc.vector.tensor_tensor_reduce(TW[:, 4 * S:4 * S + D], MODW[u % 2][:, c, :], COND[:, w, :],
                                                             1.0, 0.0, ALU.mult, ALU.add, MODV[:, 2 * u + c, w:w + 1])
                        if c == 1 and (w == 1 or u >= 8):
                            ins.then_inc(mod_used, 1)
                            v.wait_ge(mod_used, u + 1)
                        else:
                            step(ins)

            def sum_square(c, chunk, j):
                sq = nc.vector.tensor_tensor(T[:, j, :], chunk, chunk, ALU.mult)
                if isinstance(c, int) and c == DC - 1:
                    sq.then_inc(square_ready, 1)
                    return
                step(sq)
                if isinstance(c, int) and c == 0:
                    step(nc.vector.tensor_copy(T[:, 3, :], T[:, j, :]))
                    return
                ins = nc.vector.tensor_tensor(T[:, 3, :], T[:, 3, :], T[:, j, :], ALU.add)
                if isinstance(c, int) and c == DC - 2:
                    ins.then_inc(sum_ready, 1)
                else:
                    step(ins)

            def residual(ph, dst, mode, squares=True):
                def body(i, j):
                    v.wait_ge(ph.done, 2 * i + j + 1)
                    c = 2 * i + j
                    d = dst[:, c, :] if isinstance(c, int) else dst[:, bass.ds(c, 1), :].rearrange("p a n -> p (a n)")
                    if mode == "add":
                        nc.vector.tensor_tensor(d, bank(j), d, ALU.add).then_inc(ph.free, 1)
                    else:
                        nc.vector.tensor_scalar(d, bank(j), 1.0, None, ALU.mult).then_inc(ph.free, 1)
                    if squares:
                        v.wait_ge(ph.free, 2 * i + (j + 1))
                        sum_square(c, d, j)
                if ph.name in MOD_PHASES:
                    for u in range(ph.n):
                        body(u // 2, u % 2)
                        mod_unit(8 * MOD_PHASES.index(ph.name) + u)
                    return
                each_unit(v, ph.n, body, chain if squares else None)

            def ffn_up(ph, l, h, first, before):
                taps = [(0, 2), (1, 1), (2, 0)] if l < 2 else [(0, 1), (1, 0), (2, -1)]
                col = PCOL[f"conv{l}"] + 4 * h * HALF
                for w in before:
                    v.wait_ge(*w)

                def body(i, j):
                    u = 2 * i + j

                    def w(tap):
                        if isinstance(u, int):
                            return PRM[:, col + 4 * u + tap:col + 4 * u + tap + 1]
                        return PRM[:, bass.ds(u * 4 + (col + tap), 1)]

                    def chunk(buf):
                        return buf[:, u, :] if isinstance(u, int) else buf[:, bass.ds(u, 1), :].rearrange("p a n -> p (a n)")

                    a, b, t = bank(2 * j), bank(2 * j + 1), T[:, j, :]
                    mid = next(k for k, sft in taps if sft == 0)
                    v.wait_ge(ph.done, 2 * u + 1)
                    step(nc.vector.tensor_scalar(t, a, w(mid), w(3), ALU.mult, ALU.add))
                    rest = [x for x in taps if x[1] != 0]
                    for k, sft in rest:
                        o, s_ = (slice(sft, S), slice(0, S - sft)) if sft > 0 else (slice(0, S + sft), slice(-sft, S))
                        ins = nc.vector.scalar_tensor_tensor(out=t[:, o], in0=a[:, s_], scalar=w(k), in1=t[:, o],
                                                             op0=ALU.mult, op1=ALU.add)
                        if k == rest[-1][0]:
                            ins.then_inc(conv_ready, 1)
                        else:
                            step(ins)
                    v.wait_ge(ph.done, 2 * u + 2)
                    v.wait_ge(silu_ready, 2 * i + (j + 1 + first))
                    g = T[:, 4 + j, :]
                    nc.vector.tensor_tensor(g, b, T[:, 2 + j, :], ALU.mult).then_inc(ph.free, 1)
                    v.wait_ge(ph.free, u + 1)
                    step(nc.vector.tensor_scalar(chunk(GH), g, 1.0, None, ALU.mult))
                    nc.vector.tensor_tensor(chunk(GL), g, chunk(GH).bitcast(F32), ALU.subtract).then_inc(g_ready, 1)
                each_unit(v, ph.n, body, chain)

            def ffn(l, dst, modes):
                for h in range(2):
                    if l == 1 and h == 1:
                        derive()
                    before = [(PH[f"dn{l}0"].done, 8)] if h else []
                    ffn_up(PH[f"up{l}{h}"], l, h, (2 * l + h) * HALF, before)
                    residual(PH[f"dn{l}{h}"], dst, modes[h], squares=h == 1)

            norm("mem", lambda k: MEMT[:, k, :], lambda k: par("g_mem", k), dst=(MEMH, MEML))
            norm("mix0", lambda k: XT[:, k, :], lambda k: par("g_mix", k))

            TWO_PI = 2 * math.pi
            C1 = 6.28125
            C2 = float(np.float32(round((TWO_PI - C1) * 2 ** 20) / 2 ** 20))
            C3 = TWO_PI - C1 - C2
            MAGIC = 1.5 * 2 ** 23
            PI = 3.1415925
            v.wait_ge(h_ready, 16)
            step(nc.vector.tensor_copy(T[:, 0, :], POS[:]))
            for n, (name, quarter) in enumerate((("32", True), ("32", False), ("16", True), ("16", False))):
                ang, turns, red = T[:, 1, :], T[:, 2, :], T[:, 3 + n, :]
                step(nc.vector.tensor_scalar(ang, T[:, 0, :], cst("inv" + name), None, ALU.mult))
                step(nc.vector.tensor_scalar(turns, ang, 1 / TWO_PI, 0.25 if quarter else 0.0, ALU.mult, ALU.add))
                step(nc.vector.tensor_scalar(turns, turns, MAGIC, None, ALU.add))
                step(nc.vector.tensor_scalar(turns, turns, MAGIC, None, ALU.subtract))
                for k, c in enumerate((C1, C2, C3)):
                    step(nc.vector.scalar_tensor_tensor(out=red, in0=turns, scalar=-c, in1=red if k else ang,
                                                        op0=ALU.mult, op1=ALU.add))
                if quarter:
                    step(nc.vector.tensor_scalar(red, red, math.pi / 2, None, ALU.add))
                nc.vector.tensor_scalar(red, red, PI, -PI, ALU.min, ALU.max).then_inc(angle_ready, 1)
            v.wait_ge(tables_ready, 4)
            for k, (tab, name) in enumerate(((S32, "32"), (S16, "16"))):
                nc.vector.tensor_scalar(tab[:], tab[:], cst("sgn" + name), None, ALU.mult).then_inc(tables_ready, 1)
            v.wait_ge(tables_ready, 6)

            ph = PH["a_in"]
            v.wait_ge(ph.free, 2)
            v.wait_ge(ph.done, ph.before(1) + 1)
            v.wait_ge(misc_ready, 1)
            rope(bank(2)[0:32, :], KROPE[0:32, :], C32, S32, 16, ph.free, 3, 32)
            v.wait_ge(ph.done, ph.before(1) + 2)
            rope(bank(3), KIDX[:], C16, S16, 8, ph.free, 4)
            v.wait_ge(ph.free, 4)
            norm("ckv", lambda k: CKV[:, k, :], lambda k: par("kv_norm", k), dst=(CH, CL))
            v.wait_ge(h_ready, NORMS["ckv"][4] + 2)

            def q_unit(u, dst, n, cos, sin, half):
                for c in range(2):
                    v.wait_ge(ph.done, ph.before(u) + c + 1)
                    rope(bank((u % 2) * 2 + c), dst[:, n + c, :], cos, sin, half, ph.free, 2 * u + c + 1)

            for u in range(2, 6):
                q_unit(u, AQI, 2 * (u - 2), C16, S16, 8)
            v.wait_ge(qkv_ready, 1)
            for t in range(1, ROWT):
                acc = PICK[:, t - 1, :]
                step(nc.vector.memset(acc[:, 0:t * P], 0.0))
                step(nc.vector.tensor_copy(acc[:, t * P:(t + 1) * P], cst("le", P)))

            def pick_eight(t, last):
                acc = PICK[:, t - 1, 0:(t + 1) * P]
                step(nc.vector.max(M8[:], acc))
                step(nc.vector.match_replace(acc, M8[:], acc, PICKED))
                if last:
                    step(nc.vector.tensor_scalar(acc, acc, PICKED / 2, NEG, ALU.is_gt, ALU.mult))

            def q_rope(tile):
                u, c = 6 + tile // 2, tile % 2
                v.wait_ge(ph.done, ph.before(u) + c + 1)
                rope(bank((u % 2) * 2 + c), AQ[:, tile, :], C32, S32, 16, ph.free, 2 * u + c + 1)

            v.wait_ge(qkv_ready, 1)
            n = 0
            for t in range(1, ROWT):
                W = (t + 1) * P
                acc = PICK[:, t - 1, 0:W]
                for h in range(IDX_HEADS):
                    v.wait_ge(relu_ready, n + 1)
                    nc.vector.scalar_tensor_tensor(out=acc, in0=T[:, n % 2, 0:W], scalar=WIDX[:, t, h:h + 1], in1=acc,
                                                   op0=ALU.mult, op1=ALU.add).then_inc(idx_summed, 1)
                    v.wait_ge(idx_summed, n + 1)
                    if t > 1:
                        pick_eight(t - 1, h == TOPK // 8 - 1)
                    for tile in range(min(finished(FILL_IDX, n - 1) if n else 0, 8), min(finished(FILL_IDX, n), 8)):
                        q_rope(tile)
                    n += 1
            for h in range(TOPK // 8):
                pick_eight(ROWT - 1, h == TOPK // 8 - 1)
            attend(a_all)

            def derive():
                step(nc.vector.tensor_tensor(MODV[:, :, 0], MODV[:, :, 0], par("b_mod", 0, 48), ALU.add))
                step(nc.vector.tensor_tensor(MODV[:, 0:16, 1], MODV[:, 0:16, 1], par("b_mod", 0, 16), ALU.add))
                for n, (g, col, w, one) in enumerate((("g_pre1", 8, 0, 1), ("g_pre1", 8, 1, 1), ("g_post1", 16, 0, 0),
                                                      ("g_pre2", 32, 0, 1), ("g_post2", 40, 0, 0))):
                    step(nc.vector.scalar_tensor_tensor(out=DER[:, n, :], in0=MODV[:, col:col + 8, w], scalar=float(one),
                                                        in1=par(g, 0, 8), op0=ALU.add, op1=ALU.mult))

            residual(PH["a_out"], XT, "add")

            norm("ffn0", lambda k: XT[:, k, :], lambda k: par("g_ffn", k))
            ffn(0, XT, ("add", "add"))
            norm("mix1", lambda k: XT[:, k, :], lambda k: par("g_mix", 8 + k))

            ph = PH["b_in"]

            def b_tile(u, c, dst, count):
                v.wait_ge(ph.done, ph.before(u) + c + 1)
                rope(bank((u % 2) * 2 + c if u < 3 else c), dst, C16, S16, 8, ph.free, count, swapped=BSW)

            for c in range(2):
                b_tile(0, c, BK[:, c, :], c + 1)
            for c in range(2):
                b_tile(2, c, BQ[:, c, :], c + 3)

            def b_between(k):
                for tile in range(min(finished(FILL_B, k - 1) if k else 0, 6), min(finished(FILL_B, k), 6)):
                    b_tile(3 + tile // 2, tile % 2, BQ[:, 2 + tile, :], 5 + tile)
            attend(b_all, b_between)
            residual(PH["b_out"], XT, "add")
            norm("ffn1", lambda k: XT[:, k, :], lambda k: par("g_ffn", 8 + k))
            ffn(1, XT, ("add", "add"))

            norm("final", lambda k: XT[:, k, :], lambda k: par("g_final", k), into="self")
            norm("ctx", lambda k: CTXT[:, k, :], lambda k: DER[:, 1, k:k + 1], shift=lambda k: MODV[:, k, 1:2])
            norm("pre1", lambda k: XT[:, k, :], lambda k: DER[:, 0, k:k + 1], shift=lambda k: MODV[:, k, 0:1])
            ph = PH["c_in"]
            v.wait_ge(load_tab, 32)
            for u in range(2):
                q_unit(u, CQ, 2 * u, AXC, AXS, 16)
            v.wait_ge(ph.done, ph.before(2) + 1)
            rope(bank(0), CK[:], AXC, AXS, 16, ph.free, 5)
            attend(c_range)
            for g in range(4):
                v.wait_ge(f2_hi, g + 1)
                nc.vector.tensor_tensor(HL[:, 4 + g, :], bank(2 + g % 2), HH[:, 4 + g, :].bitcast(F32),
                                        ALU.subtract).then_inc(four_ready, 1)
            ph = PH["merge"]
            for u in range(4):
                for c in range(2):
                    m = 2 * u + c
                    v.wait_ge(gates_ready, 2)
                    v.wait_ge(ph.done, 4 * u + c + 1)
                    step(nc.vector.tensor_tensor(T[:, c, :], bank(c), GA[:, m, :], ALU.mult))
                    v.wait_ge(ph.done, 4 * u + c + 3)
                    step(nc.vector.tensor_tensor(T[:, 2 + c, :], bank(2 + c), GF[:, m, :], ALU.mult))
                    t = T[:, 4 + m % 2, :]
                    nc.vector.tensor_tensor(t, T[:, c, :], T[:, 2 + c, :], ALU.add).then_inc(m_ready, 1)
                    v.wait_ge(m_hi, m + 1)
                    nc.vector.tensor_tensor(ML[:, m, :], t, MH[:, m, :].bitcast(F32), ALU.subtract).then_inc(m_lo, 1)
            ph = PH["c_out"]
            for u in range(4):
                for c in range(2):
                    v.wait_ge(ph.done, 2 * u + c + 1)
                    nc.vector.tensor_copy(Y[:, 2 * u + c, :], bank((u % 2) * 2 + c)).then_inc(ph.free, 1)
                    v.wait_ge(ph.free, 2 * u + c + 1)
                    sum_square(2 * u + c, Y[:, 2 * u + c, :], c)
            norm("post1", lambda k: Y[:, k, :], lambda k: DER[:, 2, k:k + 1], into="x")
            norm("pre2", lambda k: XT[:, k, :], lambda k: DER[:, 3, k:k + 1], shift=lambda k: MODV[:, 24 + k, 0:1])
            ffn(2, Y2, ("copy", "add"))
            norm("post2", lambda k: Y2[:, k, :], lambda k: DER[:, 4, k:k + 1], into="x")

        @block.tensor
        def _(pe):
            last_read = {}

            def bank_free(b):
                if b in last_read:
                    pe.wait_ge(*last_read[b])

            def products(out, pairs, done=None):
                n = len(pairs)
                for k, (wh, wl, ah, al, swap, ready) in enumerate(pairs):
                    if ready is not None:
                        pe.wait_ge(*ready)
                    for m, (w, a) in enumerate(((wh, ah), (wh, al), (wl, ah))):
                        l, r = (a, w) if swap else (w, a)
                        ins = nc.tensor.matmul(out, l, r, start=(k == 0 and m == 0), stop=(k == n - 1 and m == 2))
                        if k == n - 1 and m == 2 and done is not None:
                            ins.then_inc(done, 1)
                        yield

            def advance(work, count=None):
                while count is None or count > 0:
                    if next(work, True):
                        return
                    count = count and count - 1

            def side_by_side(tiles, kc, act_of, ready, done):
                for _, _, b in tiles:
                    bank_free(b)
                for k in range(kc):
                    pe.wait_ge(*ready(k))
                    ah, al = act_of(k)
                    for out, weights, _ in tiles:
                        wh, wl = weights(k)
                        for m, (w, a) in enumerate(((wh, ah), (wh, al), (wl, ah))):
                            ins = nc.tensor.matmul(out, w, a, start=(k == 0 and m == 0), stop=(k == kc - 1 and m == 2))
                            if k == kc - 1 and m == 2:
                                ins.then_inc(done, 1)
                            yield

            def gemm(ph, kc, width, act_hi, act_lo, rows=S, ready=None, first8=None):
                t = ph.tiles
                period = 2 * t

                def body(i, j):
                    u = 2 * i + j
                    slot = (ph.split + j) % 2
                    pe.wait_ge(lo_ready, 2 * i + (j + ph.split + 1))
                    if ready is not None and t > 1 and isinstance(u, int) and u == 0:
                        advance(side_by_side([(bank(c, 0, rows), lambda k, c=c: (
                            HI[slot][:, k * width + c * P:k * width + (c + 1) * P],
                            LO[slot][:, k * width + c * P:k * width + (c + 1) * P]), c) for c in range(t)],
                            kc, lambda k: (act_hi[:, k, 0:rows], act_lo[:, k, 0:rows]), ready, ph.done))
                        return
                    for c in range(t):
                        b = j * t + c
                        if isinstance(i, int) and i == 0:
                            bank_free(b)
                        elif ph.name.startswith("up"):
                            pe.wait_ge(ph.free, u - 1)
                        else:
                            pe.wait_ge(ph.free, u * t + (c + 1 - period))
                        advance(products(bank(b, 0, rows), [
                            (HI[slot][:, k * width + c * P:k * width + (c + 1) * P],
                             LO[slot][:, k * width + c * P:k * width + (c + 1) * P],
                             (first8[0] if first8 and k < 8 else act_hi)[:, k, 0:rows],
                             (first8[1] if first8 and k < 8 else act_lo)[:, k, 0:rows], False,
                             ready(k) if ready is not None and isinstance(u, int) and u == 0 and c == 0 else None)
                            for k in range(kc)], ph.done))
                each_unit(pe, ph.n, body)
                for u in range(max(0, ph.n - 2), ph.n):
                    for c in range(t):
                        last_read[(u % 2) * t + c] = (ph.free, u + 1 if ph.name.startswith("up") else u * t + c + 1)

            def t_tiles(ph, u, cs, bs, width=256, rows=S, ah=HH, al=HL, kc=DC, ready=None):
                slot = (ph.split + u) % 2
                if ready:
                    yield from side_by_side([(bank(b, 0, rows), lambda k, c=c: (
                        HI[slot][:, k * width + c * P:k * width + (c + 1) * P],
                        LO[slot][:, k * width + c * P:k * width + (c + 1) * P]), b) for c, b in zip(cs, bs)],
                        kc, lambda k: (ah[:, k, 0:rows], al[:, k, 0:rows]), ready, ph.done)
                    return
                for n, (c, b) in enumerate(zip(cs, bs)):
                    bank_free(b)
                    yield from products(bank(b, 0, rows), [
                        (HI[slot][:, k * width + c * P:k * width + (c + 1) * P],
                         LO[slot][:, k * width + c * P:k * width + (c + 1) * P], ah[:, k, 0:rows], al[:, k, 0:rows],
                         False, None) for k in range(kc)], ph.done)

            def r_tiles(ph, u, rts, bs, lo, n, width=256, kc=DC, ah=HH, al=HL):
                slot = (ph.split + u) % 2
                for rt, b in zip(rts, bs):
                    bank_free(b)
                    yield from products(bank(b, 0, n), [
                        (HI[slot][:, k * width + lo:k * width + lo + n], LO[slot][:, k * width + lo:k * width + lo + n],
                         ah[:, k, rt * P:(rt + 1) * P], al[:, k, rt * P:(rt + 1) * P], True, None)
                        for k in range(kc)], ph.done)

            def unit_ready(ph, u):
                pe.wait_ge(lo_ready, ph.split + u + 1)

            def norm(name):
                i, nch, rows, b, s = NORMS[name]
                bank_free(4)
                if name in SPREAD:
                    pe.wait_ge(sum_ready, SPREAD.index(name) + 1)
                    nc.tensor.matmul(bank(4), ONES[:], T[:, 3, :], start=True, stop=False)
                    pe.wait_ge(square_ready, b + 1)
                    nc.tensor.matmul(bank(4), ONES[:], T[:, 1, :], start=False, stop=True).then_inc(square_used, 1)
                for k in range(0 if name in SPREAD else nch):
                    pe.wait_ge(square_ready, b + k + 1)
                    nc.tensor.matmul(bank(4, 0, rows), ONES[:], T[:, k % 2, 0:rows], start=(k == 0),
                                     stop=(k == nch - 1)).then_inc(square_used, 1)
                last_read[4] = (root_ready, i + 1)

            def h_chunk(name):
                s = NORMS[name][4]
                return lambda k: (h_ready, s + k + 1)

            def attend(rng, between=None):
                lo, hi = rng

                def scores(s):
                    st = steps[s]
                    if s < lo + 2:
                        for b in (2, 3):
                            bank_free(b + 2 * (s % 2))
                    else:
                        pe.wait_ge(exp_done if steps[s - 2]["mask"] is None else max_ready, s - 1)
                        if s - 2 >= c_range[0]:
                            pe.wait_ge(turned_ready, s - 2)
                    for off, q, k in st["qk"]:
                        n = k.shape[-1]
                        ins = nc.tensor.matmul(ps[:, scores_at(s, 0) + off:scores_at(s, 0) + off + n], q, k,
                                               start=True, stop=True)
                    ins.then_inc(scores_done, 1)

                def turn(s):
                    st = steps[s]
                    pe.wait_ge(p_ready, s + 1)
                    if s > lo:
                        pe.wait_ge(turned_ready, s)
                    else:
                        bank_free(6)
                    for n in range(st["nk"] * st["nh"] // P):
                        a0 = 6 * S + n * P if n < 4 else scores_at(s, 1) + S - P
                        ins = nc.tensor.transpose(ps[:, a0:a0 + P], TW[:, probs_at(s) + n * P:probs_at(s) + (n + 1) * P],
                                                  cst("ident", P))
                    ins.then_inc(turned_done, 1)

                def values(s):
                    st = steps[s]
                    f = st["flush"]
                    pe.wait_ge(turned_ready, s + 1)
                    if st["first"]:
                        if s > lo:
                            pe.wait_ge(o_ready, f)
                        else:
                            bank_free(7)
                    kb_n = st["nk"] // P
                    for n in range(st["nh"]):
                        p0, m, col = st["out"][n]
                        for b in range(kb_n):
                            c0 = turned_at(s) + (n * kb_n + b) * P
                            ins = nc.tensor.matmul(ps[p0:p0 + m, 7 * S + col * P:7 * S + (col + 1) * P],
                                                   st["pv"][n][b], TW[:, c0:c0 + P], start=(b == 0), stop=(b == kb_n - 1))
                    ins.then_inc(pv_done, 1)

                scores(lo)
                scores(lo + 1)
                for s in range(lo, hi):
                    if between:
                        between(s - lo, True)
                    if s + 2 < hi:
                        scores(s + 2)
                    turn(s)
                    if s > lo:
                        values(s - 1)
                    if between:
                        between(s - lo, False)
                values(hi - 1)
                for b in range(2, 6):
                    last_read[b] = (exp_done, hi)
                last_read[6] = (turned_ready, hi)
                last_read[7] = (o_ready, steps[hi - 1]["flush"] + 1)

            pe.wait_ge(ones_ready, 1)
            norm("mem")
            norm("mix0")
            ph = PH["memkv"]
            for u in range(4):
                unit_ready(ph, u)
                b = (u % 2) * 2
                if u >= 2:
                    last_read[b], last_read[b + 1] = (ph.free, 2 * u - 3), (ph.free, 2 * u - 2)
                if u % 2 == 0:
                    advance(t_tiles(ph, u, (0, 1), (b, b + 1), rows=MEM, ah=MEMH, al=MEML,
                                    ready=h_chunk("mem") if u == 0 else None))
                else:
                    advance(r_tiles(ph, u, (0, 1), (b, b + 1), 0, 256, ah=MEMH, al=MEML))
            for b in range(4):
                last_read[b] = (ph.free, 5 + b)

            ph = PH["a_in"]
            for u in range(6):
                unit_ready(ph, u)
                b = (u % 2) * 2
                advance(t_tiles(ph, u, (0, 1), (b, b + 1), ready=h_chunk("mix0") if u == 0 else None))
                last_read[b], last_read[b + 1] = (ph.free, 2 * u + 1), (ph.free, 2 * u + 2)
                if u == 1:
                    norm("ckv")
                    pe.wait_ge(misc_ready, 1)
                    bank_free(5)
                    for rt in range(ROWT):
                        ins = nc.tensor.transpose(bank(5, rt * P, (rt + 1) * P), PICK[:, 0, rt * P:(rt + 1) * P],
                                                  cst("ident", P))
                    ins.then_inc(misc_turned, 1)
                    last_read[5] = (qkv_ready, 1)

            def a_rest():
                for u in range(6, 11):
                    unit_ready(ph, u)
                    b = (u % 2) * 2
                    yield from t_tiles(ph, u, (0, 1), (b, b + 1))
                    last_read[b], last_read[b + 1] = (ph.free, 2 * u + 1), (ph.free, 2 * u + 2)

            rest = a_rest()
            n = 0
            pe.wait_ge(ph.free, 12)
            for t in range(1, ROWT):
                for h in range(IDX_HEADS):
                    b = 4 + n % 3
                    if n >= 3:
                        pe.wait_ge(relu_ready, n - 2)
                    else:
                        bank_free(b)
                    j = h % 2
                    nc.tensor.matmul(bank(b, 0, (t + 1) * P), AQI[64 * j:64 * j + 64, h // 2, t * P:(t + 1) * P],
                                     KIDX[64 * j:64 * j + 64, 0:(t + 1) * P], start=True, stop=True).then_inc(idx_done, 1)
                    advance(rest, FILL_IDX)
                    n += 1
            advance(rest)
            for b in (4, 5, 6):
                last_read[b] = (relu_ready, n)
            last_read[0], last_read[1] = (qkv_ready, 2), (qkv_ready, 3)

            ph = PH["uk"]
            unit_ready(ph, 0)
            pe.wait_ge(h_ready, NORMS["ckv"][4] + 2)
            for h in range(8):
                if h >= 4:
                    last_read[h % 4] = (ph.free, h - 3)
                advance(t_tiles(ph, 0, (h,), (h % 4,), width=1024, ah=CH, al=CL, kc=2))
            for b in range(4):
                last_read[b] = (ph.free, 5 + b)
            ph = PH["uv"]
            unit_ready(ph, 0)
            for n in range(8):
                if n >= 4:
                    last_read[n % 4] = (ph.free, n - 3)
                advance(r_tiles(ph, 0, (n // 2,), (n % 4,), (n % 2) * S, S, width=1024, kc=2, ah=CH, al=CL))
            for b in range(4):
                last_read[b] = (ph.free, 5 + b)
            pe.wait_ge(ph.free, 8)
            attend(a_all)
            gemm(PH["a_out"], 10, P, HH, HL, ready=lambda k: (o_ready, flushed(am_range)))

            def ffn(l, name):
                for h in range(2):
                    gemm(PH[f"up{l}{h}"], DC, 256, HH, HL, ready=h_chunk(name) if h == 0 else None)
                    gemm(PH[f"dn{l}{h}"], HALF, P, GH, GL, ready=lambda k: (g_ready, (2 * l + h) * HALF + k + 1))

            norm("ffn0")
            ffn(0, "ffn0")
            norm("mix1")
            ph = PH["b_in"]
            for u in range(3):
                unit_ready(ph, u)
                b = (u % 2) * 2
                if u == 1:
                    last_read[4] = (root_ready, NORMS["mix1"][0] + 1)
                    advance(r_tiles(ph, u, range(4), range(4, 8), 0, 256))
                    for t in range(4):
                        last_read[4 + t] = (qkv_ready, 11 + t + 1)
                else:
                    advance(t_tiles(ph, u, (0, 1), (b, b + 1), ready=h_chunk("mix1") if u == 0 else None))
                    last_read[b], last_read[b + 1] = (ph.free, u + 1), (ph.free, u + 2)

            def b_rest():
                for u in range(3, 7):
                    unit_ready(ph, u)
                    yield from t_tiles(ph, u, (0, 1), (0, 1))
                    last_read[0], last_read[1] = (ph.free, 2 * u - 1), (ph.free, 2 * u)
                last_read[0], last_read[1] = (qkv_ready, 16), (qkv_ready, 17)

            rest = b_rest()

            def b_between(k, first):
                if first:
                    group = (k + 2) // 4
                    if k % 4 == 2 and 2 <= group < 8:
                        pe.wait_ge(ph.free, 3 + group)
                    elif k % 4 == 2 and group == 8:
                        pe.wait_ge(qkv_ready, 17)
                else:
                    advance(rest, FILL_B)
            pe.wait_ge(qkv_ready, 15)
            pe.wait_ge(ph.free, 4)
            attend(b_all, b_between)
            advance(rest)
            gemm(PH["b_out"], 10, P, HH, HL, ready=lambda k: (o_ready, flushed(bm_range)), first8=BO)
            norm("ffn1")
            ffn(1, "ffn1")

            norm("final")
            norm("ctx")
            ph = PH["ctx"]
            unit_ready(ph, 0)
            advance(t_tiles(ph, 0, (0,), (0,), rows=MEM, ready=h_chunk("ctx")))
            advance(r_tiles(ph, 0, (0, 1), (1, 2), P, P))
            for b in range(3):
                last_read[b] = (ph.free, b + 1)
            norm("pre1")
            ph = PH["c_in"]
            for u in range(3):
                unit_ready(ph, u)
                b = (u % 2) * 2
                if u == 2:
                    advance(t_tiles(ph, u, (0,), (0,)))
                    last_read[0] = (ph.free, 5)
                    last_read[4] = (root_ready, NORMS["pre1"][0] + 1)
                    advance(r_tiles(ph, u, range(4), range(4, 8), P, P))
                    for t in range(4):
                        last_read[4 + t] = (qkv_ready, 17 + t + 1)
                else:
                    advance(t_tiles(ph, u, (0, 1), (b, b + 1), ready=h_chunk("pre1") if u == 0 else None))
                    last_read[b], last_read[b + 1] = (ph.free, 2 * u + 1), (ph.free, 2 * u + 2)

            def c_rest():
                for u in range(3, 13):
                    unit_ready(ph, u)
                    yield from t_tiles(ph, u, (0, 1), (0, 1))
                    last_read[0], last_read[1] = (ph.free, 2 * u), (ph.free, 2 * u + 1)

            rest = c_rest()
            pe.wait_ge(qkv_ready, 21)
            pe.wait_ge(ph.free, 5)
            attend(c_range, lambda k, first: None if first else advance(rest, FILL_C))
            advance(rest)
            pe.wait_ge(load_tab, 48)

            def by_channel(g):
                for t2 in range(2):
                    if g:
                        pe.wait_ge(f1_ready, 2 * g - 1 + t2)
                    else:
                        bank_free(t2)
                        bank_free(2 + t2)
                    for t in range(2):
                        rt = 2 * t2 + t
                        ins = nc.tensor.matmul(bank(t2, t * 256, t * 256 + 256), FT[:, g, rt * P:(rt + 1) * P],
                                               cst("dft_c", 256), start=True, stop=True)
                    ins.then_inc(f1_done, 1)

            by_channel(0)
            for g in range(4):
                if g < 3:
                    by_channel(g + 1)
                pe.wait_ge(f1_ready, 2 * g + 2)
                if g >= 2:
                    pe.wait_ge(four_ready, g - 1)
                for n in range(8):
                    rt, part = n // 2, n % 2
                    ins = nc.tensor.matmul(bank(2 + g % 2), F1[g % 2][:, rt, part * P:(part + 1) * P],
                                           DFT[:, rt, part * S:(part + 1) * S], start=(n == 0), stop=(n == 7))
                ins.then_inc(f2_done, 1)

            last_read.update({0: (f1_ready, 7), 1: (f1_ready, 8), 2: (four_ready, 3), 3: (four_ready, 4)})
            ph = PH["merge"]
            pe.wait_ge(o_ready, flushed(c_range))
            pe.wait_ge(four_ready, 4)
            for u in range(4):
                unit_ready(ph, u)
                slot = (ph.split + u) % 2
                for part in range(2):
                    for c in range(2):
                        b = 2 * part + c
                        bank_free(b)
                        advance(products(bank(b), [
                            (HI[slot][:, 1024 * part + k * 256 + c * P:1024 * part + k * 256 + (c + 1) * P],
                             LO[slot][:, 1024 * part + k * 256 + c * P:1024 * part + k * 256 + (c + 1) * P],
                             HH[:, 4 + k, :] if part else CO[0][:, k, :],
                             HL[:, 4 + k, :] if part else CO[1][:, k, :], False, None)
                            for k in range(4)], ph.done))
                        last_read[b] = (m_ready, 2 * u + c + 1)
            gemm(PH["c_out"], DC, 256, MH, ML, ready=lambda k: (m_lo, k + 1))
            norm("post1")
            norm("pre2")
            ffn(2, "pre2")
            norm("post2")


def kernel(**inputs):
    import numpy as _np
    import concourse.bacc as _bacc
    from concourse.bass_utils import run_bass_kernel_spmd as _run

    x = {k: _np.asarray(a) for k, a in inputs.items()}
    weights, params, x_t, mem_t, ctx_t, conds = lay_out(x)
    const, axial, rows = constants()
    nc = _bacc.Bacc("TRN2", target_bir_lowering=False, num_devices=1)
    arrays = {}

    def given(name, a):
        a = _np.ascontiguousarray(a)
        arrays[name] = a
        return nc.dram_tensor(name, a.shape, mybir.dt.from_np(a.dtype), kind="ExternalInput").ap()

    wd = {k: given(f"w_{k}", a) for k, a in weights.items()}
    others = [given(n, a) for n, a in (("params", params), ("constants", const), ("axial", axial), ("dft", rows),
                                       ("x_t", x_t), ("mem_t", mem_t), ("ctx_t", ctx_t), ("conditions", conds), ("positions", x["positions"]))]
    out = nc.dram_tensor("out_t", (P, DC, S), F32, kind="ExternalOutput").ap()
    program(nc, wd, *others, out)
    r = _run(nc, [arrays], core_ids=[0])
    got = r.results[0]["out_t"]
    return _np.ascontiguousarray(got.transpose(2, 1, 0).reshape(1, S, D))
```
